# Optimizing a Trainium2 kernel written in Bass

```python
import math
import jax, jax.numpy as jnp
from jax import lax
import numpy as np

D_MODEL = 1024
BATCH = 1
SEQ = 256
DEPTH = 1

A_HEADS = 4
A_HEAD_DIM = 128
IDX_HEADS = 8
IDX_DIM = 64
TOPK_MAX = 256
B_HEADS = 4
B_KEY_DIM = 128
B_VAL_DIM = 128
B_CHUNK = 64
C_HEADS = 4
C_Q_RANK = 384
C_KV_RANK = 256
C_NOPE = 128
C_ROPE = 64
C_V = 128
ROPE_THETA = 10000.0
REL_BUCKETS = 32
REL_MAX_DIST = 128
D_FF = -(-8 * D_MODEL // (3 * 256)) * 256
QBLOCK = 128
EPS = 1e-6
N_BRANCH = 3
NEG_BIG = -1e30
LB_FLOOR = 1e-30

A_WIDTH = A_HEADS * A_HEAD_DIM
B_WIDTH = B_HEADS * B_VAL_DIM
C_WIDTH = C_HEADS * C_V
IN_SPLITS = (A_HEADS * A_HEAD_DIM, A_HEAD_DIM, A_HEAD_DIM,
             IDX_HEADS * IDX_DIM, IDX_DIM, IDX_HEADS,
             B_HEADS * B_KEY_DIM, B_HEADS * B_KEY_DIM,
             B_HEADS * B_VAL_DIM, B_HEADS * B_VAL_DIM,
             C_Q_RANK, C_KV_RANK, C_ROPE,
             N_BRANCH * D_MODEL)
IN_COLS = sum(IN_SPLITS)


def rms_norm(x, g):
    x32 = x.astype(jnp.float32)
    y = x32 * lax.rsqrt(jnp.mean(x32 * x32, axis=-1, keepdims=True) + EPS)
    return (y * g.astype(jnp.float32)).astype(x.dtype)

def apply_rope(x, cos, sin):
    x32 = x.astype(jnp.float32)
    x1, x2 = jnp.split(x32, 2, axis=-1)
    return jnp.concatenate([x1 * cos - x2 * sin, x2 * cos + x1 * sin], axis=-1).astype(x.dtype)

def t5_bucket(dist):
    max_exact = REL_BUCKETS // 2
    d = jnp.maximum(dist, 0)
    dl = jnp.maximum(d, max_exact).astype(jnp.float32)
    large = max_exact + (jnp.log(dl / max_exact) / math.log(REL_MAX_DIST / max_exact)
                         * (REL_BUCKETS - max_exact)).astype(jnp.int32)
    large = jnp.minimum(large, REL_BUCKETS - 1)
    return jnp.where(d < max_exact, d, large)

def dsa_attention(q, k, v, iq, ik, iw, positions, rel_bias):
    bsz, s_len = q.shape[0], q.shape[1]
    topk = min(TOPK_MAX, s_len // 4)
    n_blk = s_len // QBLOCK
    key_idx = jnp.arange(s_len)
    scale = A_HEAD_DIM ** -0.5
    idx_scale = (IDX_DIM ** -0.5) * (IDX_HEADS ** -0.5)
    ik32 = ik.astype(jnp.float32)
    gather = jax.vmap(lambda arr, ix: arr[ix])

    def block(i):
        start = i * QBLOCK
        qb = lax.dynamic_slice_in_dim(q, start, QBLOCK, axis=1)
        iqb = lax.dynamic_slice_in_dim(iq, start, QBLOCK, axis=1).astype(jnp.float32)
        iwb = lax.dynamic_slice_in_dim(iw, start, QBLOCK, axis=1).astype(jnp.float32)
        pb = lax.dynamic_slice_in_dim(positions, start, QBLOCK, axis=1)
        t_idx = start + jnp.arange(QBLOCK)
        causal = key_idx[None, :] <= t_idx[:, None]
        logits = jnp.einsum('bthd,bsd->bths', iqb, ik32)
        score = jnp.einsum('bths,bth->bts', jax.nn.relu(logits), iwb) * idx_scale
        score = jnp.where(causal[None], score, NEG_BIG)
        _, sel = lax.top_k(score, topk)
        k_sel = gather(k, sel)
        v_sel = gather(v, sel)
        p_sel = gather(positions, sel)
        bias = rel_bias[t5_bucket(pb[:, :, None] - p_sel)]
        s = (jnp.einsum('bthd,btkd->bthk', qb, k_sel).astype(jnp.float32) * scale
             + jnp.moveaxis(bias, -1, 2).astype(jnp.float32))
        valid = sel <= t_idx[None, :, None]
        s = jnp.where(valid[:, :, None, :], s, NEG_BIG)
        p = jax.nn.softmax(s, axis=-1).astype(v.dtype)
        return jnp.einsum('bthk,btkd->bthd', p, v_sel)

    out = lax.map(block, jnp.arange(n_blk))
    return jnp.moveaxis(out, 0, 1).reshape(bsz, s_len, A_WIDTH)

def hgrn2_mixer(q, f_raw, inp, g, lb, out_gain):
    bsz, s_len = q.shape[0], q.shape[1]
    f32 = jnp.float32
    n_chunk = s_len // B_CHUNK
    fr = f_raw.astype(f32)
    log_lb = jnp.log(jnp.maximum(lb, LB_FLOOR))
    log_f = jnp.logaddexp(log_lb, jnp.log1p(-lb) + jax.nn.log_sigmoid(fr))
    k_in = (1.0 - lb) * jax.nn.sigmoid(-fr)
    q_s = q.astype(f32) * (B_KEY_DIM ** -0.5)

    def chunks(t, d):
        return t.astype(f32).reshape(bsz, n_chunk, B_CHUNK, B_HEADS, d).transpose(1, 0, 3, 2, 4)

    causal = jnp.tril(jnp.ones((B_CHUNK, B_CHUNK), dtype=bool))

    def step(state, xs):
        qc, kc, vc, lfc = xs
        b = jnp.cumsum(lfc, axis=2)
        o_inter = jnp.einsum('bhck,bhkv->bhcv', qc * jnp.exp(b), state)
        diff = b[:, :, :, None, :] - b[:, :, None, :, :]
        decay = jnp.exp(jnp.where(causal[None, None, :, :, None], diff, NEG_BIG))
        attn = jnp.einsum('bhtk,bhsk,bhtsk->bhts', qc, kc, decay)
        o_intra = jnp.einsum('bhts,bhsv->bhtv', attn, vc)
        b_last = b[:, :, -1:, :]
        new_state = (jnp.exp(b_last[:, :, 0, :])[..., None] * state
                     + jnp.einsum('bhsk,bhsv->bhkv', kc * jnp.exp(b_last - b), vc))
        return new_state, o_inter + o_intra

    xs = (chunks(q_s, B_KEY_DIM), chunks(k_in, B_KEY_DIM), chunks(inp, B_VAL_DIM), chunks(log_f, B_KEY_DIM))
    state0 = jnp.zeros((bsz, B_HEADS, B_KEY_DIM, B_VAL_DIM), f32)
    _, o = lax.scan(step, state0, xs)
    o = o.transpose(1, 0, 3, 2, 4).reshape(bsz, s_len, B_HEADS, B_VAL_DIM)
    o = rms_norm(o, out_gain) * jax.nn.silu(g.astype(f32).reshape(bsz, s_len, B_HEADS, B_VAL_DIM))
    return o.reshape(bsz, s_len, B_WIDTH).astype(q.dtype)

def mla_attention(q_nope, q_pe, k_nope, k_pe, v):
    bsz, s_len = q_nope.shape[0], q_nope.shape[1]
    n_blk = s_len // QBLOCK
    scale = (C_NOPE + C_ROPE) ** -0.5
    key_idx = jnp.arange(s_len)

    def block(i):
        start = i * QBLOCK
        qn = lax.dynamic_slice_in_dim(q_nope, start, QBLOCK, axis=1)
        qp = lax.dynamic_slice_in_dim(q_pe, start, QBLOCK, axis=1)
        t_idx = start + jnp.arange(QBLOCK)
        causal = key_idx[None, :] <= t_idx[:, None]
        s = (jnp.einsum('bthd,bshd->bhts', qn, k_nope)
             + jnp.einsum('bthr,bsr->bhts', qp, k_pe)).astype(jnp.float32) * scale
        s = jnp.where(causal[None, None], s, NEG_BIG)
        p = jax.nn.softmax(s, axis=-1).astype(v.dtype)
        return jnp.einsum('bhts,bshd->bthd', p, v)

    out = lax.map(block, jnp.arange(n_blk))
    return jnp.moveaxis(out, 0, 1).reshape(bsz, s_len, C_WIDTH)

def first_inputs(seed: int = 0) -> dict:
    key = jax.random.key(seed)
    ks = jax.random.split(key, 24)
    f32 = jnp.float32
    res_scale = (2 * DEPTH) ** -0.5

    def dense(k, shape, fan_in, scale=1.0):
        return jax.random.normal(k, shape, f32) * (scale * fan_in ** -0.5)

    def gain(k, shape):
        return 1.0 + 0.02 * jax.random.normal(k, shape, f32)

    x = jax.random.normal(ks[0], (BATCH, SEQ, D_MODEL), f32)
    offset = jax.random.randint(ks[1], (BATCH, 1), 0, 4096, dtype=jnp.int32)
    positions = offset + jnp.arange(SEQ, dtype=jnp.int32)[None, :]
    return {
        'x': x,
        'positions': positions,
        'w_in': dense(ks[2], (DEPTH, D_MODEL, IN_COLS), D_MODEL),
        'w_up_a': dense(ks[3], (DEPTH, A_WIDTH, D_MODEL), A_WIDTH),
        'w_up_b': dense(ks[4], (DEPTH, B_WIDTH, D_MODEL), B_WIDTH),
        'w_up_c': dense(ks[5], (DEPTH, C_WIDTH, D_MODEL), C_WIDTH),
        'w_out': dense(ks[6], (DEPTH, D_MODEL, D_MODEL), D_MODEL, res_scale),
        'mla_q_norm': gain(ks[7], (DEPTH, C_Q_RANK)),
        'mla_w_qb': dense(ks[8], (DEPTH, C_Q_RANK, C_HEADS * (C_NOPE + C_ROPE)), C_Q_RANK),
        'mla_kv_norm': gain(ks[9], (DEPTH, C_KV_RANK)),
        'mla_w_kvb': dense(ks[10], (DEPTH, C_KV_RANK, C_HEADS * (C_NOPE + C_V)), C_KV_RANK),
        'hgrn_lb_logits': 0.5 * jax.random.normal(ks[11], (DEPTH, B_HEADS * B_KEY_DIM), f32),
        'hgrn_out_norm': gain(ks[12], (DEPTH, B_VAL_DIM)),
        'rel_bias': 0.5 * jax.random.normal(ks[13], (REL_BUCKETS, A_HEADS), f32),
        'attn_norm': gain(ks[14], (DEPTH, D_MODEL)),
        'ffn_norm': gain(ks[15], (DEPTH, D_MODEL)),
        'w_ffn_gate': dense(ks[16], (DEPTH, D_MODEL, D_FF), D_MODEL),
        'w_ffn_up': dense(ks[17], (DEPTH, D_MODEL, D_FF), D_MODEL),
        'w_ffn_down': dense(ks[18], (DEPTH, D_FF, D_MODEL), D_FF, res_scale),
        'final_norm': gain(ks[19], (D_MODEL,)),
    }

def first_block(x, positions, w_in, w_up_a, w_up_b, w_up_c, w_out, mla_q_norm, mla_w_qb, mla_kv_norm,
              mla_w_kvb, hgrn_lb_logits, hgrn_out_norm, rel_bias, attn_norm, ffn_norm, w_ffn_gate,
              w_ffn_up, w_ffn_down, final_norm):
    bsz, s_len, _ = x.shape
    f32 = jnp.float32
    split_pts = np.cumsum(IN_SPLITS)[:-1].tolist()
    p_lb = jax.nn.softmax(hgrn_lb_logits.astype(f32), axis=0)
    lower_bounds = jnp.cumsum(p_lb, axis=0) - p_lb[0:1]
    inv_freq = ROPE_THETA ** (-jnp.arange(0, C_ROPE, 2, dtype=f32) / C_ROPE)
    ang = positions.astype(f32)[..., None] * inv_freq
    cos, sin = jnp.cos(ang), jnp.sin(ang)

    for l in range(DEPTH):
        h = rms_norm(x, attn_norm[l])
        proj = h @ w_in[l]
        (aq, ak, av, iq, ik, iw, bq, bf, bi, bg, cq, ckv, ckpe, gate_logits) = jnp.split(proj, split_pts, axis=-1)
        o_a = dsa_attention(aq.reshape(bsz, s_len, A_HEADS, A_HEAD_DIM), ak, av,
                            iq.reshape(bsz, s_len, IDX_HEADS, IDX_DIM), ik, iw, positions, rel_bias)
        o_b = hgrn2_mixer(bq, bf, bi, bg, lower_bounds[l], hgrn_out_norm[l])
        q_c = (rms_norm(cq, mla_q_norm[l]) @ mla_w_qb[l]).reshape(bsz, s_len, C_HEADS, C_NOPE + C_ROPE)
        q_nope, q_pe = q_c[..., :C_NOPE], q_c[..., C_NOPE:]
        kv_c = (rms_norm(ckv, mla_kv_norm[l]) @ mla_w_kvb[l]).reshape(bsz, s_len, C_HEADS, C_NOPE + C_V)
        k_nope, v_c = kv_c[..., :C_NOPE], kv_c[..., C_NOPE:]
        q_pe = apply_rope(q_pe, cos[:, :, None, :], sin[:, :, None, :])
        k_pe = apply_rope(ckpe, cos, sin)
        o_c = mla_attention(q_nope, q_pe, k_nope, k_pe, v_c)
        gates = jax.nn.sigmoid(gate_logits.astype(f32)).astype(x.dtype)
        g_a, g_b, g_c = jnp.split(gates, N_BRANCH, axis=-1)
        mixed = g_a * (o_a @ w_up_a[l]) + g_b * (o_b @ w_up_b[l]) + g_c * (o_c @ w_up_c[l])
        x = x + mixed @ w_out[l]
        h = rms_norm(x, ffn_norm[l])
        x = x + (jax.nn.silu(h @ w_ffn_gate[l]) * (h @ w_ffn_up[l])) @ w_ffn_down[l]

    return rms_norm(x, final_norm)


PLE_DIM = 256
HEAD_DIM = 64
FOX_HEADS = 8
SB_HEADS = 8
FOX_WIDTH = FOX_HEADS * HEAD_DIM
SB_WIDTH = SB_HEADS * HEAD_DIM
D_FF_2 = 2816
Q_BLOCK = 128
FORGET_BIAS_INIT = 2.0
IN_SIZES = (FOX_WIDTH, FOX_WIDTH, FOX_WIDTH, FOX_HEADS, SB_WIDTH, SB_WIDTH, SB_WIDTH, D_MODEL, D_MODEL)
IN_WIDTH = 3 * FOX_WIDTH + FOX_HEADS + 3 * SB_WIDTH + 2 * D_MODEL


def rms_norm_2(x, g):
    xf = x.astype(jnp.float32)
    y = xf * lax.rsqrt(jnp.mean(xf * xf, axis=-1, keepdims=True) + EPS)
    return (y * g.astype(jnp.float32)).astype(x.dtype)

def swiglu(h, w_gate, w_up, w_down):
    return (jax.nn.silu(h @ w_gate) * (h @ w_up)) @ w_down

def to_blocks(t):
    b, s = t.shape[0], t.shape[1]
    return jnp.moveaxis(t.reshape(b, s // Q_BLOCK, Q_BLOCK, *t.shape[2:]), 1, 0)

def from_blocks(t):
    nb, b = t.shape[0], t.shape[1]
    return jnp.moveaxis(t, 0, 1).reshape(b, nb * Q_BLOCK, -1)

def forgetting_attention(q, k, v, log_f):
    s_len = q.shape[1]
    scale = HEAD_DIM ** -0.5
    F = jnp.cumsum(log_f, axis=1)
    Fk = jnp.transpose(F, (0, 2, 1))[:, :, None, :]
    kpos = jnp.arange(s_len)
    qpos = kpos.reshape(s_len // Q_BLOCK, Q_BLOCK)

    def one_block(args):
        qi, Fi, pi = args
        logits = jnp.einsum('bqhd,bkhd->bhqk', qi, k).astype(jnp.float32) * scale
        logits = logits + jnp.transpose(Fi, (0, 2, 1))[..., None] - Fk
        mask = pi[:, None] >= kpos[None, :]
        logits = jnp.where(mask, logits, -jnp.inf)
        w = jax.nn.softmax(logits, axis=-1)
        return jnp.einsum('bhqk,bkhd->bqhd', w.astype(v.dtype), v)

    out = lax.map(one_block, (to_blocks(q), to_blocks(F), qpos))
    return from_blocks(out)

def stick_breaking_attention(q, k, v):
    s_len = q.shape[1]
    scale = HEAD_DIM ** -0.5
    kpos = jnp.arange(s_len)
    qpos = kpos.reshape(s_len // Q_BLOCK, Q_BLOCK)

    def one_block(args):
        qi, pi = args
        z = jnp.einsum('bqhd,bkhd->bhqk', qi, k).astype(jnp.float32) * scale
        mask = kpos[None, :] < pi[:, None]
        log_beta = jax.nn.log_sigmoid(z)
        log_1m = jnp.where(mask, jax.nn.log_sigmoid(-z), 0.0)
        after = lax.cumsum(log_1m, axis=3, reverse=True) - log_1m
        a = jnp.where(mask, jnp.exp(log_beta + after), 0.0)
        return jnp.einsum('bhqk,bkhd->bqhd', a.astype(v.dtype), v)

    out = lax.map(one_block, (to_blocks(q), qpos))
    return from_blocks(out)

def split_columns(t):
    outs, start = [], 0
    for size in IN_SIZES:
        outs.append(t[..., start:start + size])
        start += size
    return outs

def second_inputs(seed: int = 0) -> dict:
    key = jax.random.key(seed)
    ks = jax.random.split(key, 24)

    def w(k, shape, fan_in):
        return jax.random.normal(k, shape, jnp.float32) * (fan_in ** -0.5)

    def gain(k, shape):
        return 1.0 + 0.05 * jax.random.normal(k, shape, jnp.float32)

    L = DEPTH
    return {
        "x": jax.random.normal(ks[0], (BATCH, SEQ, D_MODEL), jnp.float32),
        "p": jax.random.normal(ks[1], (DEPTH, BATCH, SEQ, PLE_DIM), jnp.float32),
        "ffn1_norm": gain(ks[2], (L, D_MODEL)),
        "ffn1_w_gate": w(ks[3], (L, D_MODEL, D_FF_2), D_MODEL),
        "ffn1_w_up": w(ks[4], (L, D_MODEL, D_FF_2), D_MODEL),
        "ffn1_w_down": w(ks[5], (L, D_FF_2, D_MODEL), D_FF_2),
        "mix_norm": gain(ks[6], (L, D_MODEL)),
        "w_in": w(ks[7], (L, D_MODEL, IN_WIDTH), D_MODEL),
        "forget_bias": FORGET_BIAS_INIT + 0.1 * jax.random.normal(ks[8], (L, FOX_HEADS), jnp.float32),
        "q_norm": gain(ks[9], (L, HEAD_DIM)),
        "k_norm": gain(ks[10], (L, HEAD_DIM)),
        "w_branch_fox": w(ks[11], (L, FOX_WIDTH, D_MODEL), FOX_WIDTH),
        "w_branch_sb": w(ks[12], (L, SB_WIDTH, D_MODEL), SB_WIDTH),
        "w_out": w(ks[13], (L, D_MODEL, D_MODEL), D_MODEL),
        "ffn2_norm": gain(ks[14], (L, D_MODEL)),
        "ffn2_w_gate": w(ks[15], (L, D_MODEL, D_FF_2), D_MODEL),
        "ffn2_w_up": w(ks[16], (L, D_MODEL, D_FF_2), D_MODEL),
        "ffn2_w_down": w(ks[17], (L, D_FF_2, D_MODEL), D_FF_2),
        "ple_norm": gain(ks[18], (L, D_MODEL)),
        "w_ple_gate": w(ks[19], (L, D_MODEL, D_MODEL), D_MODEL),
        "w_ple_proj": w(ks[20], (L, PLE_DIM, D_MODEL), PLE_DIM),
    }

def second_block(x, p, ffn1_norm, ffn1_w_gate, ffn1_w_up, ffn1_w_down, mix_norm, w_in,
              forget_bias, q_norm, k_norm, w_branch_fox, w_branch_sb, w_out,
              ffn2_norm, ffn2_w_gate, ffn2_w_up, ffn2_w_down, ple_norm,
              w_ple_gate, w_ple_proj):
    b, s_len, _ = x.shape
    for i in range(DEPTH):
        x = x + 0.5 * swiglu(rms_norm_2(x, ffn1_norm[i]), ffn1_w_gate[i], ffn1_w_up[i], ffn1_w_down[i])

        h = rms_norm_2(x, mix_norm[i])
        fq, fk, fv, f_logit, sq, sk, sv, g_fox, g_sb = split_columns(h @ w_in[i])
        fq = rms_norm_2(fq.reshape(b, s_len, FOX_HEADS, HEAD_DIM), q_norm[i])
        fk = rms_norm_2(fk.reshape(b, s_len, FOX_HEADS, HEAD_DIM), k_norm[i])
        fv = fv.reshape(b, s_len, FOX_HEADS, HEAD_DIM)
        log_f = jax.nn.log_sigmoid((f_logit + forget_bias[i]).astype(jnp.float32))
        y_fox = forgetting_attention(fq, fk, fv, log_f)

        sq = sq.reshape(b, s_len, SB_HEADS, HEAD_DIM)
        sk = sk.reshape(b, s_len, SB_HEADS, HEAD_DIM)
        sv = sv.reshape(b, s_len, SB_HEADS, HEAD_DIM)
        y_sb = stick_breaking_attention(sq, sk, sv)

        merged = (jax.nn.sigmoid(g_fox) * (y_fox @ w_branch_fox[i])
                  + jax.nn.sigmoid(g_sb) * (y_sb @ w_branch_sb[i]))
        x = x + merged @ w_out[i]

        x = x + 0.5 * swiglu(rms_norm_2(x, ffn2_norm[i]), ffn2_w_gate[i], ffn2_w_up[i], ffn2_w_down[i])

        x = x + jax.nn.sigmoid(rms_norm_2(x, ple_norm[i]) @ w_ple_gate[i]) * (p[i] @ w_ple_proj[i])
    return x


def setup_inputs(seed=0):
    out = dict(first_inputs(seed))
    for name, value in second_inputs(seed + 1).items():
        if name != "x":
            out[name + "_2"] = value
    return out


def reference(
    x, positions, w_in, w_up_a, w_up_b, w_up_c, w_out, mla_q_norm, mla_w_qb, mla_kv_norm,
    mla_w_kvb, hgrn_lb_logits, hgrn_out_norm, rel_bias, attn_norm, ffn_norm, w_ffn_gate,
    w_ffn_up, w_ffn_down, final_norm, p_2, ffn1_norm_2, ffn1_w_gate_2, ffn1_w_up_2,
    ffn1_w_down_2, mix_norm_2, w_in_2, forget_bias_2, q_norm_2, k_norm_2, w_branch_fox_2,
    w_branch_sb_2, w_out_2, ffn2_norm_2, ffn2_w_gate_2, ffn2_w_up_2, ffn2_w_down_2, ple_norm_2,
    w_ple_gate_2, w_ple_proj_2,
):
    x = first_block(
        x, positions, w_in, w_up_a, w_up_b, w_up_c, w_out, mla_q_norm, mla_w_qb, mla_kv_norm,
        mla_w_kvb, hgrn_lb_logits, hgrn_out_norm, rel_bias, attn_norm, ffn_norm, w_ffn_gate,
        w_ffn_up, w_ffn_down, final_norm,
    )
    return second_block(
        x, p_2, ffn1_norm_2, ffn1_w_gate_2, ffn1_w_up_2, ffn1_w_down_2, mix_norm_2, w_in_2,
        forget_bias_2, q_norm_2, k_norm_2, w_branch_fox_2, w_branch_sb_2, w_out_2, ffn2_norm_2,
        ffn2_w_gate_2, ffn2_w_up_2, ffn2_w_down_2, ple_norm_2, w_ple_gate_2, w_ple_proj_2,
    )


_drawn_inputs = setup_inputs


def setup_inputs(seed=0):
    import zlib

    import numpy as np

    out = dict(_drawn_inputs(seed))
    spreads = {}
    factors = {'mla_q_norm': 8.0,
     'mla_kv_norm': 8.0,
     'hgrn_out_norm': 8.0,
     'attn_norm': 3.34,
     'ffn_norm': 5.05,
     'final_norm': 2.706,
     'ffn1_norm_2': 2.786,
     'forget_bias_2': 45.888,
     'q_norm_2': 8.0,
     'k_norm_2': 8.0,
     'ffn2_norm_2': 3.329,
     'ple_norm_2': 54.144}
    for name, (base, spread) in spreads.items():
        noise = np.random.default_rng([zlib.crc32(name.encode()), seed]).standard_normal(out[name].shape)
        drawn = base * np.exp(spread * noise) if base else spread * noise
        out[name] = __import__('jax').numpy.asarray(drawn.astype(out[name].dtype))
    for name, factor in factors.items():
        out[name] = (out[name] * factor).astype(out[name].dtype)
    return out
```

```python
from contextlib import ExitStack

import numpy as np

import concourse.bass as bass
from concourse import mybir

F32 = mybir.dt.float32
F32R = mybir.dt.float32r
I32 = mybir.dt.int32
ACT = mybir.ActivationFunctionType
ALU = mybir.AluOpType
AX = mybir.AxisListType

P = 128
T = 256
NT = T // P
D = 1024
KD = D // P
FF = 2816
KF = FF // P
A_H, B_H, C_H = 4, 4, 4
IDX_H, IDX_D = 8, 64
TOPK = 64
CHUNK = 64
QR, KVR, NOPE, ROPE = 384, 256, 128, 64
FOX_H, HD = 8, 64
BUCKETS, MAX_DIST = 32, 128
EPS = 1e-6
NEG = -1e30
LB_FLOOR = 1e-30
AVW = P + IDX_H
FVL = FOX_H * HD // 1 + FOX_H
SLOT = 4 * FVL
HALF_SPLIT = 2

C_ID, C_ONE, C_ONE64, C_SWAP, C_CM, C_SCM, C_S01, C_TRI, C_LEV = 0, 128, 256, 384, 512, 768, 1024, 1280, 1536
LEVELS = (0, 1, 2, 4, 8, 16, 32, 64)
C_SEL = C_LEV + P * len(LEVELS)
C_INVF = C_SEL + P * FOX_H
C_SIGN = C_INVF + 1
N_CONST = C_SIGN + 1

VEC_SIZES = [("attn_norm", KD), ("ffn_norm", KD), ("final_norm", KD), ("ffn1_norm", KD), ("mix_norm", KD),
             ("ffn2_norm", KD), ("ple_norm", KD), ("mla_q_norm", QR // P), ("mla_kv_norm", KVR // P),
             ("lb_logits", B_H), ("hgrn_out", 1), ("q_norm", 1), ("k_norm", 1)]
VEC, _at = {}, 0
for _n, _c in VEC_SIZES:
    VEC[_n] = _at
    _at += _c
N_VEC = _at


def bucket_thresholds():
    exact = BUCKETS // 2
    d = np.arange(1, MAX_DIST * 2)
    large = exact + (np.log(np.maximum(d, exact).astype(np.float32) / np.float32(exact))
                     / np.float32(np.log(MAX_DIST / exact)) * (BUCKETS - exact)).astype(np.int32)
    bucket = np.where(d < exact, d, np.minimum(large, BUCKETS - 1))
    return [float(d[np.argmax(bucket >= b)]) for b in range(1, BUCKETS)]


def constants():
    c = np.zeros((P, N_CONST), np.float32)
    r = np.arange(P)
    row, col = r[:, None], r[None, :]
    c[:, C_ID:C_ID + P] = row == col
    c[:, C_ONE:C_ONE + P] = 1
    c[:, C_ONE64:C_ONE64 + P] = row // 64 == col // 64
    c[:, C_SWAP:C_SWAP + P] = row == (col ^ 32)
    c[:, C_CM + P:C_CM + T] = np.where(col <= row, 0, np.float32(NEG))
    c[:, C_SCM + P:C_SCM + T] = np.where(col < row, 0, np.float32(NEG))
    c[:, C_S01:C_S01 + P] = 1
    c[:, C_S01 + P:C_S01 + T] = col < row
    c[:, C_TRI:C_TRI + P] = row <= col
    c[:, C_TRI + P:C_TRI + T] = 1
    for i, h in enumerate(LEVELS):
        if h == 0:
            m = row == col
        else:
            m = (row // (2 * h) == col // (2 * h)) & (row % (2 * h) < h) & (col % (2 * h) >= h)
        c[:, C_LEV + P * i:C_LEV + P * (i + 1)] = m
    for h in range(FOX_H):
        c[h, C_SEL + P * h:C_SEL + P * (h + 1)] = 1
    c[:, C_INVF] = (10000.0 ** (-(2.0 * (r % 32)) / ROPE)).astype(np.float32)
    c[:, C_SIGN] = np.where(r % 64 < 32, -1, 1)
    return c


def stream_plan():
    tiles, first = [], {}

    def add(name, n, cols, half):
        first[name] = len(tiles)
        tiles.extend((name, i, cols, half) for i in range(n))

    full = 2 * KD * P
    add("w_projT_a", 3, full, full // 2)
    add("w_avw", 1, KD * AVW, KD * AVW // 2)
    add("w_projT_b", 7, full, full // 2)
    add("w_projT_c", 2, full, full // 2)
    add("w_bi", 2, full, full // 2)
    add("w_projT_d", 2, full, full // 2)
    add("w_qb", 2, 9 * P, 6 * P)
    add("w_kvb", 1, full, full // 2)
    add("w_gates1", 12, full, full // 2)
    add("w_up1", 6, full, full // 2)
    add("w_out1", 4, full, full // 2)
    add("w_gu0", KF, full, full // 2)
    add("w_dn0", 16, KF * P // 2, 6 * P)
    add("w_gu1", KF, full, full // 2)
    add("w_dn1", 16, KF * P // 2, 6 * P)
    add("w_qk2", 8, full, full // 2)
    add("w_fvl", 2, 4 * FVL, 2 * FVL)
    add("w_sv", 2, full, full // 2)
    add("w_gates2", 8, full, full // 2)
    add("w_up2", 4, full, full // 2)
    add("w_out2", 4, full, full // 2)
    add("w_gu2", KF, full, full // 2)
    add("w_dn2", 16, KF * P // 2, 6 * P)
    add("w_pg", 4, full, full // 2)
    add("w_pp", 1, full, full // 2)
    return tiles, first


TILES, FIRST = stream_plan()

BLOCKS, ENDS = {}, {}


def plan_blocks():
    n = 0
    g = FIRST
    plan = [("kpe_ik", 2, lambda i: 0), ("iq", 4, lambda i: 1 + i // 2), ("avw", 2, lambda i: 3),
            ("projT_b", 14, lambda i: 4 + i // 2), ("bq", 4, lambda i: g["w_projT_c"] + i // 2),
            ("bi", 2, lambda i: g["w_bi"] + 1), ("bg", 4, lambda i: g["w_projT_d"] + i // 2),
            ("q_c", 6, lambda i: g["w_qb"] + i // 3), ("kv_c", 6, lambda i: g["w_kvb"]),
            ("gates1", 24, lambda i: g["w_gates1"] + i // 2), ("up1", 24, lambda i: g["w_up1"] + i // 4),
            ("out1", 8, lambda i: g["w_out1"] + i // 2),
            ("gu0", 44, lambda i: g["w_gu0"] + i // 2), ("dn0", 8, lambda i: g["w_dn0"] + 2 * i + 1),
            ("gu1", 44, lambda i: g["w_gu1"] + i // 2), ("dn1", 8, lambda i: g["w_dn1"] + 2 * i + 1),
            ("qk2", 16, lambda i: g["w_qk2"] + i // 2), ("fvl", 4, lambda i: g["w_fvl"] + 1),
            ("sv", 2, lambda i: g["w_sv"] + 1), ("gates2", 16, lambda i: g["w_gates2"] + i // 2),
            ("up2", 16, lambda i: g["w_up2"] + i // 4), ("out2", 8, lambda i: g["w_out2"] + i // 2),
            ("gu2", 44, lambda i: g["w_gu2"] + i // 2), ("dn2", 8, lambda i: g["w_dn2"] + 2 * i + 1),
            ("pgp", 16, lambda i: g["w_pg"] + i // 2 if i < 8 else g["w_pp"])]
    for name, count, end in plan:
        BLOCKS[name] = n
        for i in range(count):
            ENDS[n + i] = end(i)
        n += count
    return n


N_BLOCKS = plan_blocks()
DONE_AFTER = {g: max(n for n, e in ENDS.items() if e == g) + 1 for g in set(ENDS.values())}
PARTS = [g for g in range(len(TILES)) if g not in DONE_AFTER]


def order_of_work():
    o, tile = [], [0]

    def tiles(n):
        for _ in range(n):
            o.append(("tile", tile[0]))
            tile[0] += 1

    def steps(*names):
        o.extend(("step", s) for s in names)

    def phase(name, n):
        assert FIRST[name] == tile[0], (name, tile)
        o.append(("ffn" if "gu" in name or "dn" in name else "tiles", name))
        tile[0] += n

    steps("norm0", "tables")
    tiles(1); steps("bias0")
    tiles(1); steps("bias1")
    tiles(1); steps("bias2")
    tiles(1); steps("idx00", "idx01", "top0")
    tiles(1); steps("bias3")
    tiles(1); steps("idx10", "idx11")
    tiles(1); steps("top1", "dsa_s0")
    tiles(1); steps("dsa_t0", "norm_cq")
    tiles(1); steps("dsa_s1", "norm_ckv")
    tiles(1); steps("dsa_t1", "rope_k")
    tiles(1); steps("dsa_o", "decay")
    tiles(2); steps("level_e0", "level_e1")
    tiles(2); steps("lev0", "level_e2", "lev1")
    tiles(2); steps("level_e3", "lev2")
    tiles(3); steps("rope_q", "level_e4", "lev3")
    tiles(1); steps("mla_s0", "level_e5")
    tiles(1); steps("mla_t0", "lev4")
    tiles(1); steps("mla_s1", "level_e6", "lev5")
    tiles(1); steps("mla_t1", "level_e7", "lev6")
    tiles(1); steps("mla_o", "level_e8", "lev7")
    tiles(1); steps("far")
    tiles(1); steps("hgrn_o")
    tiles(1); steps("hgrn_n")
    tiles(4); steps("gate_sigmoid1")
    tiles(5); steps("half_mixed1")
    tiles(1); steps("split_mixed1")
    tiles(4)
    steps("norm1")
    phase("w_gu0", KF); phase("w_dn0", 16)
    steps("norm2", "norm3")
    phase("w_gu1", KF); phase("w_dn1", 16)
    steps("norm4")
    tiles(4); steps("norm_fq", "norm_fk")
    tiles(4)
    tiles(2); steps("forget")
    tiles(2); steps("fox_s00", "sb_s00")
    tiles(1); steps("fox_t00", "fox_s01", "sb_t00")
    tiles(1); steps("fox_t01", "fox_o0", "sb_s01")
    tiles(1); steps("fox_s10", "sb_t01", "sb_o0")
    tiles(1); steps("fox_t10", "fox_s11", "sb_s10")
    tiles(1); steps("fox_t11", "fox_o1", "sb_t10")
    tiles(1); steps("sb_s11")
    tiles(2); steps("sb_t11", "sb_o1", "gate_sigmoid2")
    tiles(3); steps("half_mixed2")
    tiles(1); steps("split_mixed2")
    tiles(4)
    steps("norm5")
    phase("w_gu2", KF); phase("w_dn2", 16)
    steps("norm6", "split_p")
    tiles(5)
    assert tile[0] == len(TILES), tile
    return o


ORDER = order_of_work()


def area_turns(uses):
    taken = [s for kind, s in ORDER if kind == "step" and uses(s)]
    return {s: n for n, s in enumerate(taken)}


def takes_a(s):
    return (s.startswith(("idx", "rope_", "dsa_s", "dsa_o", "mla_s", "mla_o", "fox_s", "fox_o", "sb_s", "sb_o", "hgrn_o"))
            or s in ("lev0", "lev2", "lev4", "lev6", "far"))


def takes_t(s):
    return (s.startswith(("norm", "dsa_t", "mla_t", "fox_t", "sb_t", "forget", "hgrn_n"))
            or s in ("lev1", "lev3", "lev5", "lev7"))


TURN_A, TURN_T = area_turns(takes_a), area_turns(takes_t)
NORMS = [s for k, s in ORDER if s in [f"norm{i}" for i in range(7)]]


def build(nc, a, out_t):
    with ExitStack() as ctx:
        sems = {}

        def S(name):
            if name not in sems:
                sems[name] = ctx.enter_context(nc.semaphore(name))
            return sems[name]

        top = [nc.sbuf_base + (-nc.sbuf_base) % 64]

        def at(name, shape, off, dt=F32):
            return nc.alloc_sbuf_tensor_at(name, [P, *shape], dt, offset=off)

        def fixed(name, shape, dt=F32):
            off = top[0]
            top[0] += (4 * int(np.prod(shape)) + 63) // 64 * 64
            return at(name, shape, off, dt)

        x = fixed("x", (KD, T))
        hs_off = top[0]
        hs = fixed("hs", (KD, 2 * T), F32R)
        raw = fixed("raw", (2, SLOT))
        whi = fixed("whi", (2, SLOT), F32R)
        wlo = fixed("wlo", (2, SLOT), F32R)
        tmp = fixed("tmp", (4, T))
        con = fixed("con", (N_CONST,))
        vec = fixed("vec", (N_VEC,))
        st = fixed("st", (256,))
        epsb = fixed("epsb", (1,))
        sq = at("sq", (KD, T), hs_off)
        xr = fixed("xr", (T,))
        ones_row = fixed("ones_row", (T,))
        base = top[0]

        def arena(name, off, shape, dt=F32):
            assert base + 4 * (off + int(np.prod(shape))) <= nc.sbuf_usable_end, name
            return at(name, shape, base + 4 * off, dt)

        ident = con[:, C_ID:C_ID + P]
        ones = con[:, C_ONE:C_ONE + P]
        ones64 = con[:, C_ONE64:C_ONE64 + P]
        swap = con[:, C_SWAP:C_SWAP + P]

        gates = arena("gates", 0, (24, T))
        relu_l = arena("relu_l", 0, (IDX_H, T))
        d_sc = arena("d_sc", 2048, (4, T))
        d_p = arena("d_p", 3072, (4, T))
        d_pt0 = arena("d_pt0", 4096, (4, T))
        d_pt1 = arena("d_pt1", 5120, (4, P))
        osplit = [arena(f"osplit_{n}", 6144 + 2048 * i, (4, 2 * T), F32R) for i, n in enumerate("abc")]
        m_sc = arena("m_sc", 8192, (4, T))
        m_p = arena("m_p", 9216, (4, T))
        m_pt0 = arena("m_pt0", 10240, (4, T))
        m_pt1 = arena("m_pt1", 11264, (4, P))
        cqs = arena("cqs", 10240, (3, 2 * T), F32R)
        ckvs = arena("ckvs", 8192, (2, 2 * T), F32R)
        iq = arena("iq", 12288, (4, T))
        ik = arena("ik", 13312, (T,))
        aq = arena("aq", 13568, (4, T))
        ak = arena("ak", 14592, (T,))
        av = arena("av", 14848, (NT, P))
        iw = arena("iw", 15104, (NT, IDX_H))
        bias = arena("bias", 15120, (A_H, P + T))
        qn = arena("qn", 12288, (C_H, T))
        qpe = arena("qpe", 13312, (2, T))
        kn = arena("kn", 13824, (C_H, T))
        vc = arena("vc", 14848, (NT, C_H * P))
        mixed1 = arena("mixed1", 12288, (KD, T))
        up1 = arena("up1", 14336, (4, T))
        gated1 = arena("gated1", 15360, (2, T))
        bf = arena("bf", 16656, (B_H, T))
        bq = arena("bq", 17680, (B_H, T))
        bg = arena("bg", 18704, (B_H, T))
        bi = arena("bi", 19728, (NT, B_H * P))
        cq = arena("cq", 20752, (3, T))
        ckv = arena("ckv", 21520, (2, T))
        kpe = arena("kpe", 22032, (T,))
        cos = arena("cos", 22288, (T,))
        sin = arena("sin", 22544, (T,))
        hb = arena("hb", 22800, (B_H * T,))
        hk = arena("hk", 23824, (B_H * T,))
        he = [arena(f"he{i}", 24848 + 1024 * i, (B_H * T,)) for i in range(2)]
        h0 = arena("h0", 26896, (B_H, T))
        h1 = arena("h1", 27920, (B_H, P))
        dist = arena("dist", 22800, (P + T,))
        mask = [arena(f"mask{i}", 23184 + 384 * i, (P + T,)) for i in range(2)]
        posf = arena("posf", 23952, (T,))
        relb = arena("relb", 24208, (BUCKETS * A_H,))
        drel = arena("drel", 24336, ((BUCKETS - 1) * A_H,))
        posi = nc.alloc_sbuf_tensor_at("posi", [P, T], I32, offset=base + 4 * 24464)
        post = nc.alloc_sbuf_tensor_at("post", [P, NT], I32, offset=base + 4 * 24720)
        postf = arena("postf", 24736, (NT,))
        ang = arena("ang", 24848, (T,))
        turns = arena("turns", 25104, (T,))
        rest = arena("rest", 25360, (T,))
        over = arena("over", 25616, (T,))
        score = arena("score", 26896, (T,))
        work = arena("work", 27152, (T,))
        above = arena("above", 27408, (T,))
        equal = arena("equal", 27664, (T,))
        rank = arena("rank", 27920, (T,))
        nsq = arena("nsq", 24848, (3, T))
        nrm = arena("nrm", 25616, (T,))
        nval = arena("nval", 25872, (3, T))
        hx = [he[0], he[1], arena("hx2", 26896, (B_H * T,))]
        rotated = arena("rotated", 28448, (T,))
        resetc = arena("resetc", 23824, (B_H * T,))

        sq_ring = arena("sq_ring", 19968, (2, T))
        sq_sum = arena("sq_sum", 20480, (T,))

        hid = arena("hid", 0, (KF, 2 * T), F32R)
        gbuf = arena("gbuf", 11264, (2, T))
        ubuf = arena("ubuf", 11776, (2, T))
        sbuf = arena("sbuf", 12288, (2, T))
        hbuf = arena("hbuf", 12800, (2, T))
        dsum = arena("dsum", 13312, (2, T))

        qk2 = arena("qk2", 0, (16, T))
        fq, fk, sq_, sk_ = (qk2[:, 4 * i:4 * i + 4, :] for i in range(4))
        fv = arena("fv", 4096, (NT, FOX_H * HD))
        sv = arena("sv", 5120, (NT, FOX_H * HD))
        gates2 = arena("gates2", 6144, (16, T))
        osplit2 = [arena(f"osplit2_{n}", 10240 + 2048 * i, (4, 2 * T), F32R) for i, n in enumerate(("fox", "sb"))]
        mixed2 = arena("mixed2", 14336, (KD, T))
        up2 = arena("up2", 16384, (4, T))
        gated2 = arena("gated2", 17408, (2, T))
        f_sc = arena("f_sc", 17920, (4, T))
        f_p = arena("f_p", 18944, (4, T))
        s_z = arena("s_z", 19968, (4, T))
        s_a = arena("s_a", 20992, (4, T))
        s_pad = arena("s_pad", 22016, (4 * (T + 1),))
        s_after = arena("s_after", 23048, (4 * (T + 1),))
        s_keep = arena("s_keep", 24080, (4 * (T + 1),))
        f_pt0 = arena("f_pt0", 25112, (4, T))
        f_pt1 = arena("f_pt1", 26136, (4, P))
        flog = arena("flog", 26648, (NT, FOX_H))
        flog2 = arena("flog2", 26664, (NT * FOX_H,))
        negf = arena("negf", 26680, (T,))
        fb = arena("fb", 26936, (FOX_H,))
        s_pt0 = arena("s_pt0", 26944, (4, T))
        s_pt1 = arena("s_pt1", 27968, (4, P))
        s_keep1 = arena("s_keep1", 28480, (4 * (P + 1),))
        s_keep2 = s_keep
        n2sq = arena("n2sq", 17920, (4, T))
        n2r = arena("n2r", 18944, (4, T))
        praw = arena("praw", 16384, (2, T))
        ps = arena("ps", 16896, (2, 2 * T), F32R)
        pg = arena("pg", 0, (KD, T))
        pp = arena("pp", 2048, (2, T))

        acc = [ctx.enter_context(nc.psum_tensor(f"acc{i}", [P, 512], F32)) for i in range(4)]
        area_a = ctx.enter_context(nc.psum_tensor("area_a", [P, 4, T], F32))
        area_t = ctx.enter_context(nc.psum_tensor("area_t", [P, 4, T], F32))

        def keys(tt):
            return P * (tt + 1)

        def queries(tt):
            return slice(P * tt, P * tt + P)

        def cols(h):
            return slice(64 * (h % 2), 64 * (h % 2) + 64)

        HEAD_OF_SLOT = (0, 2, 1, 3)

        def heads4(v, n):
            return v.unsqueeze(1).to_broadcast([P, 4, n])

        def causal(tt, c0):
            return con[:, c0 + (P if tt == 0 else 0):c0 + T]

        def free_value(g):
            if g in DONE_AFTER:
                return "block_done", DONE_AFTER[g]
            return "part_done", PARTS.index(g) + 1

        def norm_of(step):
            return VEC[("attn_norm", "ffn_norm", "final_norm", "ffn1_norm", "mix_norm", "ffn2_norm",
                        "ple_norm")[NORMS.index(step)]]

        SUMMED = {"norm1": "out1", "norm2": "dn0", "norm4": "dn1", "norm5": "out2", "norm6": "dn2"}
        SUMMED_NORMS = list(SUMMED)
        SQUARED = {BLOCKS[b] + k: (SUMMED_NORMS.index(n), k) for n, b in SUMMED.items() for k in range(KD)}
        DIRECT_NORMS = ["norm0", "norm3"]
        HS_NORMS = [s for s in NORMS if s != "norm2"]
        HS_WRITES = [s for k, s in ORDER if k == "step" and (s in HS_NORMS or s.endswith(("mixed1", "mixed2")))]
        HS_STARTS = [s for s in HS_WRITES if not s.startswith("half")]
        HS_BEFORE = {FIRST[n]: KD * i for i, n in enumerate(
            ("w_projT_a", "w_out1", "w_gu0", "w_gu1", "w_qk2", "w_out2", "w_gu2", "w_pg"))}

        block = ctx.enter_context(nc.Block())

        @block.sync
        def _(sp):
            sp.dma_start(x[:], a["xT"].rearrange("k p t -> p k t")).then_inc(S("x_loaded"), 16)
            sp.dma_start(con[:], a["consts"]).then_inc(S("con_loaded"), 16)
            sp.dma_start(vec[:], a["vecs"]).then_inc(S("con_loaded"), 16)
            sp.dma_start(posi[:], a["pos"].partition_broadcast(P)).then_inc(S("con_loaded"), 16)
            sp.dma_start(post[:], a["pos"].rearrange("(i p) -> p i", p=P),
                         allow_slow_non_contiguous=True).then_inc(S("con_loaded"), 16)
            sp.dma_start(relb[:], a["rel_bias"].partition_broadcast(P)).then_inc(S("con_loaded"), 16)

            def load(src, slot, n, lo_needed):
                if lo_needed is not None:
                    sp.wait_ge(S("w_lo"), lo_needed)
                sp.dma_start(raw[:, slot, 0:n], src).then_inc(S(f"w_loaded{slot}"), 16)

            def load_run(name, count):
                g0 = FIRST[name]
                n = TILES[g0][2]
                with sp.Fori(0, count // 2) as i:
                    for j in range(2):
                        load(a[name][i * 2 + j], j, n, i * 4 + 2 * (g0 + j) - 2)

            done = set()
            for g, (name, i, n, _) in enumerate(TILES):
                if name[2:4] in ("gu", "dn"):
                    if name not in done:
                        done.add(name)
                        load_run(name, KF if "gu" in name else 16)
                    if name == "w_gu0" and i == KF - 1:
                        sp.wait_ge(S("block_freed"), BLOCKS["gu0"] + 1)
                        sp.dma_start(fb[:], a["forget_bias"].partition_broadcast(P)).then_inc(S("fb_loaded"), 16)
                    if name == "w_gu2" and i == KF - 1:
                        sp.wait_ge(S("block_freed"), BLOCKS["gu2"] + 1)
                        sp.dma_start(praw[:], a["pT"].rearrange("k p t -> p k t")).then_inc(S("p_loaded"), 16)
                    continue
                load(a[name][i], g % 2, n, 2 * g - 2 if g >= 2 else None)
            for k in range(KD):
                sp.wait_ge(S("out_ready"), k + 1)
                sp.dma_start(out_t[k], x[:, k, :]).then_inc(S("stored"), 16)
            sp.wait_ge(S("stored"), 16 * KD)

        @block.tensor
        def _(pe):
            def mm(out, w, m, start, stop):
                return nc.tensor.matmul(out, w, m, start=start, stop=stop, skip_group_check=True)

            def block_t(slot, c0, n_k, n, h, k0=0, first=True, last=True):
                bank = acc[n % 4]
                for k in range(n_k):
                    c = c0 + k * P
                    hi = (bank[:, :], whi[:, slot, c:c + P], h[:, k0 + k, :])
                    lo = (bank[:, 0:T], wlo[:, slot, c:c + P], h[:, k0 + k, 0:T])
                    begin, end = first and k == 0, last and k == n_k - 1
                    if end:
                        mm(*lo, False, False)
                        m = mm(*hi, begin, True)
                    else:
                        mm(*hi, begin, False)
                        m = mm(*lo, False, False)
                return m

            def block_n(slot, c0, pitch, width, n_k, n, h, tt, k0=0, first=True, last=True):
                out = acc[n % 4][:, 0:width]
                for k in range(n_k):
                    c = c0 + k * pitch
                    hi_t = h[:, k0 + k, P * tt:P * tt + P]
                    lo_t = h[:, k0 + k, T + P * tt:T + P * tt + P]
                    mm(out, hi_t, whi[:, slot, c:c + width], first and k == 0, False)
                    mm(out, hi_t, wlo[:, slot, c:c + width], False, False)
                    m = mm(out, lo_t, whi[:, slot, c:c + width], False, last and k == n_k - 1)
                return m

            def half_ready(g, half):
                pe.wait_ge(S("w_lo"), 2 * g + half + 1)

            def first_tile(g, n):
                bank_free(n + 1)
                half_ready(g, 1)
                for k in range(KD):
                    pe.wait_ge(S("hs_lo"), HS_BEFORE[g] + k + 1)
                    for b in range(2):
                        c = (b * KD + k) * P
                        mm(acc[(n + b) % 4][:, :], whi[:, g % 2, c:c + P], hs[:, k, :], k == 0, False)
                        m = mm(acc[(n + b) % 4][:, 0:T], wlo[:, g % 2, c:c + P], hs[:, k, 0:T], False, k == KD - 1)
                        if k == KD - 1:
                            m.then_inc(S("block_done"), 1)

            def bank_free(n):
                if n >= 4:
                    pe.wait_ge(S("block_freed"), n - 3)

            def mixer_split(name, branch):
                if (name, branch) == ("w_up1", 1):
                    pe.wait_ge(S("hgrn_split"), 1)
                else:
                    last = {"w_up1": ("dsa_o", None, "mla_o"), "w_up2": ("fox_o1", "sb_o1")}[name][branch]
                    pe.wait_ge(S("a_freed"), TURN_A[last] + 1)

            def tile(g):
                name, i, _, _ = TILES[g]
                slot = g % 2
                first_of = {"w_projT_a": (BLOCKS["kpe_ik"], 2), "w_projT_b": (BLOCKS["projT_b"], 2),
                            "w_projT_c": (BLOCKS["bq"], 2), "w_projT_d": (BLOCKS["bg"], 2),
                            "w_gates1": (BLOCKS["gates1"], 2), "w_out1": (BLOCKS["out1"], 2),
                            "w_qk2": (BLOCKS["qk2"], 2), "w_gates2": (BLOCKS["gates2"], 2),
                            "w_out2": (BLOCKS["out2"], 2), "w_pg": (BLOCKS["pgp"], 2)}
                if g in HS_BEFORE:
                    first_tile(g, first_of[name][0])
                elif name in first_of:
                    n0, per = first_of[name]
                    for b in range(per):
                        n = n0 + per * i + b
                        bank_free(n)
                        half_ready(g, b)
                        block_t(slot, b * KD * P, KD, n, hs).then_inc(S("block_done"), 1)
                elif name in ("w_up1", "w_up2"):
                    n0, src = (BLOCKS["up1"], osplit) if name == "w_up1" else (BLOCKS["up2"], osplit2)
                    if i % 2 == 0:
                        mixer_split(name, i // 2)
                    for b in range(4):
                        n = n0 + 4 * i + b
                        bank_free(n)
                        half_ready(g, b // 2)
                        block_t(slot, b * 4 * P, 4, n, src[i // 2]).then_inc(S("block_done"), 1)
                elif name == "w_avw":
                    n0 = BLOCKS["avw"]
                    bank_free(n0 + 1)
                    for half in range(2):
                        half_ready(g, half)
                        for tt in range(NT):
                            m = block_n(slot, half * 4 * AVW, AVW, AVW, 4, n0 + tt, hs, tt, 4 * half,
                                        half == 0, half == 1)
                            if half:
                                m.then_inc(S("block_done"), 1)
                elif name in ("w_bi", "w_sv"):
                    n0 = BLOCKS[name[2:]]
                    if i == 0:
                        bank_free(n0 + 1)
                    for half in range(2):
                        half_ready(g, half)
                        for tt in range(NT):
                            m = block_n(slot, half * 1024, 512, 512, 2, n0 + tt, hs, tt, 4 * i + 2 * half,
                                        i == 0 and half == 0, i == 1 and half == 1)
                            if half and i:
                                m.then_inc(S("block_done"), 1)
                    if i == 0:
                        m.then_inc(S("part_done"), 1)
                elif name == "w_fvl":
                    n0 = BLOCKS["fvl"]
                    if i == 0:
                        bank_free(n0 + 3)
                    for half in range(2):
                        half_ready(g, half)
                        for tt in range(NT):
                            for what in range(2):
                                m = block_n(slot, half * 2 * FVL + 512 * what, FVL, (512, FOX_H)[what], 2,
                                            n0 + 2 * what + tt, hs, tt, 4 * i + 2 * half,
                                            i == 0 and half == 0, i == 1 and half == 1)
                    if i == 0:
                        m.then_inc(S("part_done"), 1)
                    else:
                        m.then_inc(S("block_done"), 4)
                elif name == "w_qb":
                    if i == 0:
                        pe.wait_ge(S("cq_split"), 3)
                    for b in range(3):
                        n = BLOCKS["q_c"] + 3 * i + b
                        bank_free(n)
                        half_ready(g, b // 2)
                        block_t(slot, b * 3 * P, 3, n, cqs).then_inc(S("block_done"), 1)
                elif name == "w_kvb":
                    pe.wait_ge(S("ckv_split"), 2)
                    for b in range(4):
                        n = BLOCKS["kv_c"] + b
                        bank_free(n)
                        half_ready(g, 0)
                        block_t(slot, b * 2 * P, 2, n, ckvs).then_inc(S("block_done"), 1)
                    half_ready(g, 1)
                    for tt in range(NT):
                        n = BLOCKS["kv_c"] + 4 + tt
                        bank_free(n)
                        block_n(slot, 1024, 512, 512, 2, n, ckvs, tt).then_inc(S("block_done"), 1)
                elif name == "w_pp":
                    pe.wait_ge(S("p_split"), 2)
                    for b in range(KD):
                        n = BLOCKS["pgp"] + 8 + b
                        bank_free(n)
                        half_ready(g, b // 4)
                        block_t(slot, b * 2 * P, 2, n, ps).then_inc(S("block_done"), 1)
                else:
                    raise AssertionError(name)

            def gate_up(f):
                g0, n0 = FIRST[f"w_gu{f}"], BLOCKS[f"gu{f}"]
                first_tile(g0, n0)
                for b in range(2):
                    bank_free(n0 + 2 + b)
                    half_ready(g0 + 1, b)
                    block_t((g0 + 1) % 2, b * KD * P, KD, n0 + 2 + b, hs).then_inc(S("block_done"), 1)
                with pe.Fori(1, KF // 2) as i:
                    for j in range(2):
                        for b in range(2):
                            pe.wait_ge(S("block_freed"), i * 4 + (n0 + 2 * j + b - 3))
                            pe.wait_ge(S("w_lo"), i * 4 + (2 * (g0 + j) + b + 1))
                            block_t((g0 + j) % 2, b * KD * P, KD, n0 + 2 * j + b, hs).then_inc(S("block_done"), 1)

            def down(f):
                g0, n0 = FIRST[f"w_dn{f}"], BLOCKS[f"dn{f}"]
                half = KF // 2
                pe.wait_ge(S("hid_lo"), KF * (f + 1))
                with pe.Fori(0, 2) as i:
                    for o in range(4):
                        n, g = n0 + o, g0 + 2 * o
                        pe.wait_ge(S("block_freed"), i * 4 + (n - 3))
                        for part in range(2):
                            pe.wait_ge(S("w_lo"), i * 16 + (2 * (g + part) + 1))
                            block_t((g + part) % 2, 0, 6, n, hid, half * part, part == 0, False)
                            pe.wait_ge(S("w_lo"), i * 16 + (2 * (g + part) + 2))
                            m = block_t((g + part) % 2, 6 * P, 5, n, hid, half * part + 6, False, part == 1)
                            m.then_inc(S("block_done" if part else "part_done"), 1)

            def have(*blocks):
                pe.wait_ge(S("block_freed"), max(blocks) + 1)

            def take(step):
                if step in TURN_A and TURN_A[step]:
                    pe.wait_ge(S("a_freed"), TURN_A[step])
                return area_a

            def take_t(step):
                if TURN_T[step]:
                    pe.wait_ge(S("t_freed"), TURN_T[step])
                return area_t

            flat = lambda v: v.rearrange("p a b -> p (a b)")

            def attend(step, pt0, pt1, value, turned, per_pair):
                pe.wait_ge(S("t_freed"), TURN_T[turned] + 1)
                o = take(step)
                for j in range(4):
                    h = j if step == "dsa_o" else HEAD_OF_SLOT[j]
                    if per_pair is None:
                        dst = o[:, h, :]
                    else:
                        dst = o[cols(h), h // 2, :]
                    mm(dst, value(0, h), pt0[:, j, :], True, False)
                    m = mm(dst[:, P:T], value(1, h), pt1[:, j, :], False, True)
                m.then_inc(S("a_full"), 1)

            def transposes(step, probs, tt, tag, turn):
                pe.wait_ge(S(tag), turn)
                t = flat(take_t(step))
                for c in range(tt + 1):
                    for h in range(4):
                        m = nc.tensor.transpose(t[:, 512 * c + P * h:512 * c + P * (h + 1)],
                                                probs[:, h, P * c:P * (c + 1)], ident)
                m.then_inc(S("t_full"), 1)

            def level(step):
                lv = int(step[3:])
                pe.wait_ge(S("level_e"), lv + 1)
                o = take(step) if step in TURN_A else take_t(step)
                for h in range(B_H):
                    for tt in range(NT):
                        at_ = slice(T * h + P * tt, T * h + P * tt + P)
                        if lv == 0:
                            w, m_ = hk[:, at_], flat(bq)[:, at_]
                        else:
                            w = m_ = he[lv % 2][:, at_]
                        m = mm(o[:, h, queries(tt)], w, m_, True, True)
                m.then_inc(S("a_full" if step in TURN_A else "t_full"), 1)

            def step(name):
                if name in NORMS:
                    t = take_t(name)
                    if name in SUMMED:
                        i = SUMMED_NORMS.index(name)
                        pe.wait_ge(S("squares_added"), (KD - 2) * (i + 1))
                        mm(t[:, 0, :], ones, sq_sum[:], True, False)
                        pe.wait_ge(S("square"), KD * (i + 1))
                        m = mm(t[:, 0, :], ones, sq_ring[:, (KD - 1) % 2, :], False, True)
                    else:
                        for k in range(KD):
                            pe.wait_ge(S("direct_square"), KD * DIRECT_NORMS.index(name) + k + 1)
                            m = mm(t[:, 0, :], ones, sq[:, k, :], k == 0, k == KD - 1)
                    m.then_inc(S("t_full"), 1)
                elif name.startswith("idx"):
                    tt, hg = int(name[3]), int(name[4])
                    have(BLOCKS["kpe_ik"] + 1, BLOCKS["iq"] + 3)
                    o = take(name)
                    for j in range(4):
                        h = 4 * hg + HEAD_OF_SLOT[j]
                        m = mm(o[:, j, 0:keys(tt)], iq[cols(h), h // 2, queries(tt)], ik[cols(h), 0:keys(tt)],
                               True, True)
                    m.then_inc(S("a_full"), 1)
                elif name.startswith("dsa_s"):
                    tt = int(name[5])
                    have(BLOCKS["projT_b"] + 4)
                    o = take(name)
                    for h in range(A_H):
                        m = mm(o[:, h, 0:keys(tt)], aq[:, h, queries(tt)], ak[:, 0:keys(tt)], True, True)
                    m.then_inc(S("a_full"), 1)
                elif name.startswith("dsa_t"):
                    transposes(name, d_p, int(name[5]), "dsa_probs", int(name[5]) + 1)
                elif name == "dsa_o":
                    attend(name, d_pt0, d_pt1, lambda c, h: av[:, c, :], "dsa_t1", None)
                elif name in ("norm_cq", "norm_ckv"):
                    n = 3 if name == "norm_cq" else 2
                    pe.wait_ge(S("mla_squares"), 1 if n == 3 else 2)
                    t = take_t(name)
                    for k in range(n):
                        m = mm(t[:, 0, :], ones, nsq[:, k, :], k == 0, k == n - 1)
                    m.then_inc(S("t_full"), 1)
                elif name == "rope_k":
                    have(BLOCKS["kpe_ik"])
                    o = take(name)
                    mm(o[:, 0, :], swap, kpe[:], True, True).then_inc(S("a_full"), 1)
                elif name == "rope_q":
                    have(BLOCKS["q_c"] + 5)
                    o = take(name)
                    for j in range(2):
                        m = mm(o[:, j, :], swap, qpe[:, j, :], True, True)
                    m.then_inc(S("a_full"), 1)
                elif name.startswith("mla_s"):
                    tt = int(name[5])
                    have(BLOCKS["kv_c"] + 5)
                    pe.wait_ge(S("rope_done"), 3)
                    o = take(name)
                    for j, h in enumerate(HEAD_OF_SLOT):
                        mm(o[:, j, 0:keys(tt)], qn[:, h, queries(tt)], kn[:, h, 0:keys(tt)], True, False)
                        m = mm(o[:, j, 0:keys(tt)], qpe[cols(h), h // 2, queries(tt)], kpe[cols(h), 0:keys(tt)],
                               False, True)
                    m.then_inc(S("a_full"), 1)
                elif name.startswith("mla_t"):
                    transposes(name, m_p, int(name[5]), "mla_probs", int(name[5]) + 1)
                elif name == "mla_o":
                    attend(name, m_pt0, m_pt1, lambda c, h: vc[:, c, P * h:P * h + P], "mla_t1", None)
                elif name.startswith("lev") and not name.startswith("level"):
                    level(name)
                elif name == "far":
                    pe.wait_ge(S("level_e"), 9)
                    o = take(name)
                    for h in range(B_H):
                        m = mm(o[:, h, 0:P], he[0][:, T * h:T * h + P], he[0][:, T * h + P:T * h + T], True, True)
                    m.then_inc(S("a_full"), 1)
                elif name == "hgrn_o":
                    pe.wait_ge(S("hgrn_merged"), 9)
                    o = take(name)
                    for h in range(B_H):
                        for tt in range(NT):
                            v = slice(P * h, P * h + P)
                            m = mm(o[:, h, queries(tt)], bi[:, tt, v], h0[:, h, queries(tt)], True, tt == 0)
                            if tt:
                                m = mm(o[:, h, queries(1)], bi[:, 0, v], h1[:, h, :], False, True)
                    m.then_inc(S("a_full"), 1)
                elif name == "hgrn_n":
                    pe.wait_ge(S("hgrn_squares"), 1)
                    t = flat(take_t(name))
                    for j in range(2):
                        m = mm(t[:, 512 * j:512 * j + 512], ones, hx[0][:, 512 * j:512 * j + 512], True, True)
                    m.then_inc(S("t_full"), 1)
                elif name in ("norm_fq", "norm_fk"):
                    pe.wait_ge(S("fox_squares"), 1 if name == "norm_fq" else 2)
                    t = flat(take_t(name))
                    for j in range(2):
                        m = mm(t[:, 512 * j:512 * j + 512], ones64, flat(n2sq)[:, 512 * j:512 * j + 512], True, True)
                    m.then_inc(S("t_full"), 1)
                elif name == "forget":
                    pe.wait_ge(S("log_forget"), 1)
                    t = take_t(name)
                    tri = con[:, C_TRI:C_TRI + T]
                    mm(t[0:FOX_H, 0, :], flog[:, 0, :], tri, True, False)
                    mm(t[0:FOX_H, 0, P:T], flog[:, 1, :], tri[:, 0:P], False, True).then_inc(S("t_full"), 1)
                elif name.startswith(("fox_s", "sb_s")):
                    fox = name[0] == "f"
                    hg, tt = int(name[-2]), int(name[-1])
                    q, k = (fq, fk) if fox else (sq_, sk_)
                    if fox:
                        pe.wait_ge(S("fox_normed"), 2)
                        pe.wait_ge(S("t_freed"), TURN_T["forget"] + 1)
                    else:
                        have(BLOCKS["qk2"] + 15)
                    o = take(name)
                    for j in range(4):
                        h = 4 * hg + HEAD_OF_SLOT[j]
                        dst = o[:, j, 0:keys(tt)]
                        m = mm(dst, q[cols(h), h // 2, queries(tt)], k[cols(h), h // 2, 0:keys(tt)], True, not fox)
                        if fox:
                            m = mm(dst, con[0:FOX_H, C_SEL + P * h:C_SEL + P * h + P], negf[0:FOX_H, 0:keys(tt)],
                                   False, True)
                    m.then_inc(S("a_full"), 1)
                elif name.startswith(("fox_t", "sb_t")):
                    fox = name[0] == "f"
                    hg, tt = int(name[-2]), int(name[-1])
                    transposes(name, f_p if fox else s_z, tt, "fox_probs" if fox else "sb_probs", 2 * hg + tt + 1)
                elif name.startswith(("fox_o", "sb_o")):
                    fox = name[0] == "f"
                    hg = int(name[-1])
                    v = fv if fox else sv
                    attend(name, f_pt0 if fox else s_pt0, f_pt1 if fox else s_pt1,
                           lambda c, h: v[:, c, HD * (4 * hg + h):HD * (4 * hg + h + 1)],
                           f"fox_t{hg}1" if fox else f"sb_t{hg}1", 0)

            pe.wait_ge(S("con_loaded"), 16 * 5)
            for kind, what in ORDER:
                if kind == "tile":
                    tile(what)
                elif kind == "step":
                    step(what)
                elif "gu" in what:
                    gate_up(int(what[-1]))
                else:
                    down(int(what[-1]))

        def softmax_columns(tag):
            i = 12 * ("dsa", "mla", "fox").index(tag)
            return st[:, i:i + 4], st[:, i + 4:i + 8], st[:, i + 8:i + 12]

        SUM_DEST = {}

        def dest(first, views):
            for k, v in enumerate(views):
                SUM_DEST[BLOCKS[first] + k if isinstance(first, str) else first + k] = v

        dest("kpe_ik", [kpe[:], ik[:]])
        dest("iq", [iq[:, k, :] for k in range(4)])
        dest("projT_b", [ak[:]] + [aq[:, k, :] for k in range(4)] + [cq[:, k, :] for k in range(3)]
             + [ckv[:, k, :] for k in range(2)] + [bf[:, k, :] for k in range(4)])
        dest("bq", [bq[:, k, :] for k in range(4)])
        dest("bg", [bg[:, k, :] for k in range(4)])
        dest("q_c", [qn[:, k, :] for k in range(4)] + [qpe[:, k, :] for k in range(2)])
        dest("kv_c", [kn[:, k, :] for k in range(4)])
        dest("gates1", [gates[:, k, :] for k in range(24)])
        dest("up1", [up1[:, k % 4, :] for k in range(24)])
        dest("qk2", [qk2[:, k, :] for k in range(16)])
        dest("gates2", [gates2[:, k, :] for k in range(16)])
        dest("up2", [up2[:, k % 4, :] for k in range(16)])
        dest("pgp", [pg[:, k, :] for k in range(8)] + [pp[:, k % 2, :] for k in range(8)])
        RESIDUAL = {BLOCKS[b] + k: (k, 1.0 if b in ("out1", "dn0") or b == "out2" else 0.5)
                    for b in ("out1", "dn0", "dn1", "out2", "dn2") for k in range(KD)}
        ENDING = {}
        for n_, g_ in ENDS.items():
            ENDING.setdefault(g_, []).append(n_)

        @block.scalar
        def _(act):
            def fn(out, in_, f, **kw):
                return nc.scalar.activation(out, in_, f, **kw)

            def link(ins):
                link.n += 1
                ins.then_inc(S("act_step"), 1)
                act.wait_ge(S("act_step"), link.n)
            link.n = 0

            flat = lambda v: v.rearrange("p a b -> p (a b)")

            def split_high(g, half):
                if g >= len(TILES):
                    return
                _, _, n, mid = TILES[g]
                if half == 0:
                    act.wait_ge(S(f"w_loaded{g % 2}"), 16 * (g // 2 + 1))
                    if g >= 2:
                        s, v = free_value(g - 2)
                        act.wait_ge(S(s), v)
                c = slice(0, mid) if half == 0 else slice(mid, n)
                fn(whi[:, g % 2, c], raw[:, g % 2, c], ACT.Copy).then_inc(S("w_hi"), 1)

            def square(n):
                i, k = SQUARED[n]
                act.wait_ge(S("block_freed"), n + 1)
                if k >= 2 or i:
                    act.wait_ge(S("squares_added"), (KD - 2) * i + (max(k - 2, 1) if k >= 2 else 0))
                if i and k < 2:
                    act.wait_ge(S("t_full"), TURN_T[SUMMED_NORMS[i - 1]] + 1)
                fn(sq_ring[:, k % 2, :], x[:, k, :], ACT.Square).then_inc(S("square"), 1)

            def tile(g):
                split_high(g + 1, 0)
                blocks = ENDING.get(g, [])
                for n in blocks:
                    if n in SQUARED and SQUARED[n][1]:
                        square(n - 1)
                    if n in SUM_DEST or n in RESIDUAL:
                        act.wait_ge(S("block_done"), n + 1)
                        fn(tmp[:, n % 4, :], acc[n % 4][:, T:2 * T], ACT.Copy,
                           scale=RESIDUAL.get(n, (0, 1.0))[1]).then_inc(S("half_copied"), 1)
                split_high(g + 1, 1)
                if g == FIRST["w_pg"] + 3:
                    act.wait_ge(S("block_freed"), BLOCKS["pgp"] + 8)
                    fn(flat(pg[:, :, :]), flat(pg[:, :, :]), ACT.Sigmoid).then_inc(S("ple_gate"), 1)

            def gate_up(f):
                g0, n0 = FIRST[f"w_gu{f}"], BLOCKS[f"gu{f}"]

                def split_next(t, j, half):
                    if isinstance(t, int):
                        split_high(g0 + t + 1, half)
                        return
                    c = slice(half * KD * P, (half + 1) * KD * P)
                    if half == 0:
                        act.wait_ge(S(f"w_loaded{1 - j}"), (t - j) * 8 + (16 * ((g0 + j + 1) // 2) + 16))
                    fn(whi[:, 1 - j, c], raw[:, 1 - j, c], ACT.Copy).then_inc(S("w_hi"), 1)

                def copy_half(t, j, b):
                    k = (n0 + 2 * j + b) % 4
                    act.wait_ge(S("block_done"), t * 2 + (n0 + b + 1))
                    fn(tmp[:, k, :], acc[k][:, T:2 * T], ACT.Copy).then_inc(S("half_copied"), 1)

                def body(t, j, first=False, last=False):
                    if not first:
                        act.wait_ge(S("block_freed"), t * 2 + (n0 - 1))
                        fn(sbuf[:, 1 - j, :], gbuf[:, 1 - j, :], ACT.Silu).then_inc(S("silu"), 1)
                        copy_half(t - 1, 1 - j, 1)
                    if not last:
                        split_next(t, j, 0)
                        split_next(t, j, 1)
                    if not first:
                        act.wait_ge(S("hid_value"), t + KF * f)
                        fn(hid[:, t - 1, 0:T], hbuf[:, 1 - j, :], ACT.Copy).then_inc(S("hid_hi"), 1)
                    if not last:
                        copy_half(t, j, 0)

                body(0, 0, first=True)
                with act.Fori(0, KF // 2 - 1) as i:
                    body(i * 2 + 1, 1)
                    body(i * 2 + 2, 0)
                body(KF - 1, 1)
                body(KF, 0, last=True)

            def down(f):
                for g in range(FIRST[f"w_dn{f}"], FIRST[f"w_dn{f}"] + 16):
                    tile(g)

            def hs_high(name, value_sem, value_base, src, chunks=range(KD)):
                for k in chunks:
                    act.wait_ge(S(value_sem), value_base + k + 1)
                    fn(hs[:, k, 0:T], src(k), ACT.Copy).then_inc(S("hs_hi"), 1)

            def norm(name):
                if name in SUMMED:
                    square(BLOCKS[SUMMED[name]] + KD - 1)
                else:
                    if name == "norm0":
                        act.wait_ge(S("x_loaded"), 16)
                    for k in range(KD):
                        if name == "norm3":
                            act.wait_ge(S("x_normed"), k + 1)
                        fn(sq[:, k, :], x[:, k, :], ACT.Square).then_inc(S("direct_square"), 1)
                act.wait_ge(S("t_full"), TURN_T[name] + 1)
                fn(xr[:], area_t[:, 0, :], ACT.Sqrt, scale=1.0 / D, bias=epsb[:, 0:1]).then_inc(S("t_freed"), 1)
                if name in HS_NORMS:
                    hs_high(name, "h_value", KD * HS_NORMS.index(name), lambda k: tmp[:, k % 4, :])

            def exps(tag, sc, p, tt, n):
                neg, sums, _ = softmax_columns(tag)
                act.wait_ge(S(f"{tag}_negmax"), n)
                for h in range(4):
                    m = fn(p[:, h, 0:keys(tt)], sc[:, h, 0:keys(tt)], ACT.Exp, bias=neg[:, h:h + 1],
                           accum_out=sums[:, h:h + 1])
                m.then_inc(S(f"{tag}_exp"), 1)

            def turned(step, tag, tt, pt0, pt1):
                act.wait_ge(S("t_full"), TURN_T[step] + 1)
                t = flat(area_t)
                if tt:
                    fn(pt1[:, :, :], t[:, 512:1024].rearrange("p (h n) -> p h n", h=4), ACT.Copy)
                fn(pt0[:, :, queries(tt)], t[:, 0:512].rearrange("p (h n) -> p h n", h=4), ACT.Copy)\
                    .then_inc(S("t_freed"), 1)

            def out_high(step, dst):
                act.wait_ge(S("a_full"), TURN_A[step] + 1)
                n = dst.shape[1]
                fn(dst, area_a[:, 0:n, :], ACT.Copy).then_inc(S("mix_hi"), 1)

            def log1p_exp(v, s):
                link(fn(v, v, ACT.Exp, scale=-1.0))
                fn(v, v, ACT.Ln, bias=1.0).then_inc(S(s), 1)

            def rms_factor(out, ps, width, free_sem):
                link(fn(out, ps, ACT.Ln, scale=1.0 / width, bias=epsb[:, 0:1]))
                fn(out, out, ACT.Exp, scale=-0.5).then_inc(S(free_sem), 1)

            def step(name):
                if name in NORMS:
                    norm(name)
                elif name == "tables":
                    act.wait_ge(S("angles"), 1)
                    fn(sin[:], rest[:], ACT.Sin).then_inc(S("sines"), 1)
                    fn(cos[:], over[:], ACT.Sin).then_inc(S("sines"), 1)
                elif name.startswith("idx"):
                    tt, hg = int(name[3]), int(name[4])
                    act.wait_ge(S("a_full"), TURN_A[name] + 1)
                    if tt:
                        act.wait_ge(S("scored"), 1)
                    fn(relu_l[:, 4 * hg:4 * hg + 4, 0:keys(tt)], area_a[:, :, 0:keys(tt)], ACT.Relu,
                       scale=IDX_D ** -0.5 * IDX_H ** -0.5).then_inc(S("a_freed"), 1)
                elif name.startswith("dsa_s"):
                    exps("dsa", d_sc, d_p, int(name[5]), int(name[5]) + 1)
                elif name.startswith("dsa_t"):
                    turned(name, "dsa", int(name[5]), d_pt0, d_pt1)
                elif name == "dsa_o":
                    out_high(name, osplit[0][:, :, 0:T])
                elif name in ("norm_cq", "norm_ckv"):
                    q = name == "norm_cq"
                    n, src = (3, cq) if q else (2, ckv)
                    act.wait_ge(S("block_freed"), BLOCKS["projT_b"] + (8 if q else 10))
                    if q:
                        act.wait_ge(S("sines"), 2)
                    else:
                        act.wait_ge(S("cq_split"), 3)
                    fn(flat(nsq[:, 0:n, :]), flat(src[:, :, :]), ACT.Square).then_inc(S("mla_squares"), 1)
                    act.wait_ge(S("t_full"), TURN_T[name] + 1)
                    rms_factor(nrm[:], area_t[:, 0, :], n * P, "t_freed")
                    act.wait_ge(S("mla_value"), 1 if q else 2)
                    out = cqs if q else ckvs
                    fn(out[:, :, 0:T], nval[:, 0:n, :], ACT.Copy).then_inc(S("mla_hi"), 1)
                elif name.startswith("mla_s"):
                    exps("mla", m_sc, m_p, int(name[5]), int(name[5]) + 1)
                elif name.startswith("mla_t"):
                    turned(name, "mla", int(name[5]), m_pt0, m_pt1)
                elif name == "mla_o":
                    out_high(name, osplit[2][:, :, 0:T])
                elif name == "decay":
                    act.wait_ge(S("lb_diff"), 1)
                    fn(st[:, 44:48], st[:, 40:44], ACT.Exp).then_inc(S("lb_exp"), 1)
                    act.wait_ge(S("lb_ready"), 1)
                    link(fn(st[:, 64:68], st[:, 60:64], ACT.Ln))
                    fn(st[:, 68:72], st[:, 56:60], ACT.Ln, scale=-1.0, bias=1.0).then_inc(S("lb_logs"), 1)
                    act.wait_ge(S("block_freed"), BLOCKS["projT_b"] + 14)
                    act.wait_ge(S("decay_space"), 1)
                    link(fn(hx[0][:], flat(bf[:, :, :]), ACT.Abs))
                    log1p_exp(hx[0][:], "sig_log")
                    act.wait_ge(S("decay_u"), 1)
                    link(fn(hx[0][:], hx[0][:], ACT.Abs))
                    log1p_exp(hx[0][:], "decay_log")
                    act.wait_ge(S("decay_sum"), 1)
                    fn(hk[:], flat(bf[:, :, :]), ACT.Sigmoid, scale=-1.0).then_inc(S("key_sig"), 1)
                elif name.startswith("level_e") and name != "level_e0":
                    lv = int(name[7:])
                    e = he[lv % 2]
                    act.wait_ge(S("exponents"), lv)
                    fn(e[:], e[:], ACT.Exp).then_inc(S("decays"), 1)
                elif name == "hgrn_n":
                    act.wait_ge(S("t_full"), TURN_T[name] + 1)
                    rms_factor(hx[1][:], flat(area_t), P, "t_freed")
                    act.wait_ge(S("block_freed"), BLOCKS["bg"] + 4)
                    fn(hx[0][:], flat(bg[:, :, :]), ACT.Silu).then_inc(S("hgrn_gate"), 1)
                    act.wait_ge(S("hgrn_value"), 1)
                    fn(osplit[1][:, :, 0:T], hx[2][:].rearrange("p (h n) -> p h n", h=4), ACT.Copy)\
                        .then_inc(S("hgrn_hi"), 1)
                elif name == "hgrn_o":
                    act.wait_ge(S("a_full"), TURN_A[name] + 1)
                    fn(hx[0][:], flat(area_a), ACT.Square).then_inc(S("hgrn_squares"), 1)
                elif name == "gate_sigmoid1":
                    for b in range(3):
                        act.wait_ge(S("block_freed"), BLOCKS["gates1"] + 24)
                        v = flat(gates[:, 8 * b:8 * b + 8, :])
                        fn(v, v, ACT.Sigmoid).then_inc(S("gates_on"), 1)
                elif name == "gate_sigmoid2":
                    for b in range(2):
                        act.wait_ge(S("block_freed"), BLOCKS["gates2"] + 16)
                        v = flat(gates2[:, 8 * b:8 * b + 8, :])
                        fn(v, v, ACT.Sigmoid).then_inc(S("gates_on"), 1)
                elif name.startswith("split_mixed"):
                    base_ = 16 if name[-1] == "1" else 24 + 8
                    m = mixed1 if name[-1] == "1" else mixed2
                    hs_high(name, "mixed", base_, lambda k: m[:, k, :], range(4, KD))
                elif name.startswith("half_mixed"):
                    base_ = 16 if name[-1] == "1" else 24 + 8
                    m = mixed1 if name[-1] == "1" else mixed2
                    hs_high(name, "mixed", base_, lambda k: m[:, k, :], range(4))
                elif name in ("norm_fq", "norm_fk"):
                    q = name == "norm_fq"
                    src = fq if q else fk
                    act.wait_ge(S("block_freed"), BLOCKS["qk2"] + (4 if q else 8))
                    if not q:
                        act.wait_ge(S("fox_normed"), 1)
                    fn(n2sq[:, :, :], src, ACT.Square).then_inc(S("fox_squares"), 1)
                    act.wait_ge(S("t_full"), TURN_T[name] + 1)
                    rms_factor(flat(n2r[:, :, :]), flat(area_t), HD, "t_freed")
                elif name == "forget":
                    act.wait_ge(S("block_freed"), BLOCKS["fvl"] + 4)
                    link(fn(flog2[:], flat(flog[:, :, :]), ACT.Abs))
                    log1p_exp(flog2[:], "forget_log")
                    act.wait_ge(S("t_full"), TURN_T[name] + 1)
                    fn(negf[0:FOX_H, :], area_t[0:FOX_H, 0, :], ACT.Copy, scale=-float(HD) ** 0.5)\
                        .then_inc(S("t_freed"), 1)
                elif name.startswith("fox_s"):
                    hg, tt = int(name[-2]), int(name[-1])
                    exps("fox", f_sc, f_p, tt, 2 * hg + tt + 1)
                elif name.startswith("sb_s"):
                    hg, tt = int(name[-2]), int(name[-1])
                    n = 2 * hg + tt + 1
                    act.wait_ge(S("a_full"), TURN_A[name] + 1)
                    if n > 1:
                        act.wait_ge(S("sb_arg"), n - 1)
                    ks = keys(tt)
                    link(fn(s_a[:, :, 0:ks], area_a[:, :, 0:ks], ACT.Abs, scale=HD ** -0.5))
                    link(fn(s_a[:, :, 0:ks], s_a[:, :, 0:ks], ACT.Exp, scale=-1.0))
                    fn(s_a[:, :, 0:ks], s_a[:, :, 0:ks], ACT.Ln, bias=1.0).then_inc(S("sb_log"), 1)
                    act.wait_ge(S("sb_arg"), n)
                    fn(s_z[:, :, 0:ks], s_z[:, :, 0:ks], ACT.Exp).then_inc(S("sb_probs"), 1)
                elif name.startswith("fox_t"):
                    turned(name, "fox", int(name[-1]), f_pt0, f_pt1)
                elif name.startswith("sb_t"):
                    turned(name, "sb", int(name[-1]), s_pt0, s_pt1)
                elif name.startswith(("fox_o", "sb_o")):
                    hg = int(name[-1])
                    out_high(name, osplit2[0 if name[0] == "f" else 1][:, 2 * hg:2 * hg + 2, 0:T])
                elif name == "split_p":
                    act.wait_ge(S("p_loaded"), 16)
                    fn(ps[:, :, 0:T], praw[:, :, :], ACT.Copy).then_inc(S("p_hi"), 1)

            act.wait_ge(S("eps_set"), 1)
            split_high(0, 0)
            split_high(0, 1)
            for kind, what in ORDER:
                if kind == "tile":
                    tile(what)
                elif kind == "step":
                    step(what)
                elif "gu" in what:
                    gate_up(int(what[-1]))
                else:
                    down(int(what[-1]))

        @block.vector
        def _(dve):
            v = nc.vector
            flat = lambda w: w.rearrange("p a b -> p (a b)")

            def link(ins):
                link.n += 1
                ins.then_inc(S("dve_step"), 1)
                dve.wait_ge(S("dve_step"), link.n)
            link.n = 0

            def split_low(g, half):
                if g >= len(TILES):
                    return
                _, _, n, mid = TILES[g]
                dve.wait_ge(S("w_hi"), 2 * g + half + 1)
                c = slice(0, mid) if half == 0 else slice(mid, n)
                v.tensor_tensor(wlo[:, g % 2, c], raw[:, g % 2, c], whi[:, g % 2, c].bitcast(F32), ALU.subtract)\
                    .then_inc(S("w_lo"), 1)

            halves = [0]

            def read_block(n):
                if n in SUM_DEST or n in RESIDUAL:
                    halves[0] += 1
                    dve.wait_ge(S("half_copied"), halves[0])
                    bank, t = acc[n % 4][:, 0:T], tmp[:, n % 4, :]
                else:
                    dve.wait_ge(S("block_done"), n + 1)
                    bank = acc[n % 4]
                if n in RESIDUAL:
                    k, scale = RESIDUAL[n]
                    link(v.tensor_tensor(t, t, x[:, k, :], ALU.add))
                    v.scalar_tensor_tensor(x[:, k, :], bank, scale, t, ALU.mult, ALU.add)\
                        .then_inc(S("block_freed"), 1)
                elif n in SUM_DEST:
                    u = None
                    if 0 <= n - BLOCKS["up1"] < 24:
                        u = n - BLOCKS["up1"]
                    elif 0 <= n - BLOCKS["up2"] < 16:
                        u = n - BLOCKS["up2"] + 24
                    if u is not None and u >= 4:
                        dve.wait_ge(S("mixed"), u - 3)
                    v.tensor_tensor(SUM_DEST[n], bank, t, ALU.add).then_inc(S("block_freed"), 1)
                elif n - BLOCKS["avw"] in (0, 1):
                    tt = n - BLOCKS["avw"]
                    v.tensor_copy(av[:, tt, :], bank[:, 0:P])
                    v.tensor_copy(iw[:, tt, :], bank[:, P:AVW]).then_inc(S("block_freed"), 1)
                elif n - BLOCKS["fvl"] in (2, 3):
                    dve.wait_ge(S("fb_loaded"), 16)
                    v.tensor_tensor(flog[:, n - BLOCKS["fvl"] - 2, :], bank[:, 0:FOX_H], fb[:], ALU.add)\
                        .then_inc(S("block_freed"), 1)
                else:
                    for name, buf, first in (("bi", bi, 0), ("kv_c", vc, 4), ("fvl", fv, 0), ("sv", sv, 0)):
                        if n - BLOCKS[name] - first in (0, 1):
                            v.tensor_copy(buf[:, n - BLOCKS[name] - first, :], bank[:, :])\
                                .then_inc(S("block_freed"), 1)
                            break
                    else:
                        raise AssertionError(n)
                if n >= BLOCKS["pgp"] + 8:
                    k = n - BLOCKS["pgp"] - 8
                    dve.wait_ge(S("ple_gate"), 1)
                    dve.wait_ge(S("block_freed"), n + 1)
                    link(v.tensor_tensor(pp[:, k % 2, :], pp[:, k % 2, :], pg[:, k, :], ALU.mult))
                    v.tensor_tensor(x[:, k, :], x[:, k, :], pp[:, k % 2, :], ALU.add).then_inc(S("out_ready"), 1)

            def tile(g):
                blocks = ENDING.get(g, [])
                split_low(g + 1, 0)
                for n in blocks[:len(blocks) // 2]:
                    read_block(n)
                split_low(g + 1, 1)
                for n in blocks[len(blocks) // 2:]:
                    read_block(n)

            def gate_up(f):
                g0, n0 = FIRST[f"w_gu{f}"], BLOCKS[f"gu{f}"]
                c0 = halves[0]

                def split_next(t, j, half):
                    if isinstance(t, int):
                        split_low(g0 + t + 1, half)
                        return
                    c = slice(half * KD * P, (half + 1) * KD * P)
                    dve.wait_ge(S("w_hi"), t * 2 + (2 * g0 + half + 3))
                    v.tensor_tensor(wlo[:, 1 - j, c], raw[:, 1 - j, c], whi[:, 1 - j, c].bitcast(F32),
                                    ALU.subtract).then_inc(S("w_lo"), 1)

                def sum_halves(t, j, b):
                    k = (n0 + 2 * j + b) % 4
                    dve.wait_ge(S("half_copied"), t * 2 + (c0 + b + 1))
                    v.tensor_tensor((gbuf, ubuf)[b][:, j, :], acc[k][:, 0:T], tmp[:, k, :], ALU.add)\
                        .then_inc(S("block_freed"), 1)

                def body(t, j, first=False, last=False):
                    if not first:
                        sum_halves(t - 1, 1 - j, 1)
                        dve.wait_ge(S("silu"), t + KF * f)
                        dve.wait_ge(S("block_freed"), t * 2 + n0)
                        v.tensor_tensor(hbuf[:, 1 - j, :], sbuf[:, 1 - j, :], ubuf[:, 1 - j, :], ALU.mult)\
                            .then_inc(S("hid_value"), 1)
                    if not last:
                        split_next(t, j, 0)
                        split_next(t, j, 1)
                    if not first:
                        dve.wait_ge(S("hid_hi"), t + KF * f)
                        v.tensor_tensor(hid[:, t - 1, T:2 * T], hbuf[:, 1 - j, :], hid[:, t - 1, 0:T].bitcast(F32),
                                        ALU.subtract).then_inc(S("hid_lo"), 1)
                    if not last:
                        sum_halves(t, j, 0)

                body(0, 0, first=True)
                with dve.Fori(0, KF // 2 - 1) as i:
                    body(i * 2 + 1, 1)
                    body(i * 2 + 2, 0)
                body(KF - 1, 1)
                body(KF, 0, last=True)
                halves[0] += 2 * KF

            def down(f):
                for g in range(FIRST[f"w_dn{f}"], FIRST[f"w_dn{f}"] + 16):
                    tile(g)

            def hs_low(name, k, src):
                base_ = KD * HS_STARTS.index(name.replace("half", "split"))
                dve.wait_ge(S("hs_hi"), base_ + k + 1)
                v.tensor_tensor(hs[:, k, T:2 * T], src, hs[:, k, 0:T].bitcast(F32), ALU.subtract)\
                    .then_inc(S("hs_lo"), 1)

            def norm(name):
                dve.wait_ge(S("t_freed"), TURN_T[name] + 1)
                link(v.reciprocal(xr[:], xr[:]))
                g = norm_of(name)
                for k in range(KD):
                    gain = vec[:, g + k:g + k + 1]
                    if name == "norm2":
                        v.scalar_tensor_tensor(x[:, k, :], x[:, k, :], gain, xr[:], ALU.mult, ALU.mult)\
                            .then_inc(S("x_normed"), 1)
                        continue
                    if k >= 2:
                        hs_low(name, k - 2, tmp[:, (k - 2) % 4, :])
                    v.scalar_tensor_tensor(tmp[:, k % 4, :], x[:, k, :], gain, xr[:], ALU.mult, ALU.mult)\
                        .then_inc(S("h_value"), 1)
                if name != "norm2":
                    for k in (KD - 2, KD - 1):
                        hs_low(name, k, tmp[:, k % 4, :])

            def softmax(tag, sc, p, tt, n):
                neg, sums, rec = softmax_columns(tag)
                ks = keys(tt)
                v.tensor_reduce(neg, sc[:, :, 0:ks], AX.X, ALU.max, negate=True).then_inc(S(f"{tag}_negmax"), 1)
                dve.wait_ge(S(f"{tag}_exp"), n)
                link(v.reciprocal(rec, sums))
                for h in range(4):
                    m = v.tensor_scalar(p[:, h, 0:ks], p[:, h, 0:ks], rec[:, h:h + 1], None, ALU.mult)
                m.then_inc(S(f"{tag}_probs"), 1)

            def out_low(step, dst, n_done):
                dve.wait_ge(S("mix_hi"), n_done)
                n = dst.shape[1]
                v.tensor_tensor(dst[:, :, T:2 * T], area_a[:, 0:n, :], dst[:, :, 0:T].bitcast(F32), ALU.subtract)\
                    .then_inc(S("a_freed"), 1)

            thresholds = bucket_thresholds()
            n_bias = [0]

            def bias_part(lo, hi):
                for b in range(lo, hi):
                    m = mask[b % 2]
                    link(v.tensor_scalar(m[:], dist[:], thresholds[b - 1], None, ALU.is_ge))
                    for h in range(A_H):
                        c = (b - 1) * A_H + h
                        ins = v.scalar_tensor_tensor(bias[:, h, :], m[:], drel[:, c:c + 1], bias[:, h, :],
                                                     ALU.mult, ALU.add)
                    link(ins)

            def top(tt):
                ks = keys(tt)
                sc, wk = score[:, 0:ks], work[:, 0:ks]
                dve.wait_ge(S("a_freed"), TURN_A[f"idx{tt}1"] + 1)
                dve.wait_ge(S("block_freed"), BLOCKS["avw"] + 2)
                for i in range(IDX_H):
                    into = causal(tt, C_CM) if i == 0 else sc
                    h = i // 4 * 4 + HEAD_OF_SLOT[i % 4]
                    ins = v.scalar_tensor_tensor(sc, relu_l[:, i, 0:ks], iw[:, tt, h:h + 1], into,
                                                 ALU.mult, ALU.add)
                    if i < IDX_H - 1:
                        link(ins)
                ins.then_inc(S("scored"), 1)
                dve.wait_ge(S("scored"), tt + 1)
                best = st[:, 80:88]
                cur = sc
                for r in range(TOPK // 8):
                    link(v.max(best, cur))
                    if r < TOPK // 8 - 1:
                        link(v.match_replace(wk, best, cur, -3e38))
                        cur = wk
                least = best[:, 7:8]
                count, need = st[:, 88:89], st[:, 89:90]
                gt, eq, rk = above[:, 0:ks], equal[:, 0:ks], rank[:, 0:ks]
                link(v.tensor_scalar(gt, sc, least, None, ALU.is_gt, ALU.add, accum_out=count))
                link(v.tensor_scalar(eq, sc, least, None, ALU.is_equal))
                link(v.tensor_scalar(need, count, -1.0, float(TOPK), ALU.mult, ALU.add))
                link(v.tensor_tensor_scan(rk, ones_row[:, 0:ks], eq, 0.0, ALU.mult, ALU.add))
                link(v.scalar_tensor_tensor(eq, rk, need, eq, ALU.is_le, ALU.mult))
                link(v.tensor_tensor(gt, gt, eq, ALU.add))
                link(v.tensor_scalar(gt, gt, -NEG, NEG, ALU.mult, ALU.add))
                link(v.tensor_tensor(gt, gt, causal(tt, C_CM), ALU.add))
                b = bias[:, :, 0:P] if tt == 0 else bias[:, :, P:P + T]
                link(v.tensor_tensor(b, b, heads4(gt, ks), ALU.add))

            def level_parts(buf, half):
                w = buf.rearrange("p (n s h) -> p n s h", s=2, h=half)
                return w[:, :, 0, :], w[:, :, 1, :]

            def exponents(lv):
                e = he[lv % 2][:]
                if lv >= 3:
                    dve.wait_ge(S("hgrn_merged"), lv - 1)
                if lv < 8:
                    half = LEVELS[lv]
                    bl, br = level_parts(hb[:], half)
                    el, er = level_parts(e, half)
                    n = bl.shape[1]
                    mid = bl[:, :, half - 1:half].to_broadcast([P, n, half])
                    v.tensor_tensor(el, mid, bl, ALU.subtract)
                    if half < CHUNK:
                        ins = v.tensor_tensor(er, br, mid, ALU.subtract)
                    else:
                        ins = v.tensor_copy(er, br)
                    ins.then_inc(S("exponents"), 1)
                else:
                    b4 = hb[:].rearrange("p (h c j) -> p h c j", h=B_H, j=CHUNK)
                    e4 = e.rearrange("p (h c j) -> p h c j", h=B_H, j=CHUNK)
                    for c in range(2):
                        last = b4[:, :, c, CHUNK - 1:CHUNK].to_broadcast([P, B_H, CHUNK])
                        v.tensor_tensor(e4[:, :, c, :], last, b4[:, :, c, :], ALU.subtract)
                    link(v.tensor_copy(e4[:, :, 2, :], b4[:, :, 2, :]))
                    last1 = b4[:, :, 1, CHUNK - 1:CHUNK].to_broadcast([P, B_H, CHUNK])
                    last2 = b4[:, :, 2, CHUNK - 1:CHUNK].to_broadcast([P, B_H, CHUNK])
                    link(v.tensor_tensor(e4[:, :, 0, :], e4[:, :, 0, :], last1, ALU.add))
                    v.tensor_tensor(e4[:, :, 3, :], b4[:, :, 3, :], last2, ALU.add).then_inc(S("exponents"), 1)
                dve.wait_ge(S("decays"), lv)
                half = LEVELS[lv] if lv < 8 else P
                el, er = level_parts(e, half)
                kl, _ = level_parts(hk[:], half)
                _, qr = level_parts(flat(bq[:, :, :]), half)
                v.tensor_tensor(el, el, kl, ALU.mult)
                v.tensor_tensor(er, er, qr, ALU.mult).then_inc(S("level_e"), 1)

            def step(name):
                if name in NORMS:
                    norm(name)
                elif name == "tables":
                    tables()
                elif name.startswith("bias"):
                    i = int(name[4])
                    bias_part(*[(1, 9), (9, 17), (17, 25), (25, 32)][i])
                elif name.startswith("top"):
                    top(int(name[3]))
                elif name.startswith("dsa_s"):
                    tt = int(name[5])
                    ks = keys(tt)
                    b = bias[:, :, 0:P] if tt == 0 else bias[:, :, P:P + T]
                    dve.wait_ge(S("a_full"), TURN_A[name] + 1)
                    v.scalar_tensor_tensor(d_sc[:, :, 0:ks], area_a[:, :, 0:ks], float(P) ** -0.5, b,
                                           ALU.mult, ALU.add).then_inc(S("a_freed"), 1)
                    dve.wait_ge(S("a_freed"), TURN_A[name] + 1)
                    softmax("dsa", d_sc, d_p, tt, tt + 1)
                elif name == "dsa_o":
                    out_low(name, osplit[0], 1)
                elif name in ("norm_cq", "norm_ckv"):
                    q = name == "norm_cq"
                    n, src, out, g = (3, cq, cqs, VEC["mla_q_norm"]) if q else (2, ckv, ckvs, VEC["mla_kv_norm"])
                    dve.wait_ge(S("t_freed"), TURN_T[name] + 1)
                    for k in range(n):
                        ins = v.scalar_tensor_tensor(nval[:, k, :], src[:, k, :], vec[:, g + k:g + k + 1], nrm[:],
                                                     ALU.mult, ALU.mult)
                    ins.then_inc(S("mla_value"), 1)
                    dve.wait_ge(S("mla_hi"), 1 if q else 2)
                    for k in range(n):
                        v.tensor_tensor(out[:, k, T:2 * T], nval[:, k, :], out[:, k, 0:T].bitcast(F32), ALU.subtract)\
                            .then_inc(S("cq_split" if q else "ckv_split"), 1)
                elif name == "rope_k":
                    rotate(name, 0, kpe[:], True)
                elif name == "rope_q":
                    for j in range(2):
                        rotate(name, j, qpe[:, j, :], j == 1)
                elif name.startswith("mla_s"):
                    tt = int(name[5])
                    ks = keys(tt)
                    dve.wait_ge(S("a_full"), TURN_A[name] + 1)
                    v.scalar_tensor_tensor(m_sc[:, :, 0:ks], area_a[:, :, 0:ks], float(NOPE + ROPE) ** -0.5,
                                           heads4(causal(tt, C_CM), ks), ALU.mult, ALU.add)\
                        .then_inc(S("a_freed"), 1)
                    dve.wait_ge(S("a_freed"), TURN_A[name] + 1)
                    softmax("mla", m_sc, m_p, tt, tt + 1)
                elif name == "mla_o":
                    out_low(name, osplit[2], 2)
                elif name == "decay":
                    decay()
                elif name == "level_e0":
                    dve.wait_ge(S("key_sig"), 1)
                    for h in range(B_H):
                        s = slice(T * h, T * h + T)
                        v.tensor_scalar(hk[:, s], hk[:, s], st[:, 72 + h:73 + h], None, ALU.mult)
                    v.memset(flat(h0[:, :, :]), 0.0)
                    dve.wait_ge(S("block_freed"), BLOCKS["bq"] + 4)
                    v.tensor_scalar(flat(bq[:, :, :]), flat(bq[:, :, :]), float(P) ** -0.5, None, ALU.mult)\
                        .then_inc(S("level_e"), 1)
                    dve.wait_ge(S("level_e"), 1)
                elif name.startswith("level_e"):
                    exponents(int(name[7:]))
                elif name.startswith("lev"):
                    lv = int(name[3:])
                    in_a = name in TURN_A
                    dve.wait_ge(S("a_full" if in_a else "t_full"), (TURN_A if in_a else TURN_T)[name] + 1)
                    m = con[:, C_LEV + P * lv:C_LEV + P * (lv + 1)].bitcast(I32).unsqueeze(1)
                    out = h0[:, :, :].rearrange("p h (t n) -> p (h t) n", n=P)
                    src = (area_a if in_a else area_t)[:, :, :].rearrange("p h (t n) -> p (h t) n", n=P)
                    v.copy_predicated(out, m.to_broadcast([P, 8, P]), src)\
                        .then_inc(S("a_freed" if in_a else "t_freed"), 1)
                    dve.wait_ge(S("a_freed" if in_a else "t_freed"), (TURN_A if in_a else TURN_T)[name] + 1)
                    dve.sem_inc(S("hgrn_merged"), 1)
                elif name == "far":
                    dve.wait_ge(S("a_full"), TURN_A[name] + 1)
                    v.tensor_copy(h1[:, :, :], area_a[:, :, 0:P]).then_inc(S("a_freed"), 1)
                    dve.wait_ge(S("a_freed"), TURN_A[name] + 1)
                    dve.sem_inc(S("hgrn_merged"), 1)
                elif name == "hgrn_n":
                    dve.wait_ge(S("t_freed"), TURN_T[name] + 1)
                    g = VEC["hgrn_out"]
                    v.scalar_tensor_tensor(hx[2][:], flat(area_a), vec[:, g:g + 1], hx[1][:], ALU.mult, ALU.mult)\
                        .then_inc(S("a_freed"), 1)
                    dve.wait_ge(S("a_freed"), TURN_A["hgrn_o"] + 1)
                    dve.wait_ge(S("hgrn_gate"), 1)
                    v.tensor_tensor(hx[2][:], hx[2][:], hx[0][:], ALU.mult).then_inc(S("hgrn_value"), 1)
                    dve.wait_ge(S("hgrn_hi"), 1)
                    v.tensor_tensor(osplit[1][:, :, T:2 * T], hx[2][:].rearrange("p (h n) -> p h n", h=4),
                                    osplit[1][:, :, 0:T].bitcast(F32), ALU.subtract).then_inc(S("hgrn_split"), 1)
                elif name.startswith("split_mixed"):
                    m = mixed1 if name[-1] == "1" else mixed2
                    for k in range(4, KD):
                        hs_low(name, k, m[:, k, :])
                elif name.startswith("half_mixed"):
                    m = mixed1 if name[-1] == "1" else mixed2
                    for k in range(4):
                        hs_low(name, k, m[:, k, :])
                elif name in ("norm_fq", "norm_fk"):
                    q = name == "norm_fq"
                    src, g = (fq, VEC["q_norm"]) if q else (fk, VEC["k_norm"])
                    dve.wait_ge(S("t_freed"), TURN_T[name] + 1)
                    v.scalar_tensor_tensor(src, src, vec[:, g:g + 1], n2r[:, :, :], ALU.mult, ALU.mult)\
                        .then_inc(S("fox_normed"), 1)
                elif name == "forget":
                    dve.wait_ge(S("forget_log"), 1)
                    dve.wait_ge(S("block_freed"), BLOCKS["fvl"] + 4)
                    v.scalar_tensor_tensor(flat(flog[:, :, :]), flat(flog[:, :, :]), 0.0, flog2[:], ALU.min,
                                           ALU.subtract).then_inc(S("log_forget"), 1)
                    for ks, keep in ((P, s_keep1), (T, s_keep2)):
                        link(v.memset(keep[:], 1.0))
                        k3 = keep[:].rearrange("p (h n) -> p h n", h=4)
                        link(v.memset(k3[:, :, ks:ks + 1], 0.0))
                elif name.startswith("fox_s"):
                    hg, tt = int(name[-2]), int(name[-1])
                    ks = keys(tt)
                    dve.wait_ge(S("a_full"), TURN_A[name] + 1)
                    v.scalar_tensor_tensor(f_sc[:, :, 0:ks], area_a[:, :, 0:ks], float(HD) ** -0.5,
                                           heads4(causal(tt, C_CM), ks), ALU.mult, ALU.add)\
                        .then_inc(S("a_freed"), 1)
                    dve.wait_ge(S("a_freed"), TURN_A[name] + 1)
                    softmax("fox", f_sc, f_p, tt, 2 * hg + tt + 1)
                elif name.startswith("sb_s"):
                    stick_breaking(name)
                elif name.startswith(("fox_o", "sb_o")):
                    fox, hg = name[0] == "f", int(name[-1])
                    order = ["fox_o0", "sb_o0", "fox_o1", "sb_o1"]
                    out_low(name, osplit2[0 if fox else 1][:, 2 * hg:2 * hg + 2, :], 3 + order.index(name))
                elif name == "split_p":
                    dve.wait_ge(S("p_hi"), 1)
                    for k in range(2):
                        v.tensor_tensor(ps[:, k, T:2 * T], praw[:, k, :], ps[:, k, 0:T].bitcast(F32), ALU.subtract)\
                            .then_inc(S("p_split"), 1)

            def tables():
                link(v.tensor_copy(posf[:], posi[:]))
                link(v.tensor_copy(postf[:], post[:]))
                for tt in range(NT):
                    d = dist[:, 0:P] if tt == 0 else dist[:, P:P + T]
                    link(v.tensor_scalar(d, posf[:, 0:keys(tt)], -1.0, postf[:, tt:tt + 1], ALU.mult, ALU.add))
                link(v.tensor_tensor(drel[:], relb[:, A_H:], relb[:, 0:(BUCKETS - 1) * A_H], ALU.subtract))
                for h in range(A_H):
                    ins = v.tensor_scalar(bias[:, h, :], dist[:], 0.0, relb[:, h:h + 1], ALU.mult, ALU.add)
                link(ins)
                two_pi = [6.28125, 1.9350051879882812e-03, 3.01991598196e-07]
                magic = 1.5 * 2 ** 23
                link(v.tensor_scalar(ang[:], posf[:], con[:, C_INVF:C_INVF + 1], None, ALU.mult))
                link(v.tensor_scalar(turns[:], ang[:], 1.0 / (2 * np.pi), magic, ALU.mult, ALU.add))
                link(v.tensor_scalar(turns[:], turns[:], magic, None, ALU.subtract))
                src = ang
                for c in two_pi:
                    link(v.scalar_tensor_tensor(rest[:], turns[:], -c, src[:], ALU.mult, ALU.add))
                    src = rest
                pi = 3.1415925
                link(v.tensor_scalar(over[:], rest[:], float(np.pi / 2), None, ALU.add))
                link(v.tensor_scalar(ang[:], over[:], float(np.pi), -2 * float(np.pi), ALU.is_gt, ALU.mult))
                link(v.tensor_tensor(over[:], over[:], ang[:], ALU.add))
                link(v.tensor_scalar(over[:], over[:], pi, -pi, ALU.min, ALU.max))
                v.tensor_scalar(rest[:], rest[:], pi, -pi, ALU.min, ALU.max).then_inc(S("angles"), 1)
                dve.wait_ge(S("sines"), 2)
                link(v.tensor_scalar(sin[:], sin[:], con[:, C_SIGN:C_SIGN + 1], None, ALU.mult))

            def rotate(name, j, w, last):
                dve.wait_ge(S("a_full"), TURN_A[name] + 1)
                link(v.tensor_tensor(w, w, cos[:], ALU.mult))
                ins = v.tensor_tensor(rotated[:], area_a[:, j, :], sin[:], ALU.mult)
                if last:
                    ins.then_inc(S("a_freed"), 1)
                    dve.wait_ge(S("a_freed"), TURN_A[name] + 1)
                else:
                    link(ins)
                v.tensor_tensor(w, w, rotated[:], ALU.add).then_inc(S("rope_done"), 1)

            def decay():
                lbl = vec[:, VEC["lb_logits"]:VEC["lb_logits"] + B_H]
                v.tensor_tensor(st[:, 40:44], lbl, lbl, ALU.subtract).then_inc(S("lb_diff"), 1)
                dve.wait_ge(S("lb_exp"), 1)
                link(v.reciprocal(st[:, 48:52], st[:, 44:48]))
                link(v.tensor_tensor(st[:, 52:56], st[:, 44:48], st[:, 48:52], ALU.mult))
                link(v.tensor_tensor(st[:, 56:60], st[:, 52:56], st[:, 52:56], ALU.subtract))
                link(v.tensor_scalar(st[:, 72:76], st[:, 56:60], -1.0, 1.0, ALU.mult, ALU.add))
                v.tensor_scalar(st[:, 60:64], st[:, 56:60], LB_FLOOR, 2.0 ** 60, ALU.max, ALU.mult)\
                    .then_inc(S("lb_ready"), 1)
                link(v.memset(resetc[:], 1.0))
                link(v.memset(resetc[:].rearrange("p (n j) -> p n j", j=CHUNK)[:, :, 0:1], 0.0))
                dve.wait_ge(S("rope_done"), 1)
                v.tensor_copy(st[:, 90:91], st[:, 56:57]).then_inc(S("decay_space"), 1)
                dve.wait_ge(S("lb_logs"), 1)
                link(v.tensor_scalar(st[:, 64:68], st[:, 64:68], -60 * float(np.log(2.0)), None, ALU.add))
                dve.wait_ge(S("sig_log"), 1)
                link(v.scalar_tensor_tensor(hx[1][:], flat(bf[:, :, :]), 0.0, hx[0][:], ALU.min, ALU.subtract))
                for h in range(B_H):
                    s = slice(T * h, T * h + T)
                    base_, floor = st[:, 68 + h:69 + h], st[:, 64 + h:65 + h]
                    v.tensor_scalar(hx[2][:, s], hx[1][:, s], base_, floor, ALU.add, ALU.max)
                    ins = v.tensor_scalar(hx[0][:, s], hx[1][:, s], base_, floor, ALU.add, ALU.subtract)
                ins.then_inc(S("decay_u"), 1)
                dve.wait_ge(S("decay_log"), 1)
                link(v.tensor_tensor(hx[2][:], hx[2][:], hx[0][:], ALU.add))
                v.tensor_tensor_scan(hb[:], resetc[:], hx[2][:], 0.0, ALU.mult, ALU.add)\
                    .then_inc(S("decay_sum"), 1)
                dve.wait_ge(S("decay_sum"), 1)

            def stick_breaking(name):
                hg, tt = int(name[-2]), int(name[-1])
                ks, n = keys(tt), 2 * hg + tt + 1
                keep = s_keep1 if tt == 0 else s_keep2
                width = 4 * (ks + 1)
                z, l = s_z[:, :, 0:ks], s_a[:, :, 0:ks]
                pad = s_pad[:, 0:width].rearrange("p (h n) -> p h n", h=4)
                after = s_after[:, 0:width].rearrange("p (h n) -> p h n", h=4)
                dve.wait_ge(S("sb_log"), n)
                if n > 1:
                    dve.wait_ge(S("t_freed"), TURN_T[f"sb_t{(n - 2) // 2}{(n - 2) % 2}"] + 1)
                link(v.tensor_scalar(z, area_a[:, :, 0:ks], float(HD) ** -0.5, 0.0, ALU.mult, ALU.max))
                link(v.tensor_tensor(l, z, l, ALU.add))
                v.memset(pad[:, :, ks:ks + 1], 0.0)
                link(v.tensor_tensor(pad[:, :, 0:ks], l, heads4(causal(tt, C_S01), ks), ALU.mult))
                link(v.tensor_tensor_scan(s_after[:, width - 2::-1], keep[:, width - 1:0:-1],
                                          s_pad[:, width - 1:0:-1], 0.0, ALU.mult, ALU.add))
                v.scalar_tensor_tensor(z, area_a[:, :, 0:ks], float(HD) ** -0.5, heads4(causal(tt, C_SCM), ks),
                                       ALU.mult, ALU.add).then_inc(S("a_freed"), 1)
                link(v.tensor_tensor(l, l, after[:, :, 0:ks], ALU.add))
                dve.wait_ge(S("a_freed"), TURN_A[name] + 1)
                v.tensor_tensor(z, z, l, ALU.subtract).then_inc(S("sb_arg"), 1)

            v.memset(epsb[:], EPS).then_inc(S("eps_set"), 1)
            link(v.memset(ones_row[:], 1.0))
            dve.wait_ge(S("con_loaded"), 16 * 5)
            split_low(0, 0)
            split_low(0, 1)
            for kind, what in ORDER:
                if kind == "tile":
                    tile(what)
                elif kind == "step":
                    step(what)
                elif "gu" in what:
                    gate_up(int(what[-1]))
                else:
                    down(int(what[-1]))

        @block.gpsimd
        def _(pool):
            def gated_sums(up, gate, mixed, part, block0, blocks, branches, gates_before, mixed_before):
                for u in range(blocks):
                    branch, k = u // KD, u % KD
                    if k == 0:
                        pool.wait_ge(S("gates_on"), gates_before + branch + 1)
                    pool.wait_ge(S("block_freed"), block0 + u + 1)
                    g = gate[:, u, :]
                    if branch == 0:
                        nc.gpsimd.tensor_tensor(mixed[:, k, :], up[:, u % 4, :], g, ALU.mult)\
                            .then_inc(S("mixed"), 1)
                        continue
                    nc.gpsimd.tensor_tensor(part[:, u % 2, :], up[:, u % 4, :], g, ALU.mult)\
                        .then_inc(S("pool_step"), 1)
                    steps[0] += 1
                    pool.wait_ge(S("pool_step"), steps[0])
                    pool.wait_ge(S("mixed"), mixed_before + u - KD + 1)
                    nc.gpsimd.tensor_tensor(mixed[:, k, :], mixed[:, k, :], part[:, u % 2, :], ALU.add)\
                        .then_inc(S("mixed"), 1)

            def sum_squares(i):
                if i:
                    pool.wait_ge(S("t_full"), TURN_T[SUMMED_NORMS[i - 1]] + 1)
                for k in range(1, KD - 1):
                    pool.wait_ge(S("square"), KD * i + k + 1)
                    if k > 1:
                        pool.wait_ge(S("squares_added"), (KD - 2) * i + k - 1)
                    before = sq_ring[:, 0, :] if k == 1 else sq_sum[:]
                    nc.gpsimd.tensor_tensor(sq_sum[:], before, sq_ring[:, k % 2, :], ALU.add)\
                        .then_inc(S("squares_added"), 1)

            steps = [0]
            gated_sums(up1, gates, mixed1, gated1, BLOCKS["up1"], 24, 3, 0, 0)
            for i in range(3):
                sum_squares(i)
            gated_sums(up2, gates2, mixed2, gated2, BLOCKS["up2"], 16, 2, 3, 24)
            for i in range(3, 5):
                sum_squares(i)


def tiled(w, n_out):
    k, n = w.shape
    full = np.zeros((k, n_out * P), w.dtype)
    full[:, :n] = w
    return full.reshape(k // P, P, n_out, P).transpose(2, 1, 0, 3).reshape(n_out, P, (k // P) * P)


def grouped(t, per):
    n, p, c = t.shape
    return np.ascontiguousarray(t.reshape(n // per, per, p, c).transpose(0, 2, 1, 3).reshape(n // per, p, per * c))


def chunked(w, per):
    k, n = w.shape
    return np.ascontiguousarray(w.reshape(k // P // per, per, P, n).transpose(0, 2, 1, 3).reshape(-1, P, per * n))


def kernel(**inputs):
    import concourse.bacc as bacc
    from concourse.bass_utils import run_bass_kernel_spmd

    i = {k: np.asarray(v) for k, v in inputs.items()}
    w = i["w_in"][0]
    sizes = (A_H * P, P, P, IDX_H * IDX_D, IDX_D, IDX_H, 512, 512, 512, 512, QR, KVR, ROPE, 3 * D)
    aq, ak, av, iq, ik, iw, bq, bf, bi, bg, cq, ckv, kpe, gl = np.split(w, np.cumsum(sizes)[:-1].tolist(), axis=1)
    a = {}
    a["xT"] = np.ascontiguousarray(i["x"][0].T).reshape(KD, P, T)
    a["pT"] = np.ascontiguousarray(i["p_2"][0, 0].T).reshape(2, P, T)
    a["pos"] = np.ascontiguousarray(i["positions"][0])
    a["rel_bias"] = np.ascontiguousarray(i["rel_bias"].reshape(-1))
    a["forget_bias"] = np.ascontiguousarray(i["forget_bias_2"][0])
    a["consts"] = constants()
    vectors = {"attn_norm": i["attn_norm"][0], "ffn_norm": i["ffn_norm"][0], "final_norm": i["final_norm"],
               "ffn1_norm": i["ffn1_norm_2"][0], "mix_norm": i["mix_norm_2"][0], "ffn2_norm": i["ffn2_norm_2"][0],
               "ple_norm": i["ple_norm_2"][0], "mla_q_norm": i["mla_q_norm"][0], "mla_kv_norm": i["mla_kv_norm"][0],
               "lb_logits": i["hgrn_lb_logits"][0], "hgrn_out": i["hgrn_out_norm"][0],
               "q_norm": np.concatenate([i["q_norm_2"][0]] * 2), "k_norm": np.concatenate([i["k_norm_2"][0]] * 2)}
    a["vecs"] = np.ascontiguousarray(np.concatenate([vectors[n].reshape(c, P).T for n, c in VEC_SIZES], axis=1))

    def cat(*v):
        return np.concatenate(v, axis=1)

    proj = cat(kpe, kpe, ik, ik, iq)
    a["w_projT_a"] = grouped(tiled(proj, 6), 2)
    a["w_avw"] = chunked(cat(av, iw), KD)
    a["w_projT_b"] = grouped(tiled(cat(ak, aq, cq, ckv, bf), 14), 2)
    a["w_projT_c"] = grouped(tiled(bq, 4), 2)
    a["w_bi"] = chunked(bi, 4)
    a["w_projT_d"] = grouped(tiled(bg, 4), 2)
    qb = i["mla_w_qb"][0].reshape(QR, C_H, NOPE + ROPE)
    qb = cat(qb[:, :, :NOPE].reshape(QR, -1), qb[:, :, NOPE:].reshape(QR, -1))
    a["w_qb"] = grouped(tiled(qb, 6), 3)
    kvb = i["mla_w_kvb"][0].reshape(KVR, C_H, NOPE + P)
    kb = grouped(tiled(kvb[:, :, :NOPE].reshape(KVR, -1), 4), 4)
    vb = chunked(np.ascontiguousarray(kvb[:, :, NOPE:].reshape(KVR, -1)), 2)
    a["w_kvb"] = np.concatenate([kb, vb], axis=2)
    a["w_gates1"] = grouped(tiled(gl, 24), 2)
    a["w_up1"] = np.concatenate([grouped(tiled(i[n][0], 8), 4) for n in ("w_up_a", "w_up_b", "w_up_c")])
    a["w_out1"] = grouped(tiled(i["w_out"][0], 8), 2)

    def gate_up(gate, up):
        return np.concatenate([tiled(gate, KF), tiled(up, KF)], axis=2)

    def down(m):
        t = tiled(m, KD)
        return np.ascontiguousarray(t.reshape(KD, P, 2, KF // 2 * P).transpose(0, 2, 1, 3).reshape(16, P, -1))

    for f, (g, u, d) in enumerate((("w_ffn_gate", "w_ffn_up", "w_ffn_down"),
                                   ("ffn1_w_gate_2", "ffn1_w_up_2", "ffn1_w_down_2"),
                                   ("ffn2_w_gate_2", "ffn2_w_up_2", "ffn2_w_down_2"))):
        a[f"w_gu{f}"] = gate_up(i[g][0], i[u][0])
        a[f"w_dn{f}"] = down(i[d][0])
    w = i["w_in_2"][0]
    sizes = (512, 512, 512, FOX_H, 512, 512, 512, D, D)
    fq, fk, fv, fl, sq, sk, sv, gf, gs = np.split(w, np.cumsum(sizes)[:-1].tolist(), axis=1)
    a["w_qk2"] = grouped(tiled(cat(fq, fk, sq, sk), 16), 2)
    a["w_fvl"] = chunked(cat(fv, fl), 4)
    a["w_sv"] = chunked(sv, 4)
    a["w_gates2"] = grouped(tiled(cat(gf, gs), 16), 2)
    a["w_up2"] = np.concatenate([grouped(tiled(i[n][0], 8), 4) for n in ("w_branch_fox_2", "w_branch_sb_2")])
    a["w_out2"] = grouped(tiled(i["w_out_2"][0], 8), 2)
    a["w_pg"] = grouped(tiled(i["w_ple_gate_2"][0], 8), 2)
    a["w_pp"] = grouped(tiled(i["w_ple_proj_2"][0], 8), 8)
    for name, n, c, _ in TILES:
        assert a[name][n].shape == (P, c), (name, a[name].shape, c)

    nc = bacc.Bacc("TRN2", target_bir_lowering=False, num_devices=1)
    arrays, aps = {}, {}
    for name, arr in a.items():
        arr = np.ascontiguousarray(arr)
        arrays[f"in_{name}"] = arr
        aps[name] = nc.dram_tensor(f"in_{name}", arr.shape, mybir.dt.from_np(arr.dtype), kind="ExternalInput").ap()
    out = nc.dram_tensor("out", (KD, P, T), F32, kind="ExternalOutput").ap()
    build(nc, aps, out)
    r = run_bass_kernel_spmd(nc, [arrays], core_ids=[0])
    got = r.results[0]["out"]
    return np.ascontiguousarray(got.reshape(D, T).T).reshape(1, T, D)
```

```python
from contextlib import ExitStack

import numpy as np

import concourse.bass as bass
from concourse import mybir

F32 = mybir.dt.float32
F32R = mybir.dt.float32r
I32 = mybir.dt.int32
ACT = mybir.ActivationFunctionType
ALU = mybir.AluOpType
AX = mybir.AxisListType

P = 128
T = 256
NT = T // P
D = 1024
KD = D // P
FF = 2816
KF = FF // P
A_H, B_H, C_H = 4, 4, 4
POOL_H = 3
IDX_H, IDX_D = 8, 64
TOPK = 64
CHUNK = 64
QR, KVR, NOPE, ROPE = 384, 256, 128, 64
FOX_H, HD = 8, 64
BUCKETS, MAX_DIST = 32, 128
EPS = 1e-6
NEG = -1e30
LB_FLOOR = 1e-30
AVW = P + IDX_H
FVL = FOX_H * HD + FOX_H
SLOT = 4 * FVL

C_ONE, C_INVF, C_SIGN, C_ID, C_ONE64, C_SWAP = 0, 128, 129, 136, 264, 392
EARLY_CONST = 520
C_CM, C_SCM, C_S01, C_TRI, C_LEV = 520, 776, 1032, 1288, 1544
LEVELS = (0, 1, 2, 4, 8, 16, 32, 64)
C_SEL = C_LEV + P * len(LEVELS)
N_CONST = C_SEL + P * FOX_H

VEC_SIZES = [("attn_norm", KD), ("ffn_norm", KD), ("final_norm", KD), ("ffn1_norm", KD), ("mix_norm", KD),
             ("ffn2_norm", KD), ("ple_norm", KD), ("mla_q_norm", QR // P), ("mla_kv_norm", KVR // P),
             ("lb_logits", B_H), ("hgrn_out", 1), ("q_norm", 1), ("k_norm", 1)]
VEC, _at = {}, 0
for _n, _c in VEC_SIZES:
    VEC[_n] = _at
    _at += _c
N_VEC = _at


def bucket_thresholds():
    exact = BUCKETS // 2
    d = np.arange(1, MAX_DIST * 2)
    large = exact + (np.log(np.maximum(d, exact).astype(np.float32) / np.float32(exact))
                     / np.float32(np.log(MAX_DIST / exact)) * (BUCKETS - exact)).astype(np.int32)
    bucket = np.where(d < exact, d, np.minimum(large, BUCKETS - 1))
    return [float(d[np.argmax(bucket >= b)]) for b in range(1, BUCKETS)]


def constants():
    c = np.zeros((P, N_CONST), np.float32)
    r = np.arange(P)
    row, col = r[:, None], r[None, :]
    c[:, C_ID:C_ID + P] = row == col
    c[:, C_ONE:C_ONE + P] = 1
    c[:, C_ONE64:C_ONE64 + P] = row // 64 == col // 64
    c[:, C_SWAP:C_SWAP + P] = row == (col ^ 32)
    c[:, C_CM + P:C_CM + T] = np.where(col <= row, 0, np.float32(NEG))
    c[:, C_SCM + P:C_SCM + T] = np.where(col < row, 0, np.float32(NEG))
    c[:, C_S01:C_S01 + P] = 1
    c[:, C_S01 + P:C_S01 + T] = col < row
    c[:, C_TRI:C_TRI + P] = row <= col
    c[:, C_TRI + P:C_TRI + T] = 1
    for i, h in enumerate(LEVELS):
        if h == 0:
            m = row == col
        else:
            m = (row // (2 * h) == col // (2 * h)) & (row % (2 * h) < h) & (col % (2 * h) >= h)
        c[:, C_LEV + P * i:C_LEV + P * (i + 1)] = m
    for h in range(FOX_H):
        c[h, C_SEL + P * h:C_SEL + P * (h + 1)] = 1
    c[:, C_INVF] = (10000.0 ** (-(2.0 * (r % 32)) / ROPE)).astype(np.float32)
    c[:, C_SIGN] = np.where(r % 64 < 32, -1, 1)
    return c


def stream_plan():
    tiles, first = [], {}

    def add(name, n, cols, half):
        first[name] = len(tiles)
        tiles.extend((name, i, cols, half) for i in range(n))

    full = 2 * KD * P
    add("w_projT_a", 3, full, full // 2)
    add("w_avw", 1, KD * AVW, KD * AVW // 2)
    add("w_projT_b", 7, full, full // 2)
    add("w_projT_c", 2, full, full // 2)
    add("w_bi", 2, full, full // 2)
    add("w_projT_d", 2, full, full // 2)
    add("w_gates1a", 4, full, full // 2)
    add("w_qb", 2, 9 * P, 6 * P)
    add("w_kvb", 1, full, full // 2)
    add("w_gates1b", 8, full, full // 2)
    add("w_up1", 6, full, full // 2)
    add("w_out1", 4, full, full // 2)
    add("w_gu0", KF, full, full // 2)
    add("w_dn0", 16, KF * P // 2, 6 * P)
    add("w_gu1", KF, full, full // 2)
    add("w_dn1", 16, KF * P // 2, 6 * P)
    add("w_fvl", 2, 4 * FVL, 2 * FVL)
    add("w_qk2", 8, full, full // 2)
    add("w_sv", 2, full, full // 2)
    add("w_gates2", 8, full, full // 2)
    add("w_up2", 4, full, full // 2)
    add("w_out2", 4, full, full // 2)
    add("w_gu2", KF, full, full // 2)
    add("w_dn2", 16, KF * P // 2, 6 * P)
    add("w_pg", 4, full, full // 2)
    add("w_pp", 1, full, full // 2)
    return tiles, first


TILES, FIRST = stream_plan()

BLOCKS, ENDS = {}, {}


def plan_blocks():
    n = 0
    g = FIRST
    plan = [("kpe_ik", 2, lambda i: 0), ("iq", 4, lambda i: 1 + i // 2), ("avw", 2, lambda i: 3),
            ("projT_b", 14, lambda i: 4 + i // 2), ("bq", 4, lambda i: g["w_projT_c"] + i // 2),
            ("bi", 2, lambda i: g["w_bi"] + 1), ("bg", 4, lambda i: g["w_projT_d"] + i // 2),
            ("gates1a", 8, lambda i: g["w_gates1a"] + i // 2),
            ("q_c", 6, lambda i: g["w_qb"] + i // 3), ("kv_c", 6, lambda i: g["w_kvb"]),
            ("gates1b", 16, lambda i: g["w_gates1b"] + i // 2), ("up1", 24, lambda i: g["w_up1"] + i // 4),
            ("out1", 8, lambda i: g["w_out1"] + i // 2),
            ("gu0", 44, lambda i: g["w_gu0"] + i // 2), ("dn0", 8, lambda i: g["w_dn0"] + 2 * i + 1),
            ("gu1", 44, lambda i: g["w_gu1"] + i // 2), ("dn1", 8, lambda i: g["w_dn1"] + 2 * i + 1),
            ("fvl", 4, lambda i: g["w_fvl"] + 1), ("qk2", 16, lambda i: g["w_qk2"] + i // 2),
            ("sv", 2, lambda i: g["w_sv"] + 1), ("gates2", 16, lambda i: g["w_gates2"] + i // 2),
            ("up2", 16, lambda i: g["w_up2"] + i // 4), ("out2", 8, lambda i: g["w_out2"] + i // 2),
            ("gu2", 44, lambda i: g["w_gu2"] + i // 2), ("dn2", 8, lambda i: g["w_dn2"] + 2 * i + 1),
            ("pgp", 16, lambda i: g["w_pg"] + i // 2 if i < 8 else g["w_pp"])]
    for name, count, end in plan:
        BLOCKS[name] = n
        for i in range(count):
            ENDS[n + i] = end(i)
        n += count
    return n


N_BLOCKS = plan_blocks()
DONE_AFTER = {g: max(n for n, e in ENDS.items() if e == g) + 1 for g in set(ENDS.values())}
PARTS = [g for g in range(len(TILES)) if g not in DONE_AFTER]


def order_of_work():
    o, tile = [], [0]

    def tiles(n):
        for _ in range(n):
            o.append(("tile", tile[0]))
            tile[0] += 1

    def steps(*names):
        o.extend(("step", s) for s in names)

    def phase(name, n):
        assert FIRST[name] == tile[0], (name, tile)
        o.append(("ffn" if "gu" in name or "dn" in name else "tiles", name))
        tile[0] += n

    steps("norm0", "distances")
    tiles(1); steps("bound0", "bias0")
    tiles(1); steps("idx00", "bound1", "bias1")
    tiles(1); steps("idx01", "tables", "bias2")
    tiles(1); steps("top_a0", "idx10", "bias3")
    tiles(1); steps("top_b0", "idx11", "bias4")
    tiles(1); steps("top_c0", "bias5")
    tiles(1); steps("top_d0", "bias6")
    tiles(1); steps("top_a1", "bias7")
    tiles(1); steps("input_squares", "top_b1", "bias8")
    tiles(1); steps("mla_norm", "top_c1", "bias9")
    tiles(1); steps("top_d1", "bias10", "decay_a")
    tiles(1); steps("decay_xa", "mla_normed", "rope_k", "bias11")
    tiles(1); steps("bias12", "decay_b")
    tiles(1); steps("decay_xb", "bias13")
    tiles(1); steps("bias14", "decay_c")
    tiles(1); steps("decay_xc", "level_m0", "level_e1", "bias15")
    tiles(1); steps("level_x1", "level_m1", "lev0", "level_e2")
    tiles(1); steps("level_x2", "level_m2", "lev1", "level_e3")
    tiles(1); steps("level_x3", "level_m3", "dsa_s0", "lev2", "level_e4")
    tiles(1); steps("level_x4", "level_m4", "dsa_p0", "lev3", "level_e5")
    tiles(1); steps("dsa_t0", "dsa_s1", "level_x5", "level_m5")
    tiles(1); steps("dsa_p1", "lev4", "level_e6")
    tiles(1); steps("dsa_t1", "rope_q", "level_x6", "level_m6")
    tiles(1); steps("dsa_o", "lev5", "level_e7")
    tiles(1); steps("mla_s0", "level_x7", "level_m7", "lev6", "level_e8")
    tiles(1); steps("mla_p0", "level_x8", "level_m8", "lev7")
    tiles(1); steps("mla_t0", "mla_s1")
    tiles(1); steps("mla_p1", "far")
    tiles(1); steps("mla_t1", "hgrn_o", "gate_sigmoid1_0", "gate_sigmoid1_1")
    tiles(1); steps("hgrn_n")
    tiles(1); steps("mla_o")
    tiles(2); steps("gate_sigmoid1_2")
    tiles(4); steps("half_mixed1")
    tiles(1); steps("split_mixed1")
    tiles(4)
    steps("norm1")
    phase("w_gu0", KF); phase("w_dn0", 16)
    steps("norm2", "norm3")
    phase("w_gu1", KF); phase("w_dn1", 16)
    steps("norm4")
    tiles(2); steps("log_forget")
    tiles(1); steps("forget")
    tiles(3); steps("head_squares")
    tiles(1); steps("norm_fq")
    tiles(1); steps("norm_fk")
    tiles(1); steps("fox_normed")
    tiles(1); steps("fox_s00")
    tiles(1); steps("fox_p00", "sb_s00")
    tiles(1); steps("fox_t00", "fox_s01", "sb_m00")
    tiles(1); steps("sb_x00", "fox_p01", "sb_t00", "sb_s01")
    tiles(1); steps("fox_t01", "fox_s10", "sb_m01")
    tiles(1); steps("sb_x01", "fox_p10", "fox_o0", "sb_t01", "sb_s10")
    tiles(1); steps("fox_t10", "sb_o0", "fox_s11", "sb_m10")
    tiles(1); steps("sb_x10", "fox_p11", "sb_t10", "sb_s11")
    tiles(1); steps("fox_t11", "sb_m11")
    tiles(1); steps("sb_x11", "fox_o1", "sb_t11", "gate_sigmoid2_0")
    tiles(1); steps("sb_o1")
    tiles(1); steps("gate_sigmoid2_1")
    tiles(2); steps("half_mixed2")
    tiles(1); steps("split_mixed2")
    tiles(4)
    steps("norm5")
    phase("w_gu2", KF); phase("w_dn2", 16)
    steps("norm6", "split_p")
    tiles(5)
    assert tile[0] == len(TILES), tile
    return o


ORDER = order_of_work()


def area_turns(uses):
    taken = [s for kind, s in ORDER if kind == "step" and uses(s)]
    return {s: n for n, s in enumerate(taken)}


def takes_a(s):
    return (s.startswith(("idx", "rope_", "dsa_s", "dsa_o", "mla_s", "mla_o", "fox_s", "fox_o", "sb_s", "sb_o", "hgrn_o"))
            or s in ("lev0", "far"))


def takes_t(s):
    return (s.startswith(("norm", "dsa_t", "mla_t", "fox_t", "sb_t", "forget", "hgrn_n"))
            or s in ("mla_norm", "lev1", "lev2", "lev3", "lev4", "lev5", "lev6", "lev7"))


TURN_A, TURN_T = area_turns(takes_a), area_turns(takes_t)
NORMS = [s for k, s in ORDER if s in [f"norm{i}" for i in range(7)]]


def build(nc, a, out_t):
    with ExitStack() as ctx:
        sems = {}

        def S(name):
            if name not in sems:
                sems[name] = ctx.enter_context(nc.semaphore(name))
            return sems[name]

        top = [nc.sbuf_base + (-nc.sbuf_base) % 64]

        def at(name, shape, off, dt=F32):
            return nc.alloc_sbuf_tensor_at(name, [P, *shape], dt, offset=off)

        def fixed(name, shape, dt=F32):
            off = top[0]
            top[0] += (4 * int(np.prod(shape)) + 63) // 64 * 64
            return at(name, shape, off, dt)

        x = fixed("x", (KD, T))
        hs_off = top[0]
        hs = fixed("hs", (KD, 2 * T), F32R)
        raw = fixed("raw", (2, SLOT))
        whi = fixed("whi", (2, SLOT), F32R)
        wlo = fixed("wlo", (2, SLOT), F32R)
        tmp = fixed("tmp", (4, T))
        con = fixed("con", (N_CONST,))
        vec = fixed("vec", (N_VEC,))
        st = fixed("st", (256,))
        epsb = fixed("epsb", (1,))
        sq = at("sq", (KD, T), hs_off)
        xr = fixed("xr", (T,))
        ones_row = fixed("ones_row", (T,))
        base = top[0]

        def arena(name, off, shape, dt=F32):
            assert base + 4 * (off + int(np.prod(shape))) <= nc.sbuf_usable_end, name
            return at(name, shape, base + 4 * off, dt)

        ident = con[:, C_ID:C_ID + P]
        ones = con[:, C_ONE:C_ONE + P]
        ones64 = con[:, C_ONE64:C_ONE64 + P]
        swap = con[:, C_SWAP:C_SWAP + P]

        gates = arena("gates", 0, (24, T))
        relu_l = arena("relu_l", 0, (IDX_H, T))
        d_sc = arena("d_sc", 2048, (4, T))
        d_p = arena("d_p", 3072, (4, T))
        d_pt0 = arena("d_pt0", 4096, (4, T))
        d_pt1 = arena("d_pt1", 5120, (4, P))
        osplit = [arena(f"osplit_{n}", 6144 + 2048 * i, (4, 2 * T), F32R) for i, n in enumerate("abc")]
        m_sc = arena("m_sc", 8192, (4, T))
        m_p = arena("m_p", 9216, (4, T))
        m_pt0 = arena("m_pt0", 10240, (4, T))
        m_pt1 = arena("m_pt1", 11264, (4, P))
        cqs = arena("cqs", 10240, (3, 2 * T), F32R)
        ckvs = arena("ckvs", 8192, (2, 2 * T), F32R)
        iq = arena("iq", 12288, (4, T))
        ik = arena("ik", 13312, (T,))
        aq = arena("aq", 13568, (4, T))
        ak = arena("ak", 14592, (T,))
        av = arena("av", 9216, (NT, P))
        iw = arena("iw", 15104, (NT, IDX_H))
        bias = arena("bias", 15120, (A_H, P + T))
        qn = arena("qn", 12288, (C_H, T))
        qpe = arena("qpe", 13312, (2, T))
        kn = arena("kn", 13824, (C_H, T))
        vc = arena("vc", 14848, (NT, C_H * P))
        mixed1 = arena("mixed1", 12288, (KD, T))
        up1 = arena("up1", 14336, (4, T))
        gated1 = arena("gated1", 15360, (2, T))
        bf = arena("bf", 16656, (B_H, T))
        bq = arena("bq", 17680, (B_H, T))
        bg = arena("bg", 18704, (B_H, T))
        bi = arena("bi", 19728, (NT, B_H * P))
        cq = arena("cq", 20752, (3, T))
        ckv = arena("ckv", 21520, (2, T))
        kpe = arena("kpe", 22032, (T,))
        cos = arena("cos", 22288, (T,))
        sin = arena("sin", 22544, (T,))
        hb = arena("hb", 22800, (B_H * T,))
        hk = arena("hk", 23824, (B_H * T,))
        he = [arena(f"he{i}", 24848 + 1024 * i, (B_H * T,)) for i in range(2)]
        h0 = arena("h0", 26896, (B_H, T))
        h1 = arena("h1", 27920, (B_H, P))
        dist = arena("dist", 28704, (P + T,))
        rise = [arena(f"rise{i}", 2048 + i * POOL_H * (P + T), (POOL_H, P + T)) for i in range(2)]
        mask = [arena(f"mask{i}", 4352 + i * (P + T), (P + T,)) for i in range(4)]
        chosen = [arena("chosen0", 6144, (P,)), arena("chosen1", 6272, (T,))]
        posf = arena("posf", 23952, (T,))
        relb = arena("relb", 24208, (BUCKETS * A_H,))
        drel = arena("drel", 6016, ((BUCKETS - 1) * A_H,))
        posi = nc.alloc_sbuf_tensor_at("posi", [P, T], I32, offset=base + 4 * 24464)
        post = nc.alloc_sbuf_tensor_at("post", [P, NT], I32, offset=base + 4 * 24720)
        postf = arena("postf", 24736, (NT,))
        ang = arena("ang", 24848, (T,))
        turns = arena("turns", 25104, (T,))
        rest = arena("rest", 25360, (T,))
        over = arena("over", 25616, (T,))
        score = arena("score", 26896, (T,))
        work = arena("work", 27152, (T,))
        above = arena("above", 27408, (T,))
        equal = arena("equal", 27664, (T,))
        rank = arena("rank", 27920, (T,))
        nsq = arena("nsq", 24848, (5, T))
        nrm = arena("nrm", 26128, (2, T))
        nval = arena("nval", 26640, (5, T))
        hx = [he[0], he[1], arena("hx2", 26896, (B_H * T,))]
        rotated = arena("rotated", 28448, (T,))
        resetc = arena("resetc", 23824, (B_H * T,))

        sq_ring = arena("sq_ring", 19968, (2, T))
        sq_sum = arena("sq_sum", 20480, (T,))

        hid = arena("hid", 0, (KF, 2 * T), F32R)
        gbuf = arena("gbuf", 11264, (2, T))
        ubuf = arena("ubuf", 11776, (2, T))
        sbuf = arena("sbuf", 12288, (2, T))
        hbuf = arena("hbuf", 12800, (2, T))
        dsum = arena("dsum", 13312, (2, T))

        qk2 = arena("qk2", 0, (16, T))
        fq, fk, sq_, sk_ = (qk2[:, 4 * i:4 * i + 4, :] for i in range(4))
        fv = arena("fv", 4096, (NT, FOX_H * HD))
        sv = arena("sv", 5120, (NT, FOX_H * HD))
        gates2 = arena("gates2", 6144, (16, T))
        osplit2 = [arena(f"osplit2_{n}", 10240 + 2048 * i, (4, 2 * T), F32R) for i, n in enumerate(("fox", "sb"))]
        mixed2 = arena("mixed2", 14336, (KD, T))
        up2 = arena("up2", 16384, (4, T))
        gated2 = arena("gated2", 17408, (2, T))
        f_sc = arena("f_sc", 17920, (4, T))
        f_p = arena("f_p", 18944, (4, T))
        s_z = arena("s_z", 19968, (4, T))
        s_a = arena("s_a", 20992, (4, T))
        s_pad = arena("s_pad", 22016, (4 * (T + 1),))
        s_after = arena("s_after", 23048, (4 * (T + 1),))
        s_keep = arena("s_keep", 24080, (4 * (T + 1),))
        f_pt0 = arena("f_pt0", 25112, (4, T))
        f_pt1 = arena("f_pt1", 26136, (4, P))
        flog = arena("flog", 26648, (NT, FOX_H))
        flog2 = arena("flog2", 26664, (NT * FOX_H,))
        negf = arena("negf", 26680, (T,))
        fb = arena("fb", 26936, (FOX_H,))
        s_pt0 = arena("s_pt0", 26944, (4, T))
        s_pt1 = arena("s_pt1", 27968, (4, P))
        s_keep1 = arena("s_keep1", 28480, (4 * (P + 1),))
        s_keep2 = s_keep
        n2sq = arena("n2sq", 17920, (8, T))
        n2r = arena("n2r", 19968, (8, T))
        praw = arena("praw", 16384, (2, T))
        ps = arena("ps", 16896, (2, 2 * T), F32R)
        pg = arena("pg", 0, (KD, T))
        pp = arena("pp", 2048, (2, T))

        acc = [ctx.enter_context(nc.psum_tensor(f"acc{i}", [P, 512], F32)) for i in range(4)]
        area_a = ctx.enter_context(nc.psum_tensor("area_a", [P, 4, T], F32))
        area_t = ctx.enter_context(nc.psum_tensor("area_t", [P, 4, T], F32))

        def keys(tt):
            return P * (tt + 1)

        def queries(tt):
            return slice(P * tt, P * tt + P)

        def cols(h):
            return slice(64 * (h % 2), 64 * (h % 2) + 64)

        HEAD_OF_SLOT = (0, 2, 1, 3)

        def heads4(v, n):
            return v.unsqueeze(1).to_broadcast([P, 4, n])

        def causal(tt, c0):
            return con[:, c0 + (P if tt == 0 else 0):c0 + T]

        def free_value(g):
            if g in DONE_AFTER:
                return "block_done", DONE_AFTER[g]
            return "part_done", PARTS.index(g) + 1

        def norm_of(step):
            return VEC[("attn_norm", "ffn_norm", "final_norm", "ffn1_norm", "mix_norm", "ffn2_norm",
                        "ple_norm")[NORMS.index(step)]]

        SUMMED = {"norm1": "out1", "norm2": "dn0", "norm4": "dn1", "norm5": "out2", "norm6": "dn2"}
        SUMMED_NORMS = list(SUMMED)
        SQUARED = {BLOCKS[b] + k: (SUMMED_NORMS.index(n), k) for n, b in SUMMED.items() for k in range(KD)}
        DIRECT_NORMS = ["norm0", "norm3"]
        HS_NORMS = [s for s in NORMS if s != "norm2"]
        HS_WRITES = [s for k, s in ORDER if k == "step" and (s in HS_NORMS or s.endswith(("mixed1", "mixed2")))]
        HS_STARTS = [s for s in HS_WRITES if not s.startswith("half")]
        HS_BEFORE = {FIRST[n]: KD * i for i, n in enumerate(
            ("w_projT_a", "w_out1", "w_gu0", "w_gu1", "w_fvl", "w_out2", "w_gu2", "w_pg"))}

        block = ctx.enter_context(nc.Block())

        @block.sync
        def _(sp):
            e = EARLY_CONST
            sp.dma_start(con[:, 0:e], a["consts"][:, 0:e]).then_inc(S("con_loaded"), 16)
            xT = a["xT"].rearrange("k p t -> p k t")
            for half in range(2):
                c = slice(half * KD // 2, (half + 1) * KD // 2)
                sp.dma_start(x[:, c, :], xT[:, c, :]).then_inc(S(f"x_loaded{half}"), 16)
            sp.dma_start(vec[:], a["vecs"]).then_inc(S("vec_loaded"), 16)
            sp.dma_start(raw[:, 0, 0:TILES[0][2]], a["w_projT_a"][0]).then_inc(S("w_loaded0"), 16)
            sp.dma_start(posi[:], a["pos"].partition_broadcast(P)).then_inc(S("pos_loaded"), 16)
            sp.dma_start(post[:], a["pos"].rearrange("(i p) -> p i", p=P),
                         allow_slow_non_contiguous=True).then_inc(S("pos_loaded"), 16)
            sp.dma_start(relb[:], a["rel_bias"].partition_broadcast(P)).then_inc(S("pos_loaded"), 16)
            sp.dma_start(raw[:, 1, 0:TILES[1][2]], a["w_projT_a"][1]).then_inc(S("w_loaded1"), 16)
            sp.dma_start(con[:, e:], a["consts"][:, e:]).then_inc(S("masks_loaded"), 16)

            def load(src, slot, n, lo_needed):
                sp.wait_ge(S("w_lo"), lo_needed)
                sp.dma_start(raw[:, slot, 0:n], src).then_inc(S(f"w_loaded{slot}"), 16)

            def load_run(name, count):
                g0 = FIRST[name]
                n = TILES[g0][2]
                with sp.Fori(0, count // 2) as i:
                    for j in range(2):
                        load(a[name][i * 2 + j], j, n, i * 4 + 2 * (g0 + j) - 2)

            done = set()
            for g, (name, i, n, _) in enumerate(TILES):
                if name[2:4] in ("gu", "dn"):
                    if name not in done:
                        done.add(name)
                        load_run(name, KF if "gu" in name else 16)
                    if name == "w_gu0" and i == KF - 1:
                        sp.wait_ge(S("block_freed"), BLOCKS["gu0"] + 1)
                        sp.dma_start(fb[:], a["forget_bias"].partition_broadcast(P)).then_inc(S("fb_loaded"), 16)
                    if name == "w_gu2" and i == KF - 1:
                        sp.wait_ge(S("block_freed"), BLOCKS["gu2"] + 1)
                        sp.dma_start(praw[:], a["pT"].rearrange("k p t -> p k t")).then_inc(S("p_loaded"), 16)
                    continue
                if g >= 2:
                    load(a[name][i], g % 2, n, 2 * g - 2)
            for k in range(KD):
                sp.wait_ge(S("out_ready"), k + 1)
                sp.dma_start(out_t[k], x[:, k, :]).then_inc(S("stored"), 16)
            sp.wait_ge(S("stored"), 16 * KD)

        @block.tensor
        def _(pe):
            def mm(out, w, m, start, stop):
                return nc.tensor.matmul(out, w, m, start=start, stop=stop, skip_group_check=True)

            def block_t(slot, c0, n_k, n, h, k0=0, first=True, last=True):
                bank = acc[n % 4]
                for k in range(n_k):
                    c = c0 + k * P
                    hi = (bank[:, :], whi[:, slot, c:c + P], h[:, k0 + k, :])
                    lo = (bank[:, 0:T], wlo[:, slot, c:c + P], h[:, k0 + k, 0:T])
                    begin, end = first and k == 0, last and k == n_k - 1
                    if end:
                        mm(*lo, False, False)
                        m = mm(*hi, begin, True)
                    else:
                        mm(*hi, begin, False)
                        m = mm(*lo, False, False)
                return m

            def block_n(slot, c0, pitch, width, n_k, n, h, tt, k0=0, first=True, last=True):
                out = acc[n % 4][:, 0:width]
                for k in range(n_k):
                    c = c0 + k * pitch
                    hi_t = h[:, k0 + k, P * tt:P * tt + P]
                    lo_t = h[:, k0 + k, T + P * tt:T + P * tt + P]
                    mm(out, hi_t, whi[:, slot, c:c + width], first and k == 0, False)
                    mm(out, hi_t, wlo[:, slot, c:c + width], False, False)
                    m = mm(out, lo_t, whi[:, slot, c:c + width], False, last and k == n_k - 1)
                return m

            def half_ready(g, half):
                pe.wait_ge(S("w_lo"), 2 * g + half + 1)

            def first_tile(g, n):
                bank_free(n + 1)
                half_ready(g, 1)
                for k in range(KD):
                    pe.wait_ge(S("hs_lo"), HS_BEFORE[g] + k + 1)
                    for b in range(2):
                        c = (b * KD + k) * P
                        mm(acc[(n + b) % 4][:, :], whi[:, g % 2, c:c + P], hs[:, k, :], k == 0, False)
                        m = mm(acc[(n + b) % 4][:, 0:T], wlo[:, g % 2, c:c + P], hs[:, k, 0:T], False, k == KD - 1)
                        if k == KD - 1:
                            m.then_inc(S("block_done"), 1)

            def bank_free(n):
                if n >= 4:
                    pe.wait_ge(S("block_freed"), n - 3)

            def mixer_split(name, branch):
                if (name, branch) == ("w_up1", 1):
                    pe.wait_ge(S("hgrn_split"), 1)
                else:
                    last = {"w_up1": ("dsa_o", None, "mla_o"), "w_up2": ("fox_o1", "sb_o1")}[name][branch]
                    pe.wait_ge(S("a_freed"), TURN_A[last] + 1)

            def tile(g):
                name, i, _, _ = TILES[g]
                slot = g % 2
                first_of = {"w_projT_a": (BLOCKS["kpe_ik"], 2), "w_projT_b": (BLOCKS["projT_b"], 2),
                            "w_projT_c": (BLOCKS["bq"], 2), "w_projT_d": (BLOCKS["bg"], 2),
                            "w_gates1a": (BLOCKS["gates1a"], 2),
                            "w_gates1b": (BLOCKS["gates1b"], 2), "w_out1": (BLOCKS["out1"], 2),
                            "w_qk2": (BLOCKS["qk2"], 2), "w_gates2": (BLOCKS["gates2"], 2),
                            "w_out2": (BLOCKS["out2"], 2), "w_pg": (BLOCKS["pgp"], 2)}
                if g in HS_BEFORE and name != "w_fvl":
                    first_tile(g, first_of[name][0])
                elif name in first_of:
                    n0, per = first_of[name]
                    for b in range(per):
                        n = n0 + per * i + b
                        bank_free(n)
                        half_ready(g, b)
                        block_t(slot, b * KD * P, KD, n, hs).then_inc(S("block_done"), 1)
                elif name in ("w_up1", "w_up2"):
                    n0, src = (BLOCKS["up1"], osplit) if name == "w_up1" else (BLOCKS["up2"], osplit2)
                    if i % 2 == 0:
                        mixer_split(name, i // 2)
                    for b in range(4):
                        n = n0 + 4 * i + b
                        bank_free(n)
                        half_ready(g, b // 2)
                        block_t(slot, b * 4 * P, 4, n, src[i // 2]).then_inc(S("block_done"), 1)
                elif name == "w_avw":
                    n0 = BLOCKS["avw"]
                    bank_free(n0 + 1)
                    for half in range(2):
                        half_ready(g, half)
                        for tt in range(NT):
                            m = block_n(slot, half * 4 * AVW, AVW, AVW, 4, n0 + tt, hs, tt, 4 * half,
                                        half == 0, half == 1)
                            if half:
                                m.then_inc(S("block_done"), 1)
                elif name in ("w_bi", "w_sv"):
                    n0 = BLOCKS[name[2:]]
                    if i == 0:
                        bank_free(n0 + 1)
                    for half in range(2):
                        half_ready(g, half)
                        for tt in range(NT):
                            m = block_n(slot, half * 1024, 512, 512, 2, n0 + tt, hs, tt, 4 * i + 2 * half,
                                        i == 0 and half == 0, i == 1 and half == 1)
                            if half and i:
                                m.then_inc(S("block_done"), 1)
                    if i == 0:
                        m.then_inc(S("part_done"), 1)
                elif name == "w_fvl":
                    n0 = BLOCKS["fvl"]
                    if i == 0:
                        bank_free(n0 + 3)
                    for half in range(2):
                        half_ready(g, half)
                        pe.wait_ge(S("hs_lo"), HS_BEFORE[FIRST[name]] + 4 * i + 2 * half + 2)
                        for tt in range(NT):
                            for what in range(2):
                                m = block_n(slot, half * 2 * FVL + 512 * what, FVL, (512, FOX_H)[what], 2,
                                            n0 + 2 * what + tt, hs, tt, 4 * i + 2 * half,
                                            i == 0 and half == 0, i == 1 and half == 1)
                    if i == 0:
                        m.then_inc(S("part_done"), 1)
                    else:
                        m.then_inc(S("block_done"), 4)
                elif name == "w_qb":
                    if i == 0:
                        pe.wait_ge(S("mla_split"), 1)
                    for b in range(3):
                        n = BLOCKS["q_c"] + 3 * i + b
                        bank_free(n)
                        half_ready(g, b // 2)
                        block_t(slot, b * 3 * P, 3, n, cqs).then_inc(S("block_done"), 1)
                elif name == "w_kvb":
                    for b in range(4):
                        n = BLOCKS["kv_c"] + b
                        bank_free(n)
                        half_ready(g, 0)
                        block_t(slot, b * 2 * P, 2, n, ckvs).then_inc(S("block_done"), 1)
                    half_ready(g, 1)
                    for tt in range(NT):
                        n = BLOCKS["kv_c"] + 4 + tt
                        bank_free(n)
                        block_n(slot, 1024, 512, 512, 2, n, ckvs, tt).then_inc(S("block_done"), 1)
                elif name == "w_pp":
                    pe.wait_ge(S("p_split"), 2)
                    for b in range(KD):
                        n = BLOCKS["pgp"] + 8 + b
                        bank_free(n)
                        half_ready(g, b // 4)
                        block_t(slot, b * 2 * P, 2, n, ps).then_inc(S("block_done"), 1)
                else:
                    raise AssertionError(name)

            def gate_up(f):
                g0, n0 = FIRST[f"w_gu{f}"], BLOCKS[f"gu{f}"]
                first_tile(g0, n0)
                for b in range(2):
                    bank_free(n0 + 2 + b)
                    half_ready(g0 + 1, b)
                    block_t((g0 + 1) % 2, b * KD * P, KD, n0 + 2 + b, hs).then_inc(S("block_done"), 1)
                with pe.Fori(1, KF // 2) as i:
                    for j in range(2):
                        for b in range(2):
                            pe.wait_ge(S("block_freed"), i * 4 + (n0 + 2 * j + b - 3))
                            pe.wait_ge(S("w_lo"), i * 4 + (2 * (g0 + j) + b + 1))
                            block_t((g0 + j) % 2, b * KD * P, KD, n0 + 2 * j + b, hs).then_inc(S("block_done"), 1)

            def down(f):
                g0, n0 = FIRST[f"w_dn{f}"], BLOCKS[f"dn{f}"]
                half = KF // 2
                with pe.Fori(0, 2) as i:
                    for o in range(4):
                        n, g = n0 + o, g0 + 2 * o
                        pe.wait_ge(S("block_freed"), i * 4 + (n - 3))
                        for part in range(2):
                            pe.wait_ge(S("hid_lo"), KF * f + half * (part + 1))
                            pe.wait_ge(S("w_lo"), i * 16 + (2 * (g + part) + 1))
                            block_t((g + part) % 2, 0, 6, n, hid, half * part, part == 0, False)
                            pe.wait_ge(S("w_lo"), i * 16 + (2 * (g + part) + 2))
                            m = block_t((g + part) % 2, 6 * P, 5, n, hid, half * part + 6, False, part == 1)
                            m.then_inc(S("block_done" if part else "part_done"), 1)

            def have(*blocks):
                pe.wait_ge(S("block_freed"), max(blocks) + 1)

            def take(step):
                if step in TURN_A and TURN_A[step]:
                    pe.wait_ge(S("a_freed"), TURN_A[step])
                return area_a

            def take_t(step):
                if TURN_T[step]:
                    pe.wait_ge(S("t_freed"), TURN_T[step])
                return area_t

            flat = lambda v: v.rearrange("p a b -> p (a b)")

            def attend(step, pt0, pt1, value, turned, per_pair):
                pe.wait_ge(S("t_freed"), TURN_T[turned] + 1)
                o = take(step)
                for j in range(4):
                    h = j if step == "dsa_o" else HEAD_OF_SLOT[j]
                    if per_pair is None:
                        dst = o[:, h, :]
                    else:
                        dst = o[cols(h), h // 2, :]
                    mm(dst, value(0, h), pt0[:, j, :], True, False)
                    m = mm(dst[:, P:T], value(1, h), pt1[:, j, :], False, True)
                m.then_inc(S("a_full"), 1)

            def transposes(step, probs, tt, tag, turn):
                pe.wait_ge(S(tag), turn)
                t = flat(take_t(step))
                for c in range(tt + 1):
                    for h in range(4):
                        m = nc.tensor.transpose(t[:, 512 * c + P * h:512 * c + P * (h + 1)],
                                                probs[:, h, P * c:P * (c + 1)], ident)
                m.then_inc(S("t_full"), 1)

            def level(step):
                lv = int(step[3:])
                pe.wait_ge(S("level_e"), lv + 1)
                o = take(step) if step in TURN_A else take_t(step)
                for h in range(B_H):
                    for tt in range(NT):
                        at_ = slice(T * h + P * tt, T * h + P * tt + P)
                        if lv == 0:
                            w, m_ = hk[:, at_], flat(bq)[:, at_]
                        else:
                            w = m_ = he[lv % 2][:, at_]
                        m = mm(o[:, h, queries(tt)], w, m_, True, True)
                m.then_inc(S("a_full" if step in TURN_A else "t_full"), 1)

            def step(name):
                if name in NORMS:
                    t = take_t(name)
                    if name in SUMMED:
                        i = SUMMED_NORMS.index(name)
                        pe.wait_ge(S("squares_added"), (KD - 2) * (i + 1))
                        mm(t[:, 0, :], ones, sq_sum[:], True, False)
                        pe.wait_ge(S("square"), KD * (i + 1))
                        m = mm(t[:, 0, :], ones, sq_ring[:, (KD - 1) % 2, :], False, True)
                    else:
                        for k in range(KD):
                            pe.wait_ge(S("direct_square"), KD * DIRECT_NORMS.index(name) + k + 1)
                            m = mm(t[:, 0, :], ones, sq[:, k, :], k == 0, k == KD - 1)
                    m.then_inc(S("t_full"), 1)
                elif name.startswith("idx"):
                    tt, hg = int(name[3]), int(name[4])
                    have(BLOCKS["iq"] + 1 + 2 * hg)
                    o = take(name)
                    for j in range(4):
                        h = 4 * hg + HEAD_OF_SLOT[j]
                        m = mm(o[:, j, 0:keys(tt)], iq[cols(h), h // 2, queries(tt)], ik[cols(h), 0:keys(tt)],
                               True, True)
                    m.then_inc(S("a_full"), 1)
                elif name.startswith("dsa_s"):
                    tt = int(name[5])
                    have(BLOCKS["projT_b"] + 4)
                    o = take(name)
                    for h in range(A_H):
                        m = mm(o[:, h, 0:keys(tt)], aq[:, h, queries(tt)], ak[:, 0:keys(tt)], True, True)
                    m.then_inc(S("a_full"), 1)
                elif name.startswith("dsa_t"):
                    transposes(name, d_p, int(name[5]), "dsa_probs", int(name[5]) + 1)
                elif name == "dsa_o":
                    attend(name, d_pt0, d_pt1, lambda c, h: av[:, c, :], "dsa_t1", None)
                elif name == "mla_norm":
                    pe.wait_ge(S("mla_squares"), 1)
                    t = take_t(name)
                    for k in range(5):
                        m = mm(t[:, k // 3, :], ones, nsq[:, k, :], k in (0, 3), k in (2, 4))
                    m.then_inc(S("t_full"), 1)
                elif name == "rope_k":
                    have(BLOCKS["kpe_ik"])
                    o = take(name)
                    mm(o[:, 0, :], swap, kpe[:], True, True).then_inc(S("a_full"), 1)
                elif name == "rope_q":
                    have(BLOCKS["q_c"] + 5)
                    o = take(name)
                    for j in range(2):
                        m = mm(o[:, j, :], swap, qpe[:, j, :], True, True)
                    m.then_inc(S("a_full"), 1)
                elif name.startswith("mla_s"):
                    tt = int(name[5])
                    have(BLOCKS["kv_c"] + 5)
                    pe.wait_ge(S("rope_done"), 3)
                    o = take(name)
                    for j, h in enumerate(HEAD_OF_SLOT):
                        mm(o[:, j, 0:keys(tt)], qn[:, h, queries(tt)], kn[:, h, 0:keys(tt)], True, False)
                        m = mm(o[:, j, 0:keys(tt)], qpe[cols(h), h // 2, queries(tt)], kpe[cols(h), 0:keys(tt)],
                               False, True)
                    m.then_inc(S("a_full"), 1)
                elif name.startswith("mla_t"):
                    transposes(name, m_p, int(name[5]), "mla_probs", int(name[5]) + 1)
                elif name == "mla_o":
                    attend(name, m_pt0, m_pt1, lambda c, h: vc[:, c, P * h:P * h + P], "mla_t1", None)
                elif name.startswith("lev") and not name.startswith("level"):
                    level(name)
                elif name == "far":
                    pe.wait_ge(S("level_e"), 9)
                    o = take(name)
                    for h in range(B_H):
                        m = mm(o[:, h, 0:P], he[0][:, T * h:T * h + P], he[0][:, T * h + P:T * h + T], True, True)
                    m.then_inc(S("a_full"), 1)
                elif name == "hgrn_o":
                    pe.wait_ge(S("hgrn_merged"), 9)
                    o = take(name)
                    for h in range(B_H):
                        for tt in range(NT):
                            v = slice(P * h, P * h + P)
                            m = mm(o[:, h, queries(tt)], bi[:, tt, v], h0[:, h, queries(tt)], True, tt == 0)
                            if tt:
                                m = mm(o[:, h, queries(1)], bi[:, 0, v], h1[:, h, :], False, True)
                    m.then_inc(S("a_full"), 1)
                elif name == "hgrn_n":
                    pe.wait_ge(S("hgrn_squares"), 1)
                    t = flat(take_t(name))
                    for j in range(2):
                        m = mm(t[:, 512 * j:512 * j + 512], ones, hx[0][:, 512 * j:512 * j + 512], True, True)
                    m.then_inc(S("t_full"), 1)
                elif name in ("norm_fq", "norm_fk"):
                    pe.wait_ge(S("head_squares"), 1)
                    t = flat(take_t(name))
                    first = 0 if name == "norm_fq" else 4 * T
                    for j in range(2):
                        m = mm(t[:, 512 * j:512 * j + 512], ones64,
                               flat(n2sq)[:, first + 512 * j:first + 512 * j + 512], True, True)
                    m.then_inc(S("t_full"), 1)
                elif name == "forget":
                    pe.wait_ge(S("masks_loaded"), 16)
                    pe.wait_ge(S("log_forget"), 1)
                    t = take_t(name)
                    tri = con[:, C_TRI:C_TRI + T]
                    mm(t[0:FOX_H, 0, :], flog[:, 0, :], tri, True, False)
                    mm(t[0:FOX_H, 0, P:T], flog[:, 1, :], tri[:, 0:P], False, True).then_inc(S("t_full"), 1)
                elif name.startswith(("fox_s", "sb_s")):
                    fox = name[0] == "f"
                    hg, tt = int(name[-2]), int(name[-1])
                    q, k = (fq, fk) if fox else (sq_, sk_)
                    if fox:
                        pe.wait_ge(S("fox_normed"), 2)
                        pe.wait_ge(S("t_freed"), TURN_T["forget"] + 1)
                    else:
                        have(BLOCKS["qk2"] + 15)
                    o = take(name)
                    for j in range(4):
                        h = 4 * hg + HEAD_OF_SLOT[j]
                        dst = o[:, j, 0:keys(tt)]
                        m = mm(dst, q[cols(h), h // 2, queries(tt)], k[cols(h), h // 2, 0:keys(tt)], True, not fox)
                        if fox:
                            m = mm(dst, con[0:FOX_H, C_SEL + P * h:C_SEL + P * h + P], negf[0:FOX_H, 0:keys(tt)],
                                   False, True)
                    m.then_inc(S("a_full"), 1)
                elif name.startswith(("fox_t", "sb_t")):
                    fox = name[0] == "f"
                    hg, tt = int(name[-2]), int(name[-1])
                    transposes(name, f_p if fox else s_z, tt, "fox_probs" if fox else "sb_probs", 2 * hg + tt + 1)
                elif name.startswith(("fox_o", "sb_o")):
                    fox = name[0] == "f"
                    hg = int(name[-1])
                    v = fv if fox else sv
                    attend(name, f_pt0 if fox else s_pt0, f_pt1 if fox else s_pt1,
                           lambda c, h: v[:, c, HD * (4 * hg + h):HD * (4 * hg + h + 1)],
                           f"fox_t{hg}1" if fox else f"sb_t{hg}1", 0)

            pe.wait_ge(S("con_loaded"), 16)
            for kind, what in ORDER:
                if kind == "tile":
                    tile(what)
                elif kind == "step":
                    step(what)
                elif "gu" in what:
                    gate_up(int(what[-1]))
                else:
                    down(int(what[-1]))

        def softmax_columns(tag):
            i = 12 * ("dsa", "mla", "fox").index(tag)
            return st[:, i:i + 4], st[:, i + 4:i + 8], st[:, i + 8:i + 12]

        def softmaxes_before(step):
            return int(step[5]) * (2 if step.startswith("fox") else 1) + (int(step[6]) if step[6:] else 0)

        def gated_here(u):
            return u % 2 == 1 and (8 <= u < 24 or u >= 32)

        SUM_DEST = {}

        def dest(first, views):
            for k, v in enumerate(views):
                SUM_DEST[BLOCKS[first] + k if isinstance(first, str) else first + k] = v

        dest("kpe_ik", [kpe[:], ik[:]])
        dest("iq", [iq[:, k, :] for k in range(4)])
        dest("projT_b", [ak[:]] + [aq[:, k, :] for k in range(4)] + [cq[:, k, :] for k in range(3)]
             + [ckv[:, k, :] for k in range(2)] + [bf[:, k, :] for k in range(4)])
        dest("bq", [bq[:, k, :] for k in range(4)])
        dest("bg", [bg[:, k, :] for k in range(4)])
        dest("q_c", [qn[:, k, :] for k in range(4)] + [qpe[:, k, :] for k in range(2)])
        dest("kv_c", [kn[:, k, :] for k in range(4)])
        dest("gates1a", [gates[:, k, :] for k in range(8)])
        dest("gates1b", [gates[:, k, :] for k in range(8, 24)])
        dest("up1", [up1[:, k % 4, :] for k in range(24)])
        dest("qk2", [qk2[:, k, :] for k in range(16)])
        dest("gates2", [gates2[:, k, :] for k in range(16)])
        dest("up2", [up2[:, k % 4, :] for k in range(16)])
        dest("pgp", [pg[:, k, :] for k in range(8)] + [pp[:, k % 2, :] for k in range(8)])
        RESIDUAL = {BLOCKS[b] + k: (k, 1.0 if b in ("out1", "dn0") or b == "out2" else 0.5)
                    for b in ("out1", "dn0", "dn1", "out2", "dn2") for k in range(KD)}
        ENDING = {}
        for n_, g_ in ENDS.items():
            ENDING.setdefault(g_, []).append(n_)

        @block.scalar
        def _(act):
            def fn(out, in_, f, **kw):
                return nc.scalar.activation(out, in_, f, **kw)

            def link(ins):
                link.n += 1
                ins.then_inc(S("act_step"), 1)
                act.wait_ge(S("act_step"), link.n)
            link.n = 0

            flat = lambda v: v.rearrange("p a b -> p (a b)")

            def split_high(g, half):
                if g >= len(TILES):
                    return
                _, _, n, mid = TILES[g]
                if half == 0:
                    act.wait_ge(S(f"w_loaded{g % 2}"), 16 * (g // 2 + 1))
                    if g >= 2:
                        s, v = free_value(g - 2)
                        act.wait_ge(S(s), v)
                c = slice(0, mid) if half == 0 else slice(mid, n)
                fn(whi[:, g % 2, c], raw[:, g % 2, c], ACT.Copy).then_inc(S("w_hi"), 1)

            def square(n):
                i, k = SQUARED[n]
                act.wait_ge(S("block_freed"), n + 1)
                if k >= 2 or i:
                    act.wait_ge(S("squares_added"), (KD - 2) * i + (max(k - 2, 1) if k >= 2 else 0))
                if i and k < 2:
                    act.wait_ge(S("t_full"), TURN_T[SUMMED_NORMS[i - 1]] + 1)
                fn(sq_ring[:, k % 2, :], x[:, k, :], ACT.Square).then_inc(S("square"), 1)

            def tile(g):
                split_high(g + 1, 0)
                split_high(g + 1, 1)
                blocks = ENDING.get(g, [])
                for n in blocks:
                    if n in SQUARED and SQUARED[n][1]:
                        square(n - 1)
                    if n in SUM_DEST or n in RESIDUAL:
                        act.wait_ge(S("block_done"), n + 1)
                        fn(tmp[:, n % 4, :], acc[n % 4][:, T:2 * T], ACT.Copy,
                           scale=RESIDUAL.get(n, (0, 1.0))[1]).then_inc(S("half_copied"), 1)
                if g == FIRST["w_pg"] + 3:
                    act.wait_ge(S("block_freed"), BLOCKS["pgp"] + 8)
                    fn(flat(pg[:, :, :]), flat(pg[:, :, :]), ACT.Sigmoid).then_inc(S("ple_gate"), 1)

            def gate_up(f):
                g0, n0 = FIRST[f"w_gu{f}"], BLOCKS[f"gu{f}"]

                def split_next(t, j, half):
                    if isinstance(t, int):
                        split_high(g0 + t + 1, half)
                        return
                    c = slice(half * KD * P, (half + 1) * KD * P)
                    if half == 0:
                        act.wait_ge(S(f"w_loaded{1 - j}"), (t - j) * 8 + (16 * ((g0 + j + 1) // 2) + 16))
                    fn(whi[:, 1 - j, c], raw[:, 1 - j, c], ACT.Copy).then_inc(S("w_hi"), 1)

                def copy_half(t, j, b):
                    k = (n0 + 2 * j + b) % 4
                    act.wait_ge(S("block_done"), t * 2 + (n0 + b + 1))
                    fn(tmp[:, k, :], acc[k][:, T:2 * T], ACT.Copy).then_inc(S("half_copied"), 1)

                def body(t, j, first=False, last=False):
                    if not first:
                        act.wait_ge(S("block_freed"), t * 2 + (n0 - 1))
                        fn(sbuf[:, 1 - j, :], gbuf[:, 1 - j, :], ACT.Silu).then_inc(S("silu"), 1)
                        copy_half(t - 1, 1 - j, 1)
                    if not last:
                        split_next(t, j, 0)
                        split_next(t, j, 1)
                    if not first:
                        act.wait_ge(S("hid_value"), t + KF * f)
                        fn(hid[:, t - 1, 0:T], hbuf[:, 1 - j, :], ACT.Copy).then_inc(S("hid_hi"), 1)
                    if not last:
                        copy_half(t, j, 0)

                body(0, 0, first=True)
                with act.Fori(0, KF // 2 - 1) as i:
                    body(i * 2 + 1, 1)
                    body(i * 2 + 2, 0)
                body(KF - 1, 1)
                body(KF, 0, last=True)

            def down(f):
                for g in range(FIRST[f"w_dn{f}"], FIRST[f"w_dn{f}"] + 16):
                    tile(g)

            def hs_high(name, value_sem, value_base, src, chunks=range(KD)):
                for k in chunks:
                    act.wait_ge(S(value_sem), value_base + k + 1)
                    fn(hs[:, k, 0:T], src(k), ACT.Copy).then_inc(S("hs_hi"), 1)

            def norm(name):
                if name in SUMMED:
                    square(BLOCKS[SUMMED[name]] + KD - 1)
                else:
                    for k in range(KD):
                        if name == "norm0" and k % 4 == 0:
                            act.wait_ge(S(f"x_loaded{k // 4}"), 16)
                        if name == "norm3":
                            act.wait_ge(S("x_normed"), k + 1)
                        fn(sq[:, k, :], x[:, k, :], ACT.Square).then_inc(S("direct_square"), 1)
                act.wait_ge(S("t_full"), TURN_T[name] + 1)
                fn(xr[:], area_t[:, 0, :], ACT.Sqrt, scale=1.0 / D, bias=epsb[:, 0:1]).then_inc(S("t_freed"), 1)
                if name in HS_NORMS:
                    hs_high(name, "h_value", KD * HS_NORMS.index(name), lambda k: tmp[:, k % 4, :])

            def exps(tag, sc, p, tt, n):
                neg, sums, _ = softmax_columns(tag)
                act.wait_ge(S(f"{tag}_negmax"), n)
                for h in range(4):
                    m = fn(p[:, h, 0:keys(tt)], sc[:, h, 0:keys(tt)], ACT.Exp, bias=neg[:, h:h + 1],
                           accum_out=sums[:, h:h + 1])
                m.then_inc(S(f"{tag}_exp"), 1)

            def turned(step, tag, tt, pt0, pt1):
                act.wait_ge(S("t_full"), TURN_T[step] + 1)
                t = flat(area_t)
                if tt:
                    fn(pt1[:, :, :], t[:, 512:1024].rearrange("p (h n) -> p h n", h=4), ACT.Copy)
                fn(pt0[:, :, queries(tt)], t[:, 0:512].rearrange("p (h n) -> p h n", h=4), ACT.Copy)\
                    .then_inc(S("t_freed"), 1)

            def out_high(step, dst):
                act.wait_ge(S("a_full"), TURN_A[step] + 1)
                n = dst.shape[1]
                fn(dst, area_a[:, 0:n, :], ACT.Copy).then_inc(S("mix_hi"), 1)

            def log1p_exp(v, s):
                link(fn(v, v, ACT.Exp, scale=-1.0))
                fn(v, v, ACT.Ln, bias=1.0).then_inc(S(s), 1)

            def rms_factor(out, ps, width, free_sem):
                link(fn(out, ps, ACT.Ln, scale=1.0 / width, bias=epsb[:, 0:1]))
                fn(out, out, ACT.Exp, scale=-0.5).then_inc(S(free_sem), 1)

            def step(name):
                if name in NORMS:
                    norm(name)
                elif name == "tables":
                    act.wait_ge(S("angles"), 1)
                    fn(sin[:], rest[:], ACT.Sin).then_inc(S("sines"), 1)
                    fn(cos[:], over[:], ACT.Sin).then_inc(S("sines"), 1)
                elif name.startswith("idx"):
                    tt, hg = int(name[3]), int(name[4])
                    act.wait_ge(S("a_full"), TURN_A[name] + 1)
                    if tt:
                        act.wait_ge(S("scored"), 1)
                    fn(relu_l[:, 4 * hg:4 * hg + 4, 0:keys(tt)], area_a[:, :, 0:keys(tt)], ACT.Relu,
                       scale=IDX_D ** -0.5 * IDX_H ** -0.5).then_inc(S("a_freed"), 1)
                elif name.startswith("dsa_s"):
                    exps("dsa", d_sc, d_p, int(name[5]), int(name[5]) + 1)
                elif name.startswith("dsa_t"):
                    turned(name, "dsa", int(name[5]), d_pt0, d_pt1)
                elif name == "dsa_o":
                    out_high(name, osplit[0][:, :, 0:T])
                elif name == "input_squares":
                    act.wait_ge(S("block_freed"), BLOCKS["projT_b"] + 10)
                    act.wait_ge(S("sines"), 2)
                    fn(flat(nsq[:, 0:3, :]), flat(cq[:, :, :]), ACT.Square)
                    fn(flat(nsq[:, 3:5, :]), flat(ckv[:, :, :]), ACT.Square).then_inc(S("mla_squares"), 1)
                elif name == "mla_norm":
                    act.wait_ge(S("t_full"), TURN_T[name] + 1)
                    for i, n in enumerate((QR, KVR)):
                        ins = fn(nrm[:, i, :], area_t[:, i, :], ACT.Ln, scale=1.0 / n, bias=epsb[:, 0:1])
                    link(ins)
                    fn(flat(nrm[:, :, :]), flat(nrm[:, :, :]), ACT.Exp, scale=-0.5).then_inc(S("t_freed"), 1)
                elif name == "mla_normed":
                    act.wait_ge(S("mla_value"), 1)
                    fn(cqs[:, :, 0:T], nval[:, 0:3, :], ACT.Copy)
                    fn(ckvs[:, :, 0:T], nval[:, 3:5, :], ACT.Copy).then_inc(S("mla_hi"), 1)
                elif name.startswith(("dsa_p", "mla_p", "fox_p")):
                    tag, tt = name[:3], int(name[-1])
                    _, _, rec = softmax_columns(tag)
                    act.wait_ge(S(f"{tag}_sums"), softmaxes_before(name) + 1)
                    p = {"dsa": d_p, "mla": m_p, "fox": f_p}[tag]
                    for h in range(4):
                        m = fn(p[:, h, 0:keys(tt)], p[:, h, 0:keys(tt)], ACT.Copy, scale=rec[:, h:h + 1])
                    m.then_inc(S(f"{tag}_probs"), 1)
                elif name.startswith("mla_s"):
                    exps("mla", m_sc, m_p, int(name[5]), int(name[5]) + 1)
                elif name.startswith("mla_t"):
                    turned(name, "mla", int(name[5]), m_pt0, m_pt1)
                elif name == "mla_o":
                    out_high(name, osplit[2][:, :, 0:T])
                elif name.startswith("bias"):
                    for b in (2 * int(name[4:]), 2 * int(name[4:]) + 1):
                        if b >= BUCKETS - 1:
                            return
                        act.wait_ge(S("mask_made"), b + 1)
                        if b >= 2:
                            act.wait_ge(S("rise_used"), b - 1)
                        for h in range(POOL_H):
                            c = b * A_H + h
                            ins = fn(rise[b % 2][:, h, :], mask[b % 4][:], ACT.Copy, scale=drel[:, c:c + 1])
                        ins.then_inc(S("rise_made"), 1)
                elif name == "bound0":
                    act.wait_ge(S("lb_diff"), 1)
                    fn(st[:, 44:48], st[:, 40:44], ACT.Exp).then_inc(S("lb_exp"), 1)
                elif name == "bound1":
                    act.wait_ge(S("lb_ready"), 1)
                    fn(st[:, 64:68], st[:, 60:64], ACT.Ln)
                    fn(st[:, 68:72], st[:, 56:60], ACT.Ln, scale=-1.0, bias=1.0).then_inc(S("lb_logs"), 1)
                elif name == "decay_xa":
                    act.wait_ge(S("block_freed"), BLOCKS["projT_b"] + 14)
                    act.wait_ge(S("decay_space"), 1)
                    link(fn(hx[0][:], flat(bf[:, :, :]), ACT.Abs))
                    log1p_exp(hx[0][:], "sig_log")
                elif name == "decay_xb":
                    act.wait_ge(S("decay_u"), 1)
                    link(fn(hx[0][:], hx[0][:], ACT.Abs))
                    log1p_exp(hx[0][:], "decay_log")
                elif name == "decay_xc":
                    act.wait_ge(S("decay_sum"), 1)
                    fn(hk[:], flat(bf[:, :, :]), ACT.Sigmoid, scale=-1.0).then_inc(S("key_sig"), 1)
                elif name.startswith("level_x"):
                    lv = int(name[7:])
                    e = he[lv % 2]
                    act.wait_ge(S("exponents"), lv)
                    fn(e[:], e[:], ACT.Exp).then_inc(S("decays"), 1)
                elif name == "hgrn_n":
                    act.wait_ge(S("t_full"), TURN_T[name] + 1)
                    rms_factor(hx[1][:], flat(area_t), P, "t_freed")
                    act.wait_ge(S("block_freed"), BLOCKS["bg"] + 4)
                    fn(hx[0][:], flat(bg[:, :, :]), ACT.Silu).then_inc(S("hgrn_gate"), 1)
                    act.wait_ge(S("hgrn_value"), 1)
                    fn(osplit[1][:, :, 0:T], hx[2][:].rearrange("p (h n) -> p h n", h=4), ACT.Copy)\
                        .then_inc(S("hgrn_hi"), 1)
                elif name == "hgrn_o":
                    act.wait_ge(S("a_full"), TURN_A[name] + 1)
                    fn(hx[0][:], flat(area_a), ACT.Square).then_inc(S("hgrn_squares"), 1)
                elif name.startswith("gate_sigmoid"):
                    first_block, b = name[12] == "1", int(name[14])
                    before = BLOCKS["gates2"] if not first_block else BLOCKS["gates1b"] - KD
                    act.wait_ge(S("block_freed"), before + (b + 1) * KD)
                    v = flat((gates if first_block else gates2)[:, 8 * b:8 * b + 8, :])
                    fn(v, v, ACT.Sigmoid).then_inc(S("gates_on"), 1)
                elif name.startswith("split_mixed"):
                    base_ = 16 if name[-1] == "1" else 24 + 8
                    m = mixed1 if name[-1] == "1" else mixed2
                    hs_high(name, "mixed", base_, lambda k: m[:, k, :], range(4, KD))
                elif name.startswith("half_mixed"):
                    base_ = 16 if name[-1] == "1" else 24 + 8
                    m = mixed1 if name[-1] == "1" else mixed2
                    hs_high(name, "mixed", base_, lambda k: m[:, k, :], range(4))
                elif name == "head_squares":
                    act.wait_ge(S("block_freed"), BLOCKS["qk2"] + 8)
                    for i in range(2):
                        m = fn(flat(n2sq[:, 4 * i:4 * i + 4, :]), flat(qk2[:, 4 * i:4 * i + 4, :]), ACT.Square)
                    m.then_inc(S("head_squares"), 1)
                elif name in ("norm_fq", "norm_fk"):
                    act.wait_ge(S("t_full"), TURN_T[name] + 1)
                    i = 0 if name == "norm_fq" else 4
                    fn(flat(n2r[:, i:i + 4, :]), flat(area_t), ACT.Ln, scale=1.0 / HD, bias=epsb[:, 0:1])\
                        .then_inc(S("t_freed"), 1)
                    if name == "norm_fk":
                        act.wait_ge(S("t_freed"), TURN_T[name] + 1)
                        fn(flat(n2r[:, :, :]), flat(n2r[:, :, :]), ACT.Exp, scale=-0.5).then_inc(S("head_factor"), 1)
                elif name == "log_forget":
                    act.wait_ge(S("block_freed"), BLOCKS["fvl"] + 4)
                    link(fn(flog2[:], flat(flog[:, :, :]), ACT.Abs))
                    log1p_exp(flog2[:], "forget_log")
                elif name == "forget":
                    act.wait_ge(S("t_full"), TURN_T[name] + 1)
                    fn(negf[0:FOX_H, :], area_t[0:FOX_H, 0, :], ACT.Copy, scale=-float(HD) ** 0.5)\
                        .then_inc(S("t_freed"), 1)
                elif name.startswith("fox_s"):
                    hg, tt = int(name[-2]), int(name[-1])
                    exps("fox", f_sc, f_p, tt, 2 * hg + tt + 1)
                elif name.startswith("sb_s"):
                    hg, tt = int(name[-2]), int(name[-1])
                    n = 2 * hg + tt + 1
                    act.wait_ge(S("a_full"), TURN_A[name] + 1)
                    ks = keys(tt)
                    fn(s_z[:, :, 0:ks], area_a[:, :, 0:ks], ACT.Copy, scale=HD ** -0.5)
                    fn(s_a[:, :, 0:ks], area_a[:, :, 0:ks], ACT.Abs, scale=HD ** -0.5).then_inc(S("a_freed"), 1)
                    act.wait_ge(S("a_freed"), TURN_A[name] + 1)
                    link(fn(s_a[:, :, 0:ks], s_a[:, :, 0:ks], ACT.Exp, scale=-1.0))
                    fn(s_a[:, :, 0:ks], s_a[:, :, 0:ks], ACT.Ln, bias=1.0).then_inc(S("sb_log"), 1)
                elif name.startswith("sb_x"):
                    hg, tt = int(name[-2]), int(name[-1])
                    ks = keys(tt)
                    act.wait_ge(S("sb_arg"), 2 * hg + tt + 1)
                    fn(s_z[:, :, 0:ks], s_z[:, :, 0:ks], ACT.Exp).then_inc(S("sb_probs"), 1)
                elif name.startswith("fox_t"):
                    turned(name, "fox", int(name[-1]), f_pt0, f_pt1)
                elif name.startswith("sb_t"):
                    turned(name, "sb", int(name[-1]), s_pt0, s_pt1)
                elif name.startswith(("fox_o", "sb_o")):
                    hg = int(name[-1])
                    out_high(name, osplit2[0 if name[0] == "f" else 1][:, 2 * hg:2 * hg + 2, 0:T])
                elif name == "split_p":
                    act.wait_ge(S("p_loaded"), 16)
                    fn(ps[:, :, 0:T], praw[:, :, :], ACT.Copy).then_inc(S("p_hi"), 1)

            act.wait_ge(S("eps_set"), 1)
            split_high(0, 0)
            split_high(0, 1)
            for kind, what in ORDER:
                if kind == "tile":
                    tile(what)
                elif kind == "step":
                    step(what)
                elif "gu" in what:
                    gate_up(int(what[-1]))
                else:
                    down(int(what[-1]))

        @block.vector
        def _(dve):
            v = nc.vector
            flat = lambda w: w.rearrange("p a b -> p (a b)")

            def link(ins):
                link.n += 1
                ins.then_inc(S("dve_step"), 1)
                dve.wait_ge(S("dve_step"), link.n)
            link.n = 0

            def split_low(g, half):
                if g >= len(TILES):
                    return
                _, _, n, mid = TILES[g]
                dve.wait_ge(S("w_hi"), 2 * g + half + 1)
                c = slice(0, mid) if half == 0 else slice(mid, n)
                v.tensor_tensor(wlo[:, g % 2, c], raw[:, g % 2, c], whi[:, g % 2, c].bitcast(F32), ALU.subtract)\
                    .then_inc(S("w_lo"), 1)

            halves = [0]

            def read_block(n):
                if n in SUM_DEST or n in RESIDUAL:
                    halves[0] += 1
                    dve.wait_ge(S("half_copied"), halves[0])
                    bank, t = acc[n % 4][:, 0:T], tmp[:, n % 4, :]
                else:
                    dve.wait_ge(S("block_done"), n + 1)
                    bank = acc[n % 4]
                if n in RESIDUAL:
                    k, scale = RESIDUAL[n]
                    link(v.tensor_tensor(t, t, x[:, k, :], ALU.add))
                    v.scalar_tensor_tensor(x[:, k, :], bank, scale, t, ALU.mult, ALU.add)\
                        .then_inc(S("block_freed"), 1)
                elif n in SUM_DEST:
                    u = None
                    if 0 <= n - BLOCKS["up1"] < 24:
                        u = n - BLOCKS["up1"]
                    elif 0 <= n - BLOCKS["up2"] < 16:
                        u = n - BLOCKS["up2"] + 24
                    if u is not None and u >= 4:
                        dve.wait_ge(S("mixed"), u - 3)
                    if u is not None and gated_here(u):
                        g = gates[:, u, :] if u < 24 else gates2[:, u - 24, :]
                        dve.wait_ge(S("gates_on"), u // KD + 1)
                        link(v.tensor_tensor(SUM_DEST[n], bank, t, ALU.add))
                        v.tensor_tensor(SUM_DEST[n], SUM_DEST[n], g, ALU.mult).then_inc(S("block_freed"), 1)
                    else:
                        v.tensor_tensor(SUM_DEST[n], bank, t, ALU.add).then_inc(S("block_freed"), 1)
                elif n - BLOCKS["avw"] in (0, 1):
                    tt = n - BLOCKS["avw"]
                    v.tensor_copy(av[:, tt, :], bank[:, 0:P])
                    v.tensor_copy(iw[:, tt, :], bank[:, P:AVW]).then_inc(S("block_freed"), 1)
                elif n - BLOCKS["fvl"] in (2, 3):
                    dve.wait_ge(S("fb_loaded"), 16)
                    v.tensor_tensor(flog[:, n - BLOCKS["fvl"] - 2, :], bank[:, 0:FOX_H], fb[:], ALU.add)\
                        .then_inc(S("block_freed"), 1)
                else:
                    for name, buf, first in (("bi", bi, 0), ("kv_c", vc, 4), ("fvl", fv, 0), ("sv", sv, 0)):
                        if n - BLOCKS[name] - first in (0, 1):
                            v.tensor_copy(buf[:, n - BLOCKS[name] - first, :], bank[:, :])\
                                .then_inc(S("block_freed"), 1)
                            break
                    else:
                        raise AssertionError(n)
                if n >= BLOCKS["pgp"] + 8:
                    k = n - BLOCKS["pgp"] - 8
                    dve.wait_ge(S("ple_gate"), 1)
                    dve.wait_ge(S("block_freed"), n + 1)
                    link(v.tensor_tensor(pp[:, k % 2, :], pp[:, k % 2, :], pg[:, k, :], ALU.mult))
                    v.tensor_tensor(x[:, k, :], x[:, k, :], pp[:, k % 2, :], ALU.add).then_inc(S("out_ready"), 1)

            def tile(g):
                split_low(g + 1, 0)
                split_low(g + 1, 1)
                for n in ENDING.get(g, []):
                    read_block(n)

            def gate_up(f):
                g0, n0 = FIRST[f"w_gu{f}"], BLOCKS[f"gu{f}"]
                c0 = halves[0]

                def split_next(t, j, half):
                    if isinstance(t, int):
                        split_low(g0 + t + 1, half)
                        return
                    c = slice(half * KD * P, (half + 1) * KD * P)
                    dve.wait_ge(S("w_hi"), t * 2 + (2 * g0 + half + 3))
                    v.tensor_tensor(wlo[:, 1 - j, c], raw[:, 1 - j, c], whi[:, 1 - j, c].bitcast(F32),
                                    ALU.subtract).then_inc(S("w_lo"), 1)

                def sum_halves(t, j, b):
                    k = (n0 + 2 * j + b) % 4
                    dve.wait_ge(S("half_copied"), t * 2 + (c0 + b + 1))
                    v.tensor_tensor((gbuf, ubuf)[b][:, j, :], acc[k][:, 0:T], tmp[:, k, :], ALU.add)\
                        .then_inc(S("block_freed"), 1)

                def body(t, j, first=False, last=False):
                    if not first:
                        sum_halves(t - 1, 1 - j, 1)
                        dve.wait_ge(S("silu"), t + KF * f)
                        dve.wait_ge(S("block_freed"), t * 2 + n0)
                        v.tensor_tensor(hbuf[:, 1 - j, :], sbuf[:, 1 - j, :], ubuf[:, 1 - j, :], ALU.mult)\
                            .then_inc(S("hid_value"), 1)
                    if not last:
                        split_next(t, j, 0)
                        split_next(t, j, 1)
                    if not first:
                        dve.wait_ge(S("hid_hi"), t + KF * f)
                        v.tensor_tensor(hid[:, t - 1, T:2 * T], hbuf[:, 1 - j, :], hid[:, t - 1, 0:T].bitcast(F32),
                                        ALU.subtract).then_inc(S("hid_lo"), 1)
                    if not last:
                        sum_halves(t, j, 0)

                body(0, 0, first=True)
                with dve.Fori(0, KF // 2 - 1) as i:
                    body(i * 2 + 1, 1)
                    body(i * 2 + 2, 0)
                body(KF - 1, 1)
                body(KF, 0, last=True)
                halves[0] += 2 * KF

            def down(f):
                for g in range(FIRST[f"w_dn{f}"], FIRST[f"w_dn{f}"] + 16):
                    tile(g)

            def hs_low(name, k, src):
                base_ = KD * HS_STARTS.index(name.replace("half", "split"))
                dve.wait_ge(S("hs_hi"), base_ + k + 1)
                v.tensor_tensor(hs[:, k, T:2 * T], src, hs[:, k, 0:T].bitcast(F32), ALU.subtract)\
                    .then_inc(S("hs_lo"), 1)

            def norm(name):
                dve.wait_ge(S("t_freed"), TURN_T[name] + 1)
                link(v.reciprocal(xr[:], xr[:]))
                g = norm_of(name)
                for k in range(KD):
                    gain = vec[:, g + k:g + k + 1]
                    if name == "norm2":
                        v.scalar_tensor_tensor(x[:, k, :], x[:, k, :], gain, xr[:], ALU.mult, ALU.mult)\
                            .then_inc(S("x_normed"), 1)
                        continue
                    if k >= 2:
                        hs_low(name, k - 2, tmp[:, (k - 2) % 4, :])
                    v.scalar_tensor_tensor(tmp[:, k % 4, :], x[:, k, :], gain, xr[:], ALU.mult, ALU.mult)\
                        .then_inc(S("h_value"), 1)
                if name != "norm2":
                    for k in (KD - 2, KD - 1):
                        hs_low(name, k, tmp[:, k % 4, :])

            def row_max(tag, sc, tt):
                neg, _, _ = softmax_columns(tag)
                v.tensor_reduce(neg, sc[:, :, 0:keys(tt)], AX.X, ALU.max, negate=True)\
                    .then_inc(S(f"{tag}_negmax"), 1)

            def out_low(step, dst, n_done):
                dve.wait_ge(S("mix_hi"), n_done)
                n = dst.shape[1]
                v.tensor_tensor(dst[:, :, T:2 * T], area_a[:, 0:n, :], dst[:, :, 0:T].bitcast(F32), ALU.subtract)\
                    .then_inc(S("a_freed"), 1)

            thresholds = bucket_thresholds()

            def bucket_masks(part):
                for b in (2 * part, 2 * part + 1):
                    if b >= BUCKETS - 1:
                        return
                    if b >= 4:
                        dve.wait_ge(S("rise_made"), b - 3)
                    v.tensor_scalar(mask[b % 4][:], dist[:], thresholds[b], None, ALU.is_ge)\
                        .then_inc(S("mask_made"), 1)

            def bias_part(part):
                for b in (2 * part, 2 * part + 1):
                    if b < BUCKETS - 1:
                        dve.wait_ge(S("mask_made"), b + 1)
                        for h in range(POOL_H, A_H):
                            c = b * A_H + h
                            ins = v.scalar_tensor_tensor(bias[:, h, :], mask[b % 4][:], drel[:, c:c + 1],
                                                         bias[:, h, :], ALU.mult, ALU.add)
                        link(ins)
                bucket_masks(part + 1)

            def top(part, tt):
                ks = keys(tt)
                sc, wk = score[:, 0:ks], work[:, 0:ks]
                best = st[:, 80:88]
                if part == "a":
                    dve.wait_ge(S("a_freed"), TURN_A[f"idx{tt}1"] + 1)
                    dve.wait_ge(S("block_freed"), BLOCKS["avw"] + 2)
                    dve.wait_ge(S("masks_loaded"), 16)
                    for i in range(IDX_H):
                        into = causal(tt, C_CM) if i == 0 else sc
                        h = i // 4 * 4 + HEAD_OF_SLOT[i % 4]
                        ins = v.scalar_tensor_tensor(sc, relu_l[:, i, 0:ks], iw[:, tt, h:h + 1], into,
                                                     ALU.mult, ALU.add)
                        if i < IDX_H - 1:
                            link(ins)
                    ins.then_inc(S("scored"), 1)
                    dve.wait_ge(S("scored"), tt + 1)
                    return
                if part in "bc":
                    rounds = range(TOPK // 8)[:4] if part == "b" else range(TOPK // 8)[4:]
                    for r in rounds:
                        cur = sc if r == 0 else wk
                        link(v.max(best, cur))
                        if r < TOPK // 8 - 1:
                            link(v.match_replace(wk, best, cur, -3e38))
                    return
                least = best[:, 7:8]
                count, need = st[:, 88:89], st[:, 89:90]
                gt, eq, rk = above[:, 0:ks], equal[:, 0:ks], rank[:, 0:ks]
                link(v.tensor_scalar(gt, sc, least, None, ALU.is_gt, ALU.add, accum_out=count))
                link(v.tensor_scalar(eq, sc, least, None, ALU.is_equal))
                link(v.tensor_scalar(need, count, -1.0, float(TOPK), ALU.mult, ALU.add))
                link(v.tensor_tensor_scan(rk, ones_row[:, 0:ks], eq, 0.0, ALU.mult, ALU.add))
                link(v.scalar_tensor_tensor(eq, rk, need, eq, ALU.is_le, ALU.mult))
                link(v.tensor_tensor(gt, gt, eq, ALU.add))
                link(v.tensor_scalar(gt, gt, -NEG, NEG, ALU.mult, ALU.add))
                link(v.tensor_tensor(chosen[tt][:], gt, causal(tt, C_CM), ALU.add))

            def level_parts(buf, half):
                w = buf.rearrange("p (n s h) -> p n s h", s=2, h=half)
                return w[:, :, 0, :], w[:, :, 1, :]

            def exponents(lv):
                e = he[lv % 2][:]
                if lv >= 3:
                    dve.wait_ge(S("hgrn_merged"), lv - 1)
                if lv < 8:
                    half = LEVELS[lv]
                    bl, br = level_parts(hb[:], half)
                    el, er = level_parts(e, half)
                    n = bl.shape[1]
                    mid = bl[:, :, half - 1:half].to_broadcast([P, n, half])
                    v.tensor_tensor(el, mid, bl, ALU.subtract)
                    if half < CHUNK:
                        ins = v.tensor_tensor(er, br, mid, ALU.subtract)
                    else:
                        ins = v.tensor_copy(er, br)
                    ins.then_inc(S("exponents"), 1)
                else:
                    b4 = hb[:].rearrange("p (h c j) -> p h c j", h=B_H, j=CHUNK)
                    e4 = e.rearrange("p (h c j) -> p h c j", h=B_H, j=CHUNK)
                    for c in range(2):
                        last = b4[:, :, c, CHUNK - 1:CHUNK].to_broadcast([P, B_H, CHUNK])
                        v.tensor_tensor(e4[:, :, c, :], last, b4[:, :, c, :], ALU.subtract)
                    link(v.tensor_copy(e4[:, :, 2, :], b4[:, :, 2, :]))
                    last1 = b4[:, :, 1, CHUNK - 1:CHUNK].to_broadcast([P, B_H, CHUNK])
                    last2 = b4[:, :, 2, CHUNK - 1:CHUNK].to_broadcast([P, B_H, CHUNK])
                    link(v.tensor_tensor(e4[:, :, 0, :], e4[:, :, 0, :], last1, ALU.add))
                    v.tensor_tensor(e4[:, :, 3, :], b4[:, :, 3, :], last2, ALU.add).then_inc(S("exponents"), 1)

            def decayed(lv):
                e = he[lv % 2][:]
                dve.wait_ge(S("decays"), lv)
                half = LEVELS[lv] if lv < 8 else P
                el, er = level_parts(e, half)
                kl, _ = level_parts(hk[:], half)
                _, qr = level_parts(flat(bq[:, :, :]), half)
                v.tensor_tensor(el, el, kl, ALU.mult)
                v.tensor_tensor(er, er, qr, ALU.mult).then_inc(S("level_e"), 1)

            def step(name):
                if name in NORMS:
                    norm(name)
                elif name == "tables":
                    tables()
                elif name == "distances":
                    distances()
                elif name.startswith("bias"):
                    bias_part(int(name[4:]))
                elif name.startswith("top"):
                    top(name[4], int(name[5]))
                elif name.startswith("dsa_s"):
                    tt = int(name[5])
                    ks = keys(tt)
                    b = bias[:, :, 0:P] if tt == 0 else bias[:, :, P:P + T]
                    dve.wait_ge(S("a_full"), TURN_A[name] + 1)
                    dve.wait_ge(S("rise_used"), BUCKETS - 1)
                    v.scalar_tensor_tensor(d_sc[:, :, 0:ks], area_a[:, :, 0:ks], float(P) ** -0.5, b,
                                           ALU.mult, ALU.add).then_inc(S("a_freed"), 1)
                    dve.wait_ge(S("a_freed"), TURN_A[name] + 1)
                    link(v.tensor_tensor(d_sc[:, :, 0:ks], d_sc[:, :, 0:ks], heads4(chosen[tt][:], ks), ALU.add))
                    row_max("dsa", d_sc, tt)
                elif name.startswith(("dsa_p", "mla_p", "fox_p")):
                    tag = name[:3]
                    _, sums, rec = softmax_columns(tag)
                    dve.wait_ge(S(f"{tag}_exp"), softmaxes_before(name) + 1)
                    v.reciprocal(rec, sums).then_inc(S(f"{tag}_sums"), 1)
                elif name == "dsa_o":
                    out_low(name, osplit[0], 1)
                elif name == "mla_normed":
                    dve.wait_ge(S("t_freed"), TURN_T["mla_norm"] + 1)
                    for k in range(5):
                        src = cq[:, k, :] if k < 3 else ckv[:, k - 3, :]
                        g = VEC["mla_q_norm"] + k if k < 3 else VEC["mla_kv_norm"] + k - 3
                        ins = v.scalar_tensor_tensor(nval[:, k, :], src, vec[:, g:g + 1], nrm[:, k // 3, :],
                                                     ALU.mult, ALU.mult)
                    ins.then_inc(S("mla_value"), 1)
                    dve.wait_ge(S("mla_hi"), 1)
                    v.tensor_tensor(cqs[:, :, T:2 * T], nval[:, 0:3, :], cqs[:, :, 0:T].bitcast(F32), ALU.subtract)
                    v.tensor_tensor(ckvs[:, :, T:2 * T], nval[:, 3:5, :], ckvs[:, :, 0:T].bitcast(F32),
                                    ALU.subtract).then_inc(S("mla_split"), 1)
                elif name == "rope_k":
                    rotate(name, 0, kpe[:], True)
                elif name == "rope_q":
                    for j in range(2):
                        rotate(name, j, qpe[:, j, :], j == 1)
                elif name.startswith("mla_s"):
                    tt = int(name[5])
                    ks = keys(tt)
                    dve.wait_ge(S("a_full"), TURN_A[name] + 1)
                    v.scalar_tensor_tensor(m_sc[:, :, 0:ks], area_a[:, :, 0:ks], float(NOPE + ROPE) ** -0.5,
                                           heads4(causal(tt, C_CM), ks), ALU.mult, ALU.add)\
                        .then_inc(S("a_freed"), 1)
                    dve.wait_ge(S("a_freed"), TURN_A[name] + 1)
                    row_max("mla", m_sc, tt)
                elif name == "mla_o":
                    out_low(name, osplit[2], 2)
                elif name == "bound0":
                    lbl = vec[:, VEC["lb_logits"]:VEC["lb_logits"] + B_H]
                    v.tensor_tensor(st[:, 40:44], lbl, lbl, ALU.subtract).then_inc(S("lb_diff"), 1)
                elif name == "bound1":
                    dve.wait_ge(S("lb_exp"), 1)
                    link(v.reciprocal(st[:, 48:52], st[:, 44:48]))
                    link(v.tensor_tensor(st[:, 52:56], st[:, 44:48], st[:, 48:52], ALU.mult))
                    link(v.tensor_tensor(st[:, 56:60], st[:, 52:56], st[:, 52:56], ALU.subtract))
                    link(v.tensor_scalar(st[:, 72:76], st[:, 56:60], -1.0, 1.0, ALU.mult, ALU.add))
                    v.tensor_scalar(st[:, 60:64], st[:, 56:60], LB_FLOOR, 2.0 ** 60, ALU.max, ALU.mult)\
                        .then_inc(S("lb_ready"), 1)
                elif name in ("decay_a", "decay_b", "decay_c"):
                    decay(name[6])
                elif name == "level_m0":
                    dve.wait_ge(S("key_sig"), 1)
                    for h in range(B_H):
                        s = slice(T * h, T * h + T)
                        v.tensor_scalar(hk[:, s], hk[:, s], st[:, 72 + h:73 + h], None, ALU.mult)
                    v.memset(flat(h0[:, :, :]), 0.0)
                    dve.wait_ge(S("block_freed"), BLOCKS["bq"] + 4)
                    v.tensor_scalar(flat(bq[:, :, :]), flat(bq[:, :, :]), float(P) ** -0.5, None, ALU.mult)\
                        .then_inc(S("level_e"), 1)
                    dve.wait_ge(S("level_e"), 1)
                elif name.startswith("level_e"):
                    exponents(int(name[7:]))
                elif name.startswith("level_m"):
                    decayed(int(name[7:]))
                elif name.startswith("lev") and not name.startswith("level"):
                    lv = int(name[3:])
                    in_a = name in TURN_A
                    dve.wait_ge(S("a_full" if in_a else "t_full"), (TURN_A if in_a else TURN_T)[name] + 1)
                    m = con[:, C_LEV + P * lv:C_LEV + P * (lv + 1)].bitcast(I32).unsqueeze(1)
                    out = h0[:, :, :].rearrange("p h (t n) -> p (h t) n", n=P)
                    src = (area_a if in_a else area_t)[:, :, :].rearrange("p h (t n) -> p (h t) n", n=P)
                    v.copy_predicated(out, m.to_broadcast([P, 8, P]), src)\
                        .then_inc(S("a_freed" if in_a else "t_freed"), 1)
                    dve.wait_ge(S("a_freed" if in_a else "t_freed"), (TURN_A if in_a else TURN_T)[name] + 1)
                    dve.sem_inc(S("hgrn_merged"), 1)
                elif name == "far":
                    dve.wait_ge(S("a_full"), TURN_A[name] + 1)
                    v.tensor_copy(h1[:, :, :], area_a[:, :, 0:P]).then_inc(S("a_freed"), 1)
                    dve.wait_ge(S("a_freed"), TURN_A[name] + 1)
                    dve.sem_inc(S("hgrn_merged"), 1)
                elif name == "hgrn_n":
                    dve.wait_ge(S("t_freed"), TURN_T[name] + 1)
                    g = VEC["hgrn_out"]
                    v.scalar_tensor_tensor(hx[2][:], flat(area_a), vec[:, g:g + 1], hx[1][:], ALU.mult, ALU.mult)\
                        .then_inc(S("a_freed"), 1)
                    dve.wait_ge(S("a_freed"), TURN_A["hgrn_o"] + 1)
                    dve.wait_ge(S("hgrn_gate"), 1)
                    v.tensor_tensor(hx[2][:], hx[2][:], hx[0][:], ALU.mult).then_inc(S("hgrn_value"), 1)
                    dve.wait_ge(S("hgrn_hi"), 1)
                    v.tensor_tensor(osplit[1][:, :, T:2 * T], hx[2][:].rearrange("p (h n) -> p h n", h=4),
                                    osplit[1][:, :, 0:T].bitcast(F32), ALU.subtract).then_inc(S("hgrn_split"), 1)
                elif name.startswith("split_mixed"):
                    m = mixed1 if name[-1] == "1" else mixed2
                    for k in range(4, KD):
                        hs_low(name, k, m[:, k, :])
                elif name.startswith("half_mixed"):
                    m = mixed1 if name[-1] == "1" else mixed2
                    for k in range(4):
                        hs_low(name, k, m[:, k, :])
                elif name == "fox_normed":
                    dve.wait_ge(S("head_factor"), 1)
                    for i, (src, g) in enumerate(((fq, "q_norm"), (fk, "k_norm"))):
                        v.scalar_tensor_tensor(src, src, vec[:, VEC[g]:VEC[g] + 1], n2r[:, 4 * i:4 * i + 4, :],
                                               ALU.mult, ALU.mult).then_inc(S("fox_normed"), 1)
                elif name == "log_forget":
                    dve.wait_ge(S("forget_log"), 1)
                    dve.wait_ge(S("block_freed"), BLOCKS["fvl"] + 4)
                    v.scalar_tensor_tensor(flat(flog[:, :, :]), flat(flog[:, :, :]), 0.0, flog2[:], ALU.min,
                                           ALU.subtract).then_inc(S("log_forget"), 1)
                    for ks, keep in ((P, s_keep1), (T, s_keep2)):
                        link(v.memset(keep[:], 1.0))
                        k3 = keep[:].rearrange("p (h n) -> p h n", h=4)
                        link(v.memset(k3[:, :, ks:ks + 1], 0.0))
                elif name.startswith("fox_s"):
                    hg, tt = int(name[-2]), int(name[-1])
                    ks = keys(tt)
                    dve.wait_ge(S("a_full"), TURN_A[name] + 1)
                    v.scalar_tensor_tensor(f_sc[:, :, 0:ks], area_a[:, :, 0:ks], float(HD) ** -0.5,
                                           heads4(causal(tt, C_CM), ks), ALU.mult, ALU.add)\
                        .then_inc(S("a_freed"), 1)
                    dve.wait_ge(S("a_freed"), TURN_A[name] + 1)
                    row_max("fox", f_sc, tt)
                elif name.startswith("sb_m"):
                    stick_breaking(name)
                elif name.startswith(("fox_o", "sb_o")):
                    fox, hg = name[0] == "f", int(name[-1])
                    order = ["fox_o0", "sb_o0", "fox_o1", "sb_o1"]
                    out_low(name, osplit2[0 if fox else 1][:, 2 * hg:2 * hg + 2, :], 3 + order.index(name))
                elif name == "split_p":
                    dve.wait_ge(S("p_hi"), 1)
                    for k in range(2):
                        v.tensor_tensor(ps[:, k, T:2 * T], praw[:, k, :], ps[:, k, 0:T].bitcast(F32), ALU.subtract)\
                            .then_inc(S("p_split"), 1)

            def distances():
                dve.wait_ge(S("pos_loaded"), 16 * 3)
                link(v.tensor_copy(posf[:], posi[:]))
                link(v.tensor_copy(postf[:], post[:]))
                for tt in range(NT):
                    d = dist[:, 0:P] if tt == 0 else dist[:, P:P + T]
                    link(v.tensor_scalar(d, posf[:, 0:keys(tt)], -1.0, postf[:, tt:tt + 1], ALU.mult, ALU.add))
                v.tensor_tensor(drel[:], relb[:, A_H:], relb[:, 0:(BUCKETS - 1) * A_H], ALU.subtract)
                for h in range(A_H):
                    ins = v.tensor_scalar(bias[:, h, :], dist[:], 0.0, relb[:, h:h + 1], ALU.mult, ALU.add)
                ins.then_inc(S("bias_begun"), 1)
                bucket_masks(0)

            def tables():
                two_pi = [6.28125, 1.9350051879882812e-03, 3.01991598196e-07]
                magic = 1.5 * 2 ** 23
                link(v.tensor_scalar(ang[:], posf[:], con[:, C_INVF:C_INVF + 1], None, ALU.mult))
                link(v.tensor_scalar(turns[:], ang[:], 1.0 / (2 * np.pi), magic, ALU.mult, ALU.add))
                link(v.tensor_scalar(turns[:], turns[:], magic, None, ALU.subtract))
                src = ang
                for c in two_pi:
                    link(v.scalar_tensor_tensor(rest[:], turns[:], -c, src[:], ALU.mult, ALU.add))
                    src = rest
                pi = 3.1415925
                link(v.tensor_scalar(over[:], rest[:], float(np.pi / 2), None, ALU.add))
                link(v.tensor_scalar(ang[:], over[:], float(np.pi), -2 * float(np.pi), ALU.is_gt, ALU.mult))
                link(v.tensor_tensor(over[:], over[:], ang[:], ALU.add))
                link(v.tensor_scalar(over[:], over[:], pi, -pi, ALU.min, ALU.max))
                v.tensor_scalar(rest[:], rest[:], pi, -pi, ALU.min, ALU.max).then_inc(S("angles"), 1)
                dve.wait_ge(S("sines"), 2)
                link(v.tensor_scalar(sin[:], sin[:], con[:, C_SIGN:C_SIGN + 1], None, ALU.mult))

            def rotate(name, j, w, last):
                dve.wait_ge(S("a_full"), TURN_A[name] + 1)
                link(v.tensor_tensor(w, w, cos[:], ALU.mult))
                ins = v.tensor_tensor(rotated[:], area_a[:, j, :], sin[:], ALU.mult)
                if last:
                    ins.then_inc(S("a_freed"), 1)
                    dve.wait_ge(S("a_freed"), TURN_A[name] + 1)
                else:
                    link(ins)
                v.tensor_tensor(w, w, rotated[:], ALU.add).then_inc(S("rope_done"), 1)

            def decay(part):
                if part == "a":
                    link(v.memset(resetc[:], 1.0))
                    link(v.memset(resetc[:].rearrange("p (n j) -> p n j", j=CHUNK)[:, :, 0:1], 0.0))
                    dve.wait_ge(S("lb_logs"), 1)
                    v.tensor_scalar(st[:, 64:68], st[:, 64:68], -60 * float(np.log(2.0)), None, ALU.add)\
                        .then_inc(S("decay_space"), 1)
                    dve.wait_ge(S("decay_space"), 1)
                elif part == "b":
                    dve.wait_ge(S("sig_log"), 1)
                    link(v.scalar_tensor_tensor(hx[1][:], flat(bf[:, :, :]), 0.0, hx[0][:], ALU.min, ALU.subtract))
                    for h in range(B_H):
                        s = slice(T * h, T * h + T)
                        base_, floor = st[:, 68 + h:69 + h], st[:, 64 + h:65 + h]
                        v.tensor_scalar(hx[2][:, s], hx[1][:, s], base_, floor, ALU.add, ALU.max)
                        ins = v.tensor_scalar(hx[0][:, s], hx[1][:, s], base_, floor, ALU.add, ALU.subtract)
                    ins.then_inc(S("decay_u"), 1)
                else:
                    dve.wait_ge(S("decay_log"), 1)
                    link(v.tensor_tensor(hx[2][:], hx[2][:], hx[0][:], ALU.add))
                    v.tensor_tensor_scan(hb[:], resetc[:], hx[2][:], 0.0, ALU.mult, ALU.add)\
                        .then_inc(S("decay_sum"), 1)
                    dve.wait_ge(S("decay_sum"), 1)

            def stick_breaking(name):
                hg, tt = int(name[-2]), int(name[-1])
                ks, n = keys(tt), 2 * hg + tt + 1
                keep = s_keep1 if tt == 0 else s_keep2
                width = 4 * (ks + 1)
                z, l = s_z[:, :, 0:ks], s_a[:, :, 0:ks]
                pad = s_pad[:, 0:width].rearrange("p (h n) -> p h n", h=4)
                after = s_after[:, 0:width].rearrange("p (h n) -> p h n", h=4)
                dve.wait_ge(S("sb_log"), n)
                link(v.scalar_tensor_tensor(l, z, 0.0, l, ALU.max, ALU.add))
                v.memset(pad[:, :, ks:ks + 1], 0.0)
                link(v.tensor_tensor(pad[:, :, 0:ks], l, heads4(causal(tt, C_S01), ks), ALU.mult))
                link(v.tensor_tensor_scan(s_after[:, width - 2::-1], keep[:, width - 1:0:-1],
                                          s_pad[:, width - 1:0:-1], 0.0, ALU.mult, ALU.add))
                v.tensor_tensor(z, z, heads4(causal(tt, C_SCM), ks), ALU.add)
                link(v.tensor_tensor(l, l, after[:, :, 0:ks], ALU.add))
                v.tensor_tensor(z, z, l, ALU.subtract).then_inc(S("sb_arg"), 1)

            v.memset(epsb[:], EPS).then_inc(S("eps_set"), 1)
            link(v.memset(ones_row[:], 1.0))
            dve.wait_ge(S("con_loaded"), 16)
            dve.wait_ge(S("vec_loaded"), 16)
            split_low(0, 0)
            split_low(0, 1)
            for kind, what in ORDER:
                if kind == "tile":
                    tile(what)
                elif kind == "step":
                    step(what)
                elif "gu" in what:
                    gate_up(int(what[-1]))
                else:
                    down(int(what[-1]))

        @block.gpsimd
        def _(pool):
            def gated_sums(up, gate, mixed, part, block0, blocks, branches, gates_before, mixed_before):
                for u in range(blocks):
                    branch, k = u // KD, u % KD
                    if k == 0:
                        pool.wait_ge(S("gates_on"), gates_before + branch + 1)
                    pool.wait_ge(S("block_freed"), block0 + u + 1)
                    g = gate[:, u, :]
                    if branch == 0:
                        nc.gpsimd.tensor_tensor(mixed[:, k, :], up[:, u % 4, :], g, ALU.mult)\
                            .then_inc(S("mixed"), 1)
                        continue
                    if gated_here(u + mixed_before):
                        term = up[:, u % 4, :]
                    else:
                        term = part[:, u // 2 % 2, :]
                        nc.gpsimd.tensor_tensor(term, up[:, u % 4, :], g, ALU.mult).then_inc(S("pool_step"), 1)
                        steps[0] += 1
                        pool.wait_ge(S("pool_step"), steps[0])
                    pool.wait_ge(S("mixed"), mixed_before + u - KD + 1)
                    nc.gpsimd.tensor_tensor(mixed[:, k, :], mixed[:, k, :], term, ALU.add)\
                        .then_inc(S("mixed"), 1)

            def sum_squares(i):
                if i:
                    pool.wait_ge(S("t_full"), TURN_T[SUMMED_NORMS[i - 1]] + 1)
                for k in range(1, KD - 1):
                    pool.wait_ge(S("square"), KD * i + k + 1)
                    if k > 1:
                        pool.wait_ge(S("squares_added"), (KD - 2) * i + k - 1)
                    before = sq_ring[:, 0, :] if k == 1 else sq_sum[:]
                    nc.gpsimd.tensor_tensor(sq_sum[:], before, sq_ring[:, k % 2, :], ALU.add)\
                        .then_inc(S("squares_added"), 1)

            def biases():
                pool.wait_ge(S("bias_begun"), 1)
                for b in range(BUCKETS - 1):
                    pool.wait_ge(S("rise_made"), b + 1)
                    nc.gpsimd.tensor_tensor(bias[:, 0:POOL_H, :], bias[:, 0:POOL_H, :], rise[b % 2][:, :, :],
                                            ALU.add).then_inc(S("rise_used"), 1)
                    pool.wait_ge(S("rise_used"), b + 1)

            biases()
            steps = [0]
            gated_sums(up1, gates, mixed1, gated1, BLOCKS["up1"], 24, 3, 0, 0)
            sum_squares(0)
            sum_squares(1)
            sum_squares(2)
            gated_sums(up2, gates2, mixed2, gated2, BLOCKS["up2"], 16, 2, 3, 24)
            sum_squares(3)
            sum_squares(4)


def tiled(w, n_out):
    k, n = w.shape
    full = np.zeros((k, n_out * P), w.dtype)
    full[:, :n] = w
    return full.reshape(k // P, P, n_out, P).transpose(2, 1, 0, 3).reshape(n_out, P, (k // P) * P)


def grouped(t, per):
    n, p, c = t.shape
    return np.ascontiguousarray(t.reshape(n // per, per, p, c).transpose(0, 2, 1, 3).reshape(n // per, p, per * c))


def chunked(w, per):
    k, n = w.shape
    return np.ascontiguousarray(w.reshape(k // P // per, per, P, n).transpose(0, 2, 1, 3).reshape(-1, P, per * n))


def kernel(**inputs):
    import concourse.bacc as bacc
    from concourse.bass_utils import run_bass_kernel_spmd

    i = {k: np.asarray(v) for k, v in inputs.items()}
    w = i["w_in"][0]
    sizes = (A_H * P, P, P, IDX_H * IDX_D, IDX_D, IDX_H, 512, 512, 512, 512, QR, KVR, ROPE, 3 * D)
    aq, ak, av, iq, ik, iw, bq, bf, bi, bg, cq, ckv, kpe, gl = np.split(w, np.cumsum(sizes)[:-1].tolist(), axis=1)
    a = {}
    a["xT"] = np.ascontiguousarray(i["x"][0].T).reshape(KD, P, T)
    a["pT"] = np.ascontiguousarray(i["p_2"][0, 0].T).reshape(2, P, T)
    a["pos"] = np.ascontiguousarray(i["positions"][0])
    a["rel_bias"] = np.ascontiguousarray(i["rel_bias"].reshape(-1))
    a["forget_bias"] = np.ascontiguousarray(i["forget_bias_2"][0])
    a["consts"] = constants()
    vectors = {"attn_norm": i["attn_norm"][0], "ffn_norm": i["ffn_norm"][0], "final_norm": i["final_norm"],
               "ffn1_norm": i["ffn1_norm_2"][0], "mix_norm": i["mix_norm_2"][0], "ffn2_norm": i["ffn2_norm_2"][0],
               "ple_norm": i["ple_norm_2"][0], "mla_q_norm": i["mla_q_norm"][0], "mla_kv_norm": i["mla_kv_norm"][0],
               "lb_logits": i["hgrn_lb_logits"][0], "hgrn_out": i["hgrn_out_norm"][0],
               "q_norm": np.concatenate([i["q_norm_2"][0]] * 2), "k_norm": np.concatenate([i["k_norm_2"][0]] * 2)}
    a["vecs"] = np.ascontiguousarray(np.concatenate([vectors[n].reshape(c, P).T for n, c in VEC_SIZES], axis=1))

    def cat(*v):
        return np.concatenate(v, axis=1)

    proj = cat(kpe, kpe, ik, ik, iq)
    a["w_projT_a"] = grouped(tiled(proj, 6), 2)
    a["w_avw"] = chunked(cat(av, iw), KD)
    a["w_projT_b"] = grouped(tiled(cat(ak, aq, cq, ckv, bf), 14), 2)
    a["w_projT_c"] = grouped(tiled(bq, 4), 2)
    a["w_bi"] = chunked(bi, 4)
    a["w_projT_d"] = grouped(tiled(bg, 4), 2)
    qb = i["mla_w_qb"][0].reshape(QR, C_H, NOPE + ROPE)
    qb = cat(qb[:, :, :NOPE].reshape(QR, -1), qb[:, :, NOPE:].reshape(QR, -1))
    a["w_qb"] = grouped(tiled(qb, 6), 3)
    kvb = i["mla_w_kvb"][0].reshape(KVR, C_H, NOPE + P)
    kb = grouped(tiled(kvb[:, :, :NOPE].reshape(KVR, -1), 4), 4)
    vb = chunked(np.ascontiguousarray(kvb[:, :, NOPE:].reshape(KVR, -1)), 2)
    a["w_kvb"] = np.concatenate([kb, vb], axis=2)
    a["w_gates1a"] = grouped(tiled(gl[:, :D], 8), 2)
    a["w_gates1b"] = grouped(tiled(gl[:, D:], 16), 2)
    a["w_up1"] = np.concatenate([grouped(tiled(i[n][0], 8), 4) for n in ("w_up_a", "w_up_b", "w_up_c")])
    a["w_out1"] = grouped(tiled(i["w_out"][0], 8), 2)

    def gate_up(gate, up):
        return np.concatenate([tiled(gate, KF), tiled(up, KF)], axis=2)

    def down(m):
        t = tiled(m, KD)
        return np.ascontiguousarray(t.reshape(KD, P, 2, KF // 2 * P).transpose(0, 2, 1, 3).reshape(16, P, -1))

    for f, (g, u, d) in enumerate((("w_ffn_gate", "w_ffn_up", "w_ffn_down"),
                                   ("ffn1_w_gate_2", "ffn1_w_up_2", "ffn1_w_down_2"),
                                   ("ffn2_w_gate_2", "ffn2_w_up_2", "ffn2_w_down_2"))):
        a[f"w_gu{f}"] = gate_up(i[g][0], i[u][0])
        a[f"w_dn{f}"] = down(i[d][0])
    w = i["w_in_2"][0]
    sizes = (512, 512, 512, FOX_H, 512, 512, 512, D, D)
    fq, fk, fv, fl, sq, sk, sv, gf, gs = np.split(w, np.cumsum(sizes)[:-1].tolist(), axis=1)
    a["w_qk2"] = grouped(tiled(cat(fq, fk, sq, sk), 16), 2)
    a["w_fvl"] = chunked(cat(fv, fl), 4)
    a["w_sv"] = chunked(sv, 4)
    a["w_gates2"] = grouped(tiled(cat(gf, gs), 16), 2)
    a["w_up2"] = np.concatenate([grouped(tiled(i[n][0], 8), 4) for n in ("w_branch_fox_2", "w_branch_sb_2")])
    a["w_out2"] = grouped(tiled(i["w_out_2"][0], 8), 2)
    a["w_pg"] = grouped(tiled(i["w_ple_gate_2"][0], 8), 2)
    a["w_pp"] = grouped(tiled(i["w_ple_proj_2"][0], 8), 8)
    for name, n, c, _ in TILES:
        assert a[name][n].shape == (P, c), (name, a[name].shape, c)

    nc = bacc.Bacc("TRN2", target_bir_lowering=False, num_devices=1)
    arrays, aps = {}, {}
    for name, arr in a.items():
        arr = np.ascontiguousarray(arr)
        arrays[f"in_{name}"] = arr
        aps[name] = nc.dram_tensor(f"in_{name}", arr.shape, mybir.dt.from_np(arr.dtype), kind="ExternalInput").ap()
    out = nc.dram_tensor("out", (KD, P, T), F32, kind="ExternalOutput").ap()
    build(nc, aps, out)
    r = run_bass_kernel_spmd(nc, [arrays], core_ids=[0])
    got = r.results[0]["out"]
    return np.ascontiguousarray(got.reshape(D, T).T).reshape(1, T, D)
```
